# Optimizing a Trainium2 kernel written in Bass

```python
import jax, jax.numpy as jnp
from jax import lax
import numpy as np

D_MODEL = 1024
BATCH = 1
SEQ = 512
DEPTH = 1

MEM_LEN = 256
CONV_WIDTH = D_MODEL // 2
CONV_K = 3
ATT_HEADS = 8
HEAD_DIM = 64
ATT_WIDTH = ATT_HEADS * HEAD_DIM
KV_GROUPS = 2
Q_PER_KV = ATT_HEADS // KV_GROUPS
KV_WIDTH = KV_GROUPS * HEAD_DIM
MIX_WIDTH = CONV_WIDTH + ATT_WIDTH
CMP_BLOCK = 32
CMP_STRIDE = 16
CMP_HIDDEN = 256
SLC_BLOCK = 64
N_SELECT = 16
WINDOW = 512
Q_BLOCK = 128
ROPE_THETA = 10000.0
X_HEADS = 4
X_HEAD_DIM = D_MODEL // X_HEADS
D_FF = -(-8 * D_MODEL // (3 * 256)) * 256
EPS = 1e-6
FORCE = 1e4
W_IN_COLS = 3 * CONV_WIDTH + ATT_WIDTH + 6 * KV_WIDTH + 3 * ATT_HEADS


def rmsnorm(x, g):
    xf = x.astype(jnp.float32)
    y = xf * lax.rsqrt(jnp.mean(xf * xf, axis=-1, keepdims=True) + EPS)
    return (y * g.astype(jnp.float32)).astype(x.dtype)

def rope(x, pos):
    half = HEAD_DIM // 2
    inv = ROPE_THETA ** (-jnp.arange(half, dtype=jnp.float32) / half)
    ang = pos.astype(jnp.float32)[..., None] * inv
    cos = jnp.cos(ang)[:, :, None, :]
    sin = jnp.sin(ang)[:, :, None, :]
    xf = x.astype(jnp.float32)
    x1, x2 = xf[..., :half], xf[..., half:]
    return jnp.concatenate([x1 * cos - x2 * sin, x2 * cos + x1 * sin], axis=-1).astype(x.dtype)

def masked_softmax(s, mask):
    s = jnp.where(mask, s.astype(jnp.float32), -1e30)
    e = jnp.exp(s - jnp.max(s, axis=-1, keepdims=True)) * mask
    return e / jnp.maximum(jnp.sum(e, axis=-1, keepdims=True), 1e-30)

def compress(k, pe, w1, w2, n_cmp):
    b = k.shape[0]
    idx = np.arange(n_cmp)[:, None] * CMP_STRIDE + np.arange(CMP_BLOCK)[None, :]
    blocks = k[:, idx] + pe[None, None, :, None, :]
    flat = blocks.transpose(0, 1, 3, 2, 4).reshape(b, n_cmp, KV_GROUPS, CMP_BLOCK * HEAD_DIM)
    return jax.nn.silu(flat @ w1) @ w2

def short_conv_mixer(bg, cg, xin, conv_w):
    z = cg * xin
    zc = lax.conv_general_dilated(z, conv_w[:, None, :].astype(z.dtype), window_strides=(1,),
                                  padding=((CONV_K - 1, 0),), dimension_numbers=("NWC", "WIO", "NWC"),
                                  feature_group_count=CONV_WIDTH)
    return bg * zc

def nsa_mixer(q, k_cmp_raw, v_cmp_raw, k_slc, v_slc, k_win, v_win, gates, positions,
              pe_kc, w1_kc, w2_kc, pe_vc, w1_vc, w2_vc):
    b, s = q.shape[0], q.shape[1]
    n_cmp = (s - CMP_BLOCK) // CMP_STRIDE + 1
    n_slc = s // SLC_BLOCK
    n_sel = min(N_SELECT, n_slc)
    scale = HEAD_DIM ** -0.5

    q = rope(q, positions)
    cmp_end_np = np.arange(n_cmp) * CMP_STRIDE + CMP_BLOCK - 1
    cmp_end = jnp.asarray(cmp_end_np, dtype=jnp.int32)
    k_cmp = rope(compress(k_cmp_raw, pe_kc, w1_kc, w2_kc, n_cmp), positions[:, cmp_end_np])
    v_cmp = compress(v_cmp_raw, pe_vc, w1_vc, w2_vc, n_cmp)

    ci = np.arange(n_cmp)[:, None] * CMP_STRIDE
    sj = np.arange(n_slc)[None, :] * SLC_BLOCK
    ov = np.clip(np.minimum(ci + CMP_BLOCK, sj + SLC_BLOCK) - np.maximum(ci, sj), 0, None)
    slc_map = jnp.asarray(ov / CMP_BLOCK, dtype=jnp.float32)

    k_blocks = rope(k_slc, positions).reshape(b, n_slc, SLC_BLOCK, KV_GROUPS, HEAD_DIM).transpose(0, 3, 1, 2, 4)
    v_blocks = v_slc.reshape(b, n_slc, SLC_BLOCK, KV_GROUPS, HEAD_DIM).transpose(0, 3, 1, 2, 4)
    pad = ((0, 0), (WINDOW, 0), (0, 0), (0, 0))
    k_win_pad = jnp.pad(rope(k_win, positions), pad)
    v_win_pad = jnp.pad(v_win, pad)
    bi = jnp.arange(b)[:, None, None, None]
    gi = jnp.arange(KV_GROUPS)[None, :, None, None]
    blk = jnp.arange(n_slc)

    def block(i):
        s0 = i * Q_BLOCK
        t = s0 + jnp.arange(Q_BLOCK)
        qb = lax.dynamic_slice_in_dim(q, s0, Q_BLOCK, axis=1).reshape(b, Q_BLOCK, KV_GROUPS, Q_PER_KV, HEAD_DIM)
        gb = lax.dynamic_slice_in_dim(gates, s0, Q_BLOCK, axis=1).reshape(b, Q_BLOCK, KV_GROUPS, Q_PER_KV, 3)

        s_c = jnp.einsum("bqgrd,bkgd->bgrqk", qb, k_cmp) * scale
        p_c = masked_softmax(s_c, cmp_end[None, :] <= t[:, None])
        o_c = jnp.einsum("bgrqk,bkgd->bqgrd", p_c, v_cmp)

        imp = jnp.einsum("bgrqk,ks->bgqs", p_c, slc_map)
        cur = t // SLC_BLOCK
        forced = (blk[None, :] == 0) | (blk[None, :] == cur[:, None]) | (blk[None, :] == cur[:, None] - 1)
        future = blk[None, :] * SLC_BLOCK > t[:, None]
        imp = jnp.where(forced, FORCE, jnp.where(future, -FORCE, imp))
        _, sel = lax.top_k(imp, n_sel)
        ks = k_blocks[bi, gi, sel].reshape(b, KV_GROUPS, Q_BLOCK, n_sel * SLC_BLOCK, HEAD_DIM)
        vs = v_blocks[bi, gi, sel].reshape(b, KV_GROUPS, Q_BLOCK, n_sel * SLC_BLOCK, HEAD_DIM)
        kpos = (sel[..., None] * SLC_BLOCK + jnp.arange(SLC_BLOCK)).reshape(b, KV_GROUPS, Q_BLOCK, n_sel * SLC_BLOCK)
        s_s = jnp.einsum("bqgrd,bgqkd->bgrqk", qb, ks) * scale
        p_s = masked_softmax(s_s, (kpos <= t[None, None, :, None])[:, :, None])
        o_s = jnp.einsum("bgrqk,bgqkd->bqgrd", p_s, vs)

        kw = lax.dynamic_slice_in_dim(k_win_pad, s0, Q_BLOCK + WINDOW, axis=1)
        vw = lax.dynamic_slice_in_dim(v_win_pad, s0, Q_BLOCK + WINDOW, axis=1)
        wpos = s0 - WINDOW + jnp.arange(Q_BLOCK + WINDOW)
        mask_w = (wpos[None, :] <= t[:, None]) & (wpos[None, :] > t[:, None] - WINDOW) & (wpos[None, :] >= 0)
        s_w = jnp.einsum("bqgrd,bkgd->bgrqk", qb, kw) * scale
        p_w = masked_softmax(s_w, mask_w)
        o_w = jnp.einsum("bgrqk,bkgd->bqgrd", p_w, vw)

        o = gb[..., 0:1] * o_c + gb[..., 1:2] * o_s + gb[..., 2:3] * o_w
        return o.reshape(b, Q_BLOCK, ATT_WIDTH).astype(q.dtype)

    out = lax.map(block, jnp.arange(s // Q_BLOCK))
    return out.transpose(1, 0, 2, 3).reshape(b, s, ATT_WIDTH)

def first_inputs(seed: int = 0) -> dict:
    key = jax.random.key(seed)
    ks = jax.random.split(key, 32)

    def w(k, shape, fan_in):
        return jax.random.normal(k, shape, jnp.float32) * fan_in ** -0.5

    def gain(k, n):
        return 1.0 + 0.05 * jax.random.normal(k, (n,), jnp.float32)

    offs = jax.random.randint(ks[2], (BATCH, 1), 0, 2048, dtype=jnp.int32)
    return {
        "x": jax.random.normal(ks[0], (BATCH, SEQ, D_MODEL), jnp.float32),
        "mem": jax.random.normal(ks[1], (BATCH, MEM_LEN, D_MODEL), jnp.float32),
        "positions": jnp.arange(SEQ, dtype=jnp.int32)[None, :] + offs,
        "norm_mix_pre": gain(ks[3], D_MODEL),
        "w_in": w(ks[4], (D_MODEL, W_IN_COLS), D_MODEL),
        "conv_w": w(ks[5], (CONV_K, CONV_WIDTH), CONV_K),
        "pe_kc": 0.1 * jax.random.normal(ks[6], (CMP_BLOCK, HEAD_DIM), jnp.float32),
        "w1_kc": w(ks[7], (CMP_BLOCK * HEAD_DIM, CMP_HIDDEN), CMP_BLOCK * HEAD_DIM),
        "w2_kc": w(ks[8], (CMP_HIDDEN, HEAD_DIM), CMP_HIDDEN),
        "pe_vc": 0.1 * jax.random.normal(ks[9], (CMP_BLOCK, HEAD_DIM), jnp.float32),
        "w1_vc": w(ks[10], (CMP_BLOCK * HEAD_DIM, CMP_HIDDEN), CMP_BLOCK * HEAD_DIM),
        "w2_vc": w(ks[11], (CMP_HIDDEN, HEAD_DIM), CMP_HIDDEN),
        "norm_conv_out": gain(ks[12], CONV_WIDTH),
        "norm_attn_out": gain(ks[13], ATT_WIDTH),
        "w_out": w(ks[14], (MIX_WIDTH, D_MODEL), MIX_WIDTH),
        "norm_mix_post": gain(ks[15], D_MODEL),
        "norm_x_pre": gain(ks[16], D_MODEL),
        "norm_mem": gain(ks[17], D_MODEL),
        "w_q_x": w(ks[18], (D_MODEL, D_MODEL), D_MODEL),
        "w_kv_x": w(ks[19], (D_MODEL, 2 * D_MODEL), D_MODEL),
        "w_o_x": w(ks[20], (D_MODEL, D_MODEL), D_MODEL),
        "norm_x_post": gain(ks[21], D_MODEL),
        "norm_ffn_pre": gain(ks[22], D_MODEL),
        "w_gate_up": w(ks[23], (D_MODEL, 2 * D_FF), D_MODEL),
        "w_down": w(ks[24], (D_FF, D_MODEL), D_FF),
        "norm_ffn_post": gain(ks[25], D_MODEL),
    }

def first_block(x, mem, positions, norm_mix_pre, w_in, conv_w, pe_kc, w1_kc, w2_kc, pe_vc, w1_vc, w2_vc,
              norm_conv_out, norm_attn_out, w_out, norm_mix_post, norm_x_pre, norm_mem, w_q_x, w_kv_x,
              w_o_x, norm_x_post, norm_ffn_pre, w_gate_up, w_down, norm_ffn_post):
    b, s, _ = x.shape
    h = x
    for _layer in range(DEPTH):
        u = rmsnorm(h, norm_mix_pre)
        proj = u @ w_in
        cuts = np.cumsum([CONV_WIDTH, CONV_WIDTH, CONV_WIDTH, ATT_WIDTH] + [KV_WIDTH] * 6)
        bg, cg, xin, q, kc, vc, ksl, vsl, kw, vw, gl = jnp.split(proj, cuts, axis=-1)
        kv_shape = (b, s, KV_GROUPS, HEAD_DIM)
        y_conv = short_conv_mixer(bg, cg, xin, conv_w)
        y_att = nsa_mixer(q.reshape(b, s, ATT_HEADS, HEAD_DIM), kc.reshape(kv_shape), vc.reshape(kv_shape),
                          ksl.reshape(kv_shape), vsl.reshape(kv_shape), kw.reshape(kv_shape), vw.reshape(kv_shape),
                          jax.nn.sigmoid(gl).reshape(b, s, ATT_HEADS, 3), positions,
                          pe_kc, w1_kc, w2_kc, pe_vc, w1_vc, w2_vc)
        mixed = jnp.concatenate([rmsnorm(y_conv, norm_conv_out), rmsnorm(y_att, norm_attn_out)], axis=-1)
        h = h + rmsnorm(mixed @ w_out, norm_mix_post)

        hn = rmsnorm(h, norm_x_pre)
        mn = rmsnorm(mem, norm_mem)
        qx = (hn @ w_q_x).reshape(b, s, X_HEADS, X_HEAD_DIM)
        kx, vx = jnp.split(mn @ w_kv_x, 2, axis=-1)
        kx = kx.reshape(b, MEM_LEN, X_HEADS, X_HEAD_DIM)
        vx = vx.reshape(b, MEM_LEN, X_HEADS, X_HEAD_DIM)
        sx = jnp.einsum("bshd,bmhd->bhsm", qx, kx).astype(jnp.float32) * X_HEAD_DIM ** -0.5
        px = jax.nn.softmax(sx, axis=-1)
        ox = jnp.einsum("bhsm,bmhd->bshd", px, vx).astype(h.dtype).reshape(b, s, D_MODEL)
        h = h + rmsnorm(ox @ w_o_x, norm_x_post)

        hn = rmsnorm(h, norm_ffn_pre)
        g, up = jnp.split(hn @ w_gate_up, 2, axis=-1)
        h = h + rmsnorm((jax.nn.silu(g) * up) @ w_down, norm_ffn_post)
    return h


DEPTH_2 = 2

N_HEADS = 16
N_KV_HEADS = 2
GROUP = N_HEADS // N_KV_HEADS
ROT_DIM = HEAD_DIM // 4
ROPE_THETA_2 = 500000.0
WINDOW_2 = 128
BLOCK = 128
CONV_CH = D_MODEL // 2
CONV_WIDTH_2 = 31
D_FF_2 = -(-(8 * D_MODEL) // (3 * 256)) * 256
Q_W = N_HEADS * HEAD_DIM
KV_W = N_KV_HEADS * HEAD_DIM
IN_W = Q_W + 2 * KV_W + 2 * CONV_CH + 2 * D_MODEL
SPLITS = tuple(int(s) for s in np.cumsum([Q_W, KV_W, KV_W, CONV_CH, CONV_CH, D_MODEL])[:])


def rmsnorm_2(x, g):
    xf = x.astype(jnp.float32)
    y = xf * lax.rsqrt(jnp.mean(xf * xf, axis=-1, keepdims=True) + EPS)
    return (y * g.astype(jnp.float32)).astype(x.dtype)

def layernorm(x, g, b):
    xf = x.astype(jnp.float32)
    mu = jnp.mean(xf, axis=-1, keepdims=True)
    var = jnp.mean(jnp.square(xf - mu), axis=-1, keepdims=True)
    y = (xf - mu) * lax.rsqrt(var + EPS)
    return (y * g.astype(jnp.float32) + b.astype(jnp.float32)).astype(x.dtype)

def rope_tables(seq):
    inv_freq = ROPE_THETA_2 ** (-jnp.arange(0, ROT_DIM, 2, dtype=jnp.float32) / ROT_DIM)
    ang = jnp.arange(seq, dtype=jnp.float32)[:, None] * inv_freq[None, :]
    return jnp.cos(ang), jnp.sin(ang)

def partial_rope(x, cos, sin):
    half = ROT_DIM // 2
    c = cos[None, :, None, :].astype(x.dtype)
    s = sin[None, :, None, :].astype(x.dtype)
    x1, x2, xp = x[..., :half], x[..., half:ROT_DIM], x[..., ROT_DIM:]
    return jnp.concatenate([x1 * c - x2 * s, x2 * c + x1 * s, xp], axis=-1)

def sliding_window_attention(q, k, v, sinks):
    B, T = q.shape[0], q.shape[1]
    nb = T // BLOCK
    qb = q.reshape(B, nb, BLOCK, N_KV_HEADS, GROUP, HEAD_DIM)

    def band(t):
        tp = jnp.pad(t, ((0, 0), (BLOCK, 0), (0, 0), (0, 0)))
        tp = tp.reshape(B, nb + 1, BLOCK, N_KV_HEADS, HEAD_DIM)
        return jnp.concatenate([tp[:, :-1], tp[:, 1:]], axis=2)

    kb, vb = band(k), band(v)
    scale = HEAD_DIM ** -0.5
    s = jnp.einsum('bnqkgd,bnskd->bnkgqs', qb, kb,
                   preferred_element_type=jnp.float32) * scale
    qi = jnp.arange(BLOCK)[:, None]
    sj = jnp.arange(2 * BLOCK)[None, :]
    rel = qi + BLOCK - sj
    kpos = jnp.arange(nb)[:, None, None] * BLOCK - BLOCK + sj
    mask = (rel >= 0) & (rel < WINDOW_2) & (kpos >= 0)
    s = jnp.where(mask[None, :, None, None], s, -jnp.inf)
    sink = sinks.astype(jnp.float32).reshape(N_KV_HEADS, GROUP)[None, None, :, :, None, None]
    m = jnp.maximum(jnp.max(s, axis=-1, keepdims=True), sink)
    p = jnp.exp(s - m)
    p = p / (jnp.sum(p, axis=-1, keepdims=True) + jnp.exp(sink - m))
    o = jnp.einsum('bnkgqs,bnskd->bnqkgd', p.astype(v.dtype), vb)
    return o.reshape(B, T, N_HEADS * HEAD_DIM)

def conformer_conv(u, ug, w_dw, b_dw, ln_g, ln_b, w_pw):
    a = u * jax.nn.sigmoid(ug)
    y = lax.conv_general_dilated(
        a, w_dw[:, None, :].astype(a.dtype), window_strides=(1,),
        padding=[(CONV_WIDTH_2 - 1, 0)],
        dimension_numbers=('NWC', 'WIO', 'NWC'),
        feature_group_count=CONV_CH) + b_dw.astype(a.dtype)
    y = layernorm(y, ln_g, ln_b)
    y = jax.nn.silu(y)
    return jnp.einsum('btc,cd->btd', y, w_pw)

def second_inputs(seed: int = 0) -> dict:
    key = jax.random.key(seed)
    ks = jax.random.split(key, 16)
    f32 = jnp.float32

    def nrm(k, shape, scale):
        return jax.random.normal(k, shape, f32) * scale

    return {
        "x": nrm(ks[0], (BATCH, SEQ, D_MODEL), 1.0),
        "norm_mix": 1.0 + nrm(ks[1], (DEPTH_2, D_MODEL), 0.02),
        "w_in": nrm(ks[2], (DEPTH_2, D_MODEL, IN_W), D_MODEL ** -0.5),
        "q_norm": 1.0 + nrm(ks[3], (DEPTH_2, HEAD_DIM), 0.02),
        "k_norm": 1.0 + nrm(ks[4], (DEPTH_2, HEAD_DIM), 0.02),
        "sinks": nrm(ks[5], (DEPTH_2, N_HEADS), 0.5),
        "conv_w": nrm(ks[6], (DEPTH_2, CONV_WIDTH_2, CONV_CH), CONV_WIDTH_2 ** -0.5),
        "conv_b": nrm(ks[7], (DEPTH_2, CONV_CH), 0.02),
        "conv_ln_g": 1.0 + nrm(ks[8], (DEPTH_2, CONV_CH), 0.02),
        "conv_ln_b": nrm(ks[9], (DEPTH_2, CONV_CH), 0.02),
        "w_conv_out": nrm(ks[10], (DEPTH_2, CONV_CH, D_MODEL), CONV_CH ** -0.5),
        "w_out": nrm(ks[11], (DEPTH_2, D_MODEL, D_MODEL), D_MODEL ** -0.5),
        "norm_ffn": 1.0 + nrm(ks[12], (DEPTH_2, D_MODEL), 0.02),
        "w_gate_up": nrm(ks[13], (DEPTH_2, D_MODEL, 2 * D_FF_2), D_MODEL ** -0.5),
        "w_down": nrm(ks[14], (DEPTH_2, D_FF_2, D_MODEL), D_FF_2 ** -0.5),
    }

def second_block(x, norm_mix, w_in, q_norm, k_norm, sinks, conv_w, conv_b, conv_ln_g,
              conv_ln_b, w_conv_out, w_out, norm_ffn, w_gate_up, w_down):
    B, T = x.shape[0], x.shape[1]
    cos, sin = rope_tables(T)
    for l in range(DEPTH_2):
        h = rmsnorm_2(x, norm_mix[l])
        proj = jnp.einsum('btd,de->bte', h, w_in[l])
        q, k, v, u, ug, ga, gb = jnp.split(proj, SPLITS, axis=-1)
        q = q.reshape(B, T, N_HEADS, HEAD_DIM)
        k = k.reshape(B, T, N_KV_HEADS, HEAD_DIM)
        v = v.reshape(B, T, N_KV_HEADS, HEAD_DIM)
        q = partial_rope(rmsnorm_2(q, q_norm[l]), cos, sin)
        k = partial_rope(rmsnorm_2(k, k_norm[l]), cos, sin)
        a_out = sliding_window_attention(q, k, v, sinks[l])
        c_out = conformer_conv(u, ug, conv_w[l], conv_b[l], conv_ln_g[l],
                               conv_ln_b[l], w_conv_out[l])
        merged = jax.nn.sigmoid(ga) * a_out + jax.nn.sigmoid(gb) * c_out
        x = x + jnp.einsum('btd,de->bte', merged, w_out[l])
        h2 = rmsnorm_2(x, norm_ffn[l])
        gu = jnp.einsum('btd,df->btf', h2, w_gate_up[l])
        g, up = jnp.split(gu, 2, axis=-1)
        x = x + jnp.einsum('btf,fd->btd', jax.nn.silu(g) * up, w_down[l])
    return x


def setup_inputs(seed=0):
    out = dict(first_inputs(seed))
    for name, value in second_inputs(seed + 1).items():
        if name != "x":
            out[name + "_2"] = value
    return out


def reference(
    x, mem, positions, norm_mix_pre, w_in, conv_w, pe_kc, w1_kc, w2_kc, pe_vc, w1_vc, w2_vc,
    norm_conv_out, norm_attn_out, w_out, norm_mix_post, norm_x_pre, norm_mem, w_q_x, w_kv_x,
    w_o_x, norm_x_post, norm_ffn_pre, w_gate_up, w_down, norm_ffn_post, norm_mix_2, w_in_2,
    q_norm_2, k_norm_2, sinks_2, conv_w_2, conv_b_2, conv_ln_g_2, conv_ln_b_2, w_conv_out_2,
    w_out_2, norm_ffn_2, w_gate_up_2, w_down_2,
):
    x = first_block(
        x, mem, positions, norm_mix_pre, w_in, conv_w, pe_kc, w1_kc, w2_kc, pe_vc, w1_vc, w2_vc,
        norm_conv_out, norm_attn_out, w_out, norm_mix_post, norm_x_pre, norm_mem, w_q_x, w_kv_x,
        w_o_x, norm_x_post, norm_ffn_pre, w_gate_up, w_down, norm_ffn_post,
    )
    return second_block(
        x, norm_mix_2, w_in_2, q_norm_2, k_norm_2, sinks_2, conv_w_2, conv_b_2, conv_ln_g_2,
        conv_ln_b_2, w_conv_out_2, w_out_2, norm_ffn_2, w_gate_up_2, w_down_2,
    )


_drawn_inputs = setup_inputs


def setup_inputs(seed=0):
    import zlib

    import numpy as np

    out = dict(_drawn_inputs(seed))
    spreads = {}
    factors = {'pe_kc': 4.572,
     'norm_mix_2': 8.0,
     'q_norm_2': 8.0,
     'k_norm_2': 8.0,
     'sinks_2': 8.0,
     'conv_b_2': 5.647,
     'conv_ln_g_2': 8.0,
     'conv_ln_b_2': 8.0,
     'norm_ffn_2': 4.779}
    for name, (base, spread) in spreads.items():
        noise = np.random.default_rng([zlib.crc32(name.encode()), seed]).standard_normal(out[name].shape)
        drawn = base * np.exp(spread * noise) if base else spread * noise
        out[name] = __import__('jax').numpy.asarray(drawn.astype(out[name].dtype))
    for name, factor in factors.items():
        out[name] = (out[name] * factor).astype(out[name].dtype)
    return out
```

```python
from contextlib import ExitStack

import concourse.bass as bass
from concourse import mybir
import numpy as np

F32 = mybir.dt.float32
F32R = mybir.dt.float32r
BF16 = mybir.dt.bfloat16
I32 = mybir.dt.int32
ALU = mybir.AluOpType
ACT = mybir.ActivationFunctionType
AX = mybir.AxisListType.X

P = 128
T = 512
D = 1024
DT = D // P
QB = T // P
MEM = 256
FF = 2816
FT = FF // P
HD = 64
EPS = 1e-6
LAYERS = 2
NCMP = (T - 32) // 16 + 1
TAPS = 31
PAD = TAPS - 1
NEG = -1e30
LOW = -1e20
SLOTS = 3
UNIT = 2048

U_IN, U_W1, U_OUT, U_KV, U_QX, U_OX, U_GU, U_DN, U_L = 0, 11, 15, 19, 27, 31, 35, 57, 69
V_U, V_UG, V_Q, V_KV, V_GA, V_CO, V_OUT, V_GU, V_DN, V_N = 0, 2, 4, 8, 9, 17, 19, 23, 45, 57
UNITS = U_L + LAYERS * V_N
assert U_L % SLOTS == 0 and V_N % SLOTS == 0

_cols = {}


def _column(name, n):
    _cols[name] = (sum(c for _, c in _cols.values()), n)


for _n, _c in [("mix_pre", 8), ("mix_post", 8), ("x_pre", 8), ("mem", 8), ("x_post", 8), ("ffn_pre", 8),
               ("ffn_post", 8), ("conv_out", 4), ("attn_out", 4), ("conv_w", 12), ("inv", 1), ("pe_k", 16), ("pe_v", 16)]:
    _column(_n, _c)
LAYER_COLS = [("norm_mix", 8), ("norm_ffn", 8), ("q_norm", 1), ("k_norm", 1), ("sinks", 16),
              ("taps", 4 * TAPS), ("conv_b", 4), ("ln_g", 4), ("ln_b", 4)]
LAYER_BASE = sum(c for _, c in _cols.values())
_at = LAYER_BASE
for _n, _c in LAYER_COLS:
    _cols[_n] = (_at, _c)
    _at += _c
LAYER_W = _at - LAYER_BASE
PACK_W = LAYER_BASE + LAYERS * LAYER_W

C1 = 6.28125
C2 = float(np.round((2 * np.pi - C1) * 2 ** 22) / 2 ** 22)
C3 = float(2 * np.pi - C1 - C2)
ROUNDER = float(1.5 * 2 ** 23)


class Unit:

    def __init__(self, n0, layer=None, turn=None):
        self.n0, self.slot, self.n, self.round = n0, n0 % SLOTS, n0, n0 // SLOTS
        self.first = n0 < SLOTS and turn is None
        if layer is not None:
            self.n = layer * V_N + self.n
            self.round = layer * (V_N // SLOTS) + self.round
        if turn is not None:
            self.n = turn * SLOTS + self.n
            self.round = turn + self.round


def build(nc, w, x, mem, pos, pack, tables, cmask, w2, wg, rope2, out):
    ctx = ExitStack()
    with ctx:
        def sem(name):
            return ctx.enter_context(nc.semaphore(name))

        where = [(nc.sbuf_base + 63) // 64 * 64]

        def place(name, shape, dt=F32, cursor=where):
            size = int(np.prod(shape[1:])) * (2 if dt == BF16 else 4)
            t = nc.alloc_sbuf_tensor_at(name, shape, dt, offset=cursor[0])
            cursor[0] += (size + 31) // 32 * 32
            assert cursor[0] <= nc.sbuf_usable_end, (name, cursor[0])
            return t

        w_raw = place("w_raw", [P, SLOTS, UNIT])
        w_hi = place("w_hi", [P, SLOTS, UNIT], F32R)
        w_lo = place("w_lo", [P, SLOTS, UNIT], F32R)
        h = place("h", [P, DT, T])
        act_at = [where[0]]
        y_ffn = place("y_ffn", [P, DT, T], F32, act_at)
        x_hi = place("x_hi", [P, DT, T], F32R)
        x_lo = place("x_lo", [P, DT, T], F32R)
        rbc = place("rbc", [P, T])
        acc = place("acc", [P, T])
        sq = place("sq", [P, 2, T])
        gains = place("gains", [P, PACK_W])
        ident = place("ident", [P, P])
        ones = place("ones", [P, P])
        ident_b = place("ident_b", [P, P], BF16)
        mask_b = place("mask_b", [P, 2 * P], BF16)
        eps_c = place("eps_c", [P, 3])
        rcol = place("rcol", [P, QB])
        neg_sink = place("neg_sink", [P, LAYERS, 16])
        small = place("small", [P, 64])
        jcol = place("jcol", [P, 64])
        scope = where[0]

        a = [scope]
        f_hi = place("f_hi", [P, FT, T], F32R, a)
        f_lo = place("f_lo", [P, FT, T], F32R, a)
        silu = place("silu", [P, T], F32, a)

        a = [scope]
        bg = place("bg", [P, 4, T], F32, a)
        z = place("z", [P, 4, T], F32, a)
        cv = place("cv", [P, 4, T], F32, a)
        qT = place("qT", [P, 4, T], F32, a)
        kT = place("kT", [P, 2, T], F32, a)
        kTx = place("kTx", [P, 2, T], F32, a)
        b = [a[0]]
        e_c = place("e_c", [P, 2, 2 * P], F32, b)
        pt_c = place("pt_c", [P, 2, 2 * P], F32, b)
        kvc = place("kvc", [P, 2, T], F32, a)
        vtok = place("vtok", [P, QB, 2 * P], F32, a)
        cosT = place("cosT", [P, T], F32, a)
        sinT = place("sinT", [P, T], F32, a)
        ctmp = place("ctmp", [P, 2, T], F32, a)
        b = [a[0]]
        xf = place("xf", [P, 2, 16, 64], F32, b)
        o_all = place("o_all", [P, QB, T], F32, a)
        gate = place("gate", [P, QB, 24], F32, a)
        perm = place("perm", [P, P], F32, a)
        wg_s = place("wg_s", [P, 8 * 24], F32, a)
        wg_hi = place("wg_hi", [P, 8 * 24], F32R, a)
        wg_lo = place("wg_lo", [P, 8 * 24], F32R, a)
        w2_s = place("w2_s", [P, 2, 2, HD], F32, a)
        hc = place("hc", [P, 2, 2, 64], F32, a)
        pecol = place("pecol", [P, 2, 2], F32, a)
        kc2 = place("kc2", [HD, 2, NCMP], F32, a)
        kcm = place("kcm", [P, 2, 32], F32, a)
        vblk = place("vblk", [P, 4 * HD], F32, a)
        cmask_b = place("cmask_b", [P, QB, P], BF16, a)
        b = [a[0]]
        xc_hi = place("xc_hi", [P, 2, 16, 64], F32R, b)
        xc_lo = place("xc_lo", [P, 2, 16, 64], F32R, b)
        b = [a[0]]
        prob = place("prob", [P, 2, 2, T], F32, b)
        probT = place("probT", [P, 2, 2, T], F32, b)
        stage = nc.alloc_sbuf_tensor_at("stage", [P, 4 * P + QB * P], F32, offset=scope + 16 * 1024)
        pos_i = nc.alloc_sbuf_tensor_at("pos_i", [P, T], I32, offset=scope + 16 * 1024 + 4096)

        a = [scope]
        memT = place("memT", [P, DT, MEM], F32, a)
        m_hi = place("m_hi", [P, DT, MEM], F32R, a)
        m_lo = place("m_lo", [P, DT, MEM], F32R, a)
        kx = place("kx", [P, DT, MEM], F32, a)
        vx = place("vx", [P, 2, D], F32, a)
        qx = place("qx", [P, DT, T], F32, a)
        yb = place("yb", [P, DT, T], F32, a)
        xprob = place("xprob", [P, 2, 2, MEM], F32, a)
        xprobT = place("xprobT", [P, 2, 4, P], F32, a)
        xo = place("xo", [P, 2, T], F32, a)
        rmem = place("rmem", [P, MEM], F32, a)

        a = [scope]
        lq = place("lq", [P, 9, T], F32, a)
        lkx = place("lkx", [P, T], F32, a)
        lv = place("lv", [P, QB, P], F32, a)
        la = place("la", [P, 4, PAD + T], F32, a)
        cy = place("cy", [P, 4, T], F32, a)
        sga = place("sga", [P, DT, T], F32, a)
        sgb = place("sgb", [P, DT, T], F32, a)
        tab2 = place("tab2", [P, 2 * T + 2 * P], F32, a)
        cos2, sin2 = tab2[:, 0:T], tab2[:, T:2 * T]
        perm2, heads2 = tab2[:, 2 * T:2 * T + P], tab2[:, 2 * T + P:]
        lsm = place("lsm", [P, 2, 16], F32, a)
        b = [a[0]]
        lsq = place("lsq", [P, 2, T], F32, b)
        lrq = place("lrq", [P, 2, T], F32, b)
        lcos = place("lcos", [P, 2, T], F32, b)
        b = [a[0]]
        lprob = place("lprob", [P, 2, 2, MEM], F32, b)
        lprobT = place("lprobT", [P, 2, 4, P], F32, b)
        lo_s = place("lo_s", [P, 2, P], F32, b)

        bank = ctx.enter_context(nc.psum_tensor("bank", [P, 8, T], F32))
        STAT, AUX = 6, 7

        def col(name, k=0, layer=None):
            c = _cols[name][0] + k
            if layer is None:
                return gains[:, c:c + 1]
            return gains[:, bass.ds(layer * LAYER_W + c, 1)]

        def ki(t, slot):
            return t[:, slot, :].rearrange("p (k c) -> p k c", k=8)

        raw_in = [sem(f"raw_in{s}") for s in range(SLOTS)]
        hi_ready, lo_ready, unit_done = sem("hi_ready"), sem("lo_ready"), sem("unit_done")
        x_in = [sem(f"x_in{k}") for k in range(4)]
        const_in, mem_in, pos_in, tab_in, out_done = (sem(n) for n in (
            "const_in", "mem_in", "pos_in", "tab_in", "out_done"))
        const_ready, mask_ready, neg_sink_ready = sem("const_ready"), sem("mask_ready"), sem("neg_sink_ready")
        sq_ready, acc_ready, stat_done, std_ready, r_ready = (sem(n) for n in (
            "sq_ready", "acc_ready", "stat_done", "std_ready", "r_ready"))
        rcol_done, rcol_std, rcol_ready = sem("rcol_done"), sem("rcol_std"), sem("rcol_ready")
        mem_hi, mem_lo = sem("mem_hi"), sem("mem_lo")
        pre_hi, pre_lo, h_ready, t_ready, y_ready = (sem(n) for n in (
            "pre_hi", "pre_lo", "h_ready", "t_ready", "y_ready"))
        NORM_MIX, NORM_MEM, NORM_MIXP, NORM_X, NORM_XP, NORM_F, NORM_FP, NORM_L = range(8)

        def split_hi(act, u):
            act.wait_ge(raw_in[u.slot], (u.round + 1) * 16)
            if not u.first:
                act.wait_ge(unit_done, u.n - 2)
            act.activation(w_hi[:, u.slot, :], w_raw[:, u.slot, :], ACT.Copy).then_inc(hi_ready, 1)

        def split_lo(dve, u):
            dve.wait_ge(hi_ready, u.n + 1)
            dve.tensor_tensor(w_lo[:, u.slot, :], w_raw[:, u.slot, :], w_hi[:, u.slot, :],
                              ALU.subtract).then_inc(lo_ready, 1)

        def square(act, n, k, src, width=T):
            if not isinstance(n, int) or n * 7 + k >= 2:
                act.wait_ge(acc_ready, n * 7 + (0, 0, 1, 1, 2, 3, 4, 5)[k])
            act.activation(sq[:, k % 2, 0:width], src, ACT.Square).then_inc(sq_ready, 1)

        def sum_squares(pool, n, width=T):
            for k in range(1, 8):
                pool.wait_ge(sq_ready, n * 8 + k + 1)
                if k > 1:
                    pool.wait_ge(acc_ready, n * 7 + k - 1)
                elif not isinstance(n, int) or n > 0:
                    pool.wait_ge(stat_done, n)
                pool.tensor_tensor(acc[:, 0:width], sq[:, 0, 0:width] if k == 1 else acc[:, 0:width], sq[:, k % 2, 0:width],
                                   ALU.add).then_inc(acc_ready, 1)

        def stat_columns(pe, n, blocks):
            pe.wait_ge(acc_ready, n * 7 + 7)
            for b_ in range(blocks):
                mm = pe.matmul(bank[:, AUX, b_:b_ + 1], acc[:, b_ * P:(b_ + 1) * P], ones[:, 0:1],
                               start=True, stop=True)
            mm.then_inc(rcol_done, 1)

        def stat_rows(pe, n, width=T):
            pe.wait_ge(acc_ready, n * 7 + 7)
            pe.matmul(bank[:, STAT, 0:width], ones[:, :], acc[:, 0:width], start=True, stop=True)\
              .then_inc(stat_done, 1)

        def std_rows(act, n, width=T):
            act.wait_ge(stat_done, n + 1)
            act.activation(rbc[:, 0:width], bank[:, STAT, 0:width], ACT.Sqrt, bias=eps_c[:, 0:1],
                           scale=1.0 / D).then_inc(std_ready, 1)

        def inv_rows(dve, n, width=T):
            dve.wait_ge(std_ready, n + 1)
            dve.reciprocal(rbc[:, 0:width], rbc[:, 0:width]).then_inc(r_ready, 1)

        def std_columns(act, c, blocks):
            act.wait_ge(rcol_done, c + 1)
            act.activation(rcol[:, 0:blocks], bank[:, AUX, 0:blocks], ACT.Sqrt, bias=eps_c[:, 0:1],
                           scale=1.0 / D).then_inc(rcol_std, 1)

        def inv_columns(dve, c, blocks):
            dve.wait_ge(rcol_std, c + 1)
            dve.reciprocal(rcol[:, 0:blocks], rcol[:, 0:blocks]).then_inc(rcol_ready, 1)

        def pre_norm_hi(act, i, n, k, gain, layer=None):
            act.activation(x_hi[:, k, :], h[:, k, :], ACT.Copy, scale=col(gain, k, layer)).then_inc(pre_hi, 1)
            square(act, n, k, h[:, k, :])

        def pre_norm_lo(dve, i, k, gain, layer=None):
            dve.wait_ge(pre_hi, i * 8 + k + 1)
            dve.scalar_tensor_tensor(out=x_lo[:, k, :], in0=h[:, k, :], scalar=col(gain, k, layer),
                                     in1=x_hi[:, k, :], op0=ALU.mult, op1=ALU.subtract).then_inc(pre_lo, 1)

        def products(pe, u, m, k, kx_, pair, start, stop, hi, lo, width=T, chunks=8):
            wh = w_hi[:, u.slot, :].rearrange("p (k c) -> p k c", k=chunks)
            wl = w_lo[:, u.slot, :].rearrange("p (k c) -> p k c", k=chunks)
            cols = slice(m * P, (m + 1) * P)
            dst = bank[:, 2 * pair + m, 0:width]
            pe.matmul(dst, wh[:, k, cols], hi[:, kx_, 0:width], start=start, stop=False)
            pe.matmul(dst, wh[:, k, cols], lo[:, kx_, 0:width], start=False, stop=False)
            return pe.matmul(dst, wl[:, k, cols], hi[:, kx_, 0:width], start=False, stop=stop)

        def linear_tile(pe, u, m, hi=x_hi, lo=x_lo, width=T):
            for k in range(8):
                mm = products(pe, u, m, k, k, u.slot, k == 0, k == 7, hi, lo, width)
            return mm

        def linear(pe, u, hi=x_hi, lo=x_lo, width=T):
            pe.wait_ge(lo_ready, u.n + 1)
            for m in range(2):
                mm = linear_tile(pe, u, m, hi, lo, width)
            mm.then_inc(unit_done, 1)

        def linear_wide(pe, us, chunk_ready, hi=x_hi, lo=x_lo):
            for k in range(8):
                chunk_ready(k)
                for u in us:
                    if k == 0:
                        pe.wait_ge(lo_ready, u.n + 1)
                    for m in range(2):
                        mm = products(pe, u, m, k, k, u.slot, k == 0, k == 7, hi, lo)
                    if k == 7:
                        mm.then_inc(unit_done, 1)

        def tokens_major(pe, u, hi, lo, blocks, c0, n, bank_of):
            wh, wl = ki(w_hi, u.slot), ki(w_lo, u.slot)
            for b_ in range(blocks):
                bk, at = bank_of(b_)
                dst = bank[:, bk, at:at + n]
                for k in range(8):
                    xh, xl = hi[:, k, b_ * P:(b_ + 1) * P], lo[:, k, b_ * P:(b_ + 1) * P]
                    pe.matmul(dst, xh, wh[:, k, c0:c0 + n], start=(k == 0), stop=False)
                    pe.matmul(dst, xl, wh[:, k, c0:c0 + n], start=False, stop=False)
                    mm = pe.matmul(dst, xh, wl[:, k, c0:c0 + n], start=False, stop=(k == 7))
            return mm

        def units(eng, first, count, layer, body):
            turns = count // SLOTS
            if turns >= 2:
                with eng.Fori(0, turns) as i:
                    for s in range(SLOTS):
                        body(Unit(first + s, layer, i), s, i)
            else:
                turns = 0
            for j in range(turns * SLOTS, count):
                body(Unit(first + j, layer), j, None)

        g_scaled, silu_done, up_scaled, f_ready, f_hi_done, f_lo_done = (sem(n) for n in (
            "g_scaled", "silu_done", "up_scaled", "f_ready", "f_hi_done", "f_lo_done"))

        def tile_of(j, i):
            return j if i is None else i * SLOTS + j

        def pick(t, j, i):
            return t[:, j, :] if i is None else t[:, bass.ds(i * SLOTS + j, 1), :].rearrange("p o t -> p (o t)")

        def ffn_up_act(act, first, call, layer):
            def body(u, j, i):
                n = tile_of(j, i) + call * FT
                g, up = bank[:, 2 * u.slot, :], bank[:, 2 * u.slot + 1, :]
                act.wait_ge(g_scaled, n + 1)
                act.activation(silu[:, :], g, ACT.Silu).then_inc(silu_done, 1)
                act.wait_ge(f_ready, n + 1)
                act.activation(pick(f_hi, j, i), up, ACT.Copy).then_inc(f_hi_done, 1)
                split_hi(act, Unit(u.n0 + SLOTS, layer, i))
            units(act, first, FT, layer, body)

        def ffn_up_dve(dve, first, norm, call, layer):
            def body(u, j, i):
                n = tile_of(j, i) + call * FT
                g, up = bank[:, 2 * u.slot, :], bank[:, 2 * u.slot + 1, :]
                dve.wait_ge(unit_done, u.n + 1)
                dve.wait_ge(r_ready, norm + 1)
                dve.tensor_tensor(g, g, rbc[:, :], ALU.mult).then_inc(g_scaled, 1)
                dve.tensor_tensor(up, up, rbc[:, :], ALU.mult).then_inc(up_scaled, 1)
                dve.wait_ge(up_scaled, n + 1)
                dve.wait_ge(silu_done, n + 1)
                dve.tensor_tensor(up, up, silu[:, :], ALU.mult).then_inc(f_ready, 1)
                dve.wait_ge(f_hi_done, n + 1)
                dve.tensor_tensor(pick(f_lo, j, i), up, pick(f_hi, j, i), ALU.subtract).then_inc(f_lo_done, 1)
                split_lo(dve, Unit(u.n0 + SLOTS, layer, i))
            units(dve, first, FT, layer, body)

        def ffn_pe(pe, first, pre, norm, call, layer):
            linear_wide(pe, [Unit(first + s, layer) for s in range(3)],
                        lambda k: pe.wait_ge(pre_lo, pre * 8 + k + 1))
            stat_rows(pe, norm)
            units(pe, first + 3, FT - 3, layer, lambda u, j, i: linear(pe, u))
            down = first + FT
            with pe.Fori(0, 2) as i:
                for g in range(2):
                    for part in range(3):
                        u = Unit(down + g * 3 + part, layer)
                        n = i * 6 + u.n
                        if g == part == 0:
                            pe.wait_ge(f_lo_done, (call + 1) * FT)
                        pe.wait_ge(lo_ready, n + 1)
                        ks = range(8 * part, min(8 * part + 8, FT))
                        for m in range(2):
                            for k in ks:
                                mm = products(pe, u, m, k - 8 * part, k, g, k == 0, k == FT - 1, f_hi, f_lo)
                        mm.then_inc(unit_done, 1)

        block = ctx.enter_context(nc.Block())

        @block.sync
        def _(sp):
            for s in range(SLOTS):
                sp.dma_start(w_raw[:, s, :], w[s]).then_inc(raw_in[s], 16)
            with sp.Fori(1, UNITS // SLOTS) as i:
                for s in range(SLOTS):
                    sp.wait_ge(lo_ready, i * SLOTS + (s - 2))
                    sp.dma_start(w_raw[:, s, :], w[bass.ds(i * SLOTS + s, 1)].rearrange("o p c -> (o p) c"))\
                      .then_inc(raw_in[s], 16)
            sp.wait_ge(h_ready, 24 + 16 * LAYERS)
            sp.dma_start(out, h[:, :, :]).then_inc(out_done, 16)
            sp.wait_ge(out_done, 16)

        proj_ready, xin_scaled, vtok_ready, gate_done, gate_ready = (sem(n) for n in (
            "proj_ready", "xin_scaled", "vtok_ready", "gate_done", "gate_ready"))
        trig_step, sin_ready, wg_hi_ready, wg_lo_ready = (sem(n) for n in (
            "trig_step", "sin_ready", "wg_hi_ready", "wg_lo_ready"))
        rot_done, rope_cos, rope_sin, rope_done, kx_ready = (sem(n) for n in (
            "rot_done", "rope_cos", "rope_sin", "rope_done", "kx_ready"))
        xf_ready, xc_hi_ready, xc_lo_ready, hid_done, pecol_ready, hc_ready = (sem(n) for n in (
            "xf_ready", "xc_hi_ready", "xc_lo_ready", "hid_done", "pecol_ready", "hc_ready"))
        kc_done, vc_done, kc2_ready, kcrot_done, kc_rope, kcm_ready, kcm_dup, vblk_zero, vblk_ready = (
            sem(n) for n in ("kc_done", "vc_done", "kc2_ready", "kcrot_done", "kc_rope", "kcm_ready", "kcm_dup",
                             "vblk_zero", "vblk_ready"))
        conv_step, csq_ready, cstat_done, cstd_ready, cinv_ready, cn_ready, mix_hi, mix_lo = (sem(n) for n in (
            "conv_step", "csq_ready", "cstat_done", "cstd_ready", "cinv_ready", "cn_ready", "mix_hi", "mix_lo"))
        c_sub, c_sum, c_w = sem("cmp_sub"), sem("cmp_sum"), sem("cmp_weight")
        j_s, j_max, j_neg, j_exp, j_rec, j_w, j_t, j_pta, j_ptd, j_pv, j_o = (sem("job_" + n) for n in (
            "scores", "max", "neg", "exp", "recip", "weight", "turned", "turned_copied_act",
            "turned_copied_dve", "pv", "out"))
        ao_sq, ao_std, ao_inv, ao_n, ao_t = (sem("attn_norm_" + n) for n in ("squares", "std", "inv", "scaled", "turned"))
        JOBS = QB * 8

        def rope_tile(r):
            return qT[:, r, :] if r < 4 else kT[:, r - 4, :]

        def rot_pe(pe, r):
            pe.wait_ge(proj_ready, 12 + r + 1 if r < 4 else 18 + (r - 4) + 1)
            if r >= 2:
                pe.wait_ge(rope_done, r - 1)
            else:
                pe.wait_ge(rcol_std, 1)
                pe.wait_ge(std_ready, 1)
            pe.matmul(bank[:, STAT + r % 2, :], perm[:, :], rope_tile(r), start=True, stop=True).then_inc(rot_done, 1)

        def rope_pool(pool, r):
            pool.wait_ge(proj_ready, 12 + r + 1 if r < 4 else 18 + (r - 4) + 1)
            pool.wait_ge(sin_ready, 3)
            if r >= 2:
                pool.wait_ge(rope_done, r - 1)
            pool.tensor_tensor(ctmp[:, r % 2, :], rope_tile(r), cosT[:, :], ALU.mult).then_inc(rope_cos, 1)

        def rope_dve(dve, r):
            rot = bank[:, STAT + r % 2, :]
            dve.wait_ge(rot_done, r + 1)
            dve.wait_ge(sin_ready, 3)
            dve.tensor_tensor(rot, rot, sinT[:, :], ALU.mult).then_inc(rope_sin, 1)
            dve.wait_ge(rope_sin, r + 1)
            dve.wait_ge(rope_cos, r + 1)
            dve.tensor_tensor(rope_tile(r), ctmp[:, r % 2, :], rot, ALU.add).then_inc(rope_done, 1)

        def key_rows(t, tx, e, g):
            return (t if g == e else tx)[HD * e:HD * e + HD]

        def mixer1_pe(pe):
            pe.wait_ge(const_ready, 1)
            linear_wide(pe, [Unit(U_IN + s) for s in range(3)], lambda k: pe.wait_ge(pre_lo, k + 1))
            stat_columns(pe, 0, QB)
            stat_rows(pe, 0)
            pe.wait_ge(const_in, 48)
            for j in range(3, 10):
                linear(pe, Unit(U_IN + j))
                for r in {7: (0, 1), 8: (2, 3)}.get(j, ()):
                    rot_pe(pe, r)
            u = Unit(U_IN + 10)
            pe.wait_ge(lo_ready, u.n + 1)
            tokens_major(pe, u, x_hi, x_lo, QB, 0, 2 * P, lambda b_: (2 * u.slot + b_ // 2, b_ % 2 * 2 * P))\
                .then_inc(unit_done, 1)
            pe.wait_ge(wg_lo_ready, 1)
            pe.wait_ge(proj_ready, 18)
            for b_ in range(QB):
                for k in range(8):
                    xh, xl = x_hi[:, k, b_ * P:(b_ + 1) * P], x_lo[:, k, b_ * P:(b_ + 1) * P]
                    wh, wl = wg_hi[:, k * 24:(k + 1) * 24], wg_lo[:, k * 24:(k + 1) * 24]
                    dst = bank[:, 4, b_ * 24:(b_ + 1) * 24]
                    pe.matmul(dst, xh, wh, start=(k == 0), stop=False)
                    pe.matmul(dst, xl, wh, start=False, stop=False)
                    mm = pe.matmul(dst, xh, wl, start=False, stop=(k == 7))
            mm.then_inc(gate_done, 1)
            rot_pe(pe, 4)
            rot_pe(pe, 5)
            pe.wait_ge(proj_ready, 20)
            pe.wait_ge(xc_lo_ready, 1)
            for kv in range(2):
                if kv == 1:
                    pe.wait_ge(vtok_ready, QB)
                for part in range(2):
                    u = Unit(U_W1 + 2 * kv + part)
                    pe.wait_ge(lo_ready, u.n + 1)
                    for m in range(2):
                        for k in range(8):
                            c = 8 * part + k
                            wh, wl = ki(w_hi, u.slot)[:, k, m * P:(m + 1) * P], ki(w_lo, u.slot)[:, k, m * P:(m + 1) * P]
                            dst = bank[:, 2 * kv + m, 0:64]
                            pe.matmul(dst, wh, xc_hi[:, kv, c, :], start=(c == 0), stop=False)
                            pe.matmul(dst, wh, xc_lo[:, kv, c, :], start=False, stop=False)
                            mm = pe.matmul(dst, wl, xc_hi[:, kv, c, :], start=False, stop=(c == 15))
                    mm.then_inc(unit_done, 1)
            for m in range(4):
                pe.wait_ge(csq_ready, m + 1)
                mm = pe.matmul(bank[:, 5, :], ones[:, :], z[:, m, :], start=(m == 0), stop=(m == 3))
            mm.then_inc(cstat_done, 1)
            pe.wait_ge(hc_ready, 2)
            pe.wait_ge(rope_done, 6)
            for m in range(2):
                mm = pe.matmul(bank[0:HD, 6, 0:2 * NCMP], w2_s[:, 0, m, :], hc[:, 0, m, 0:2 * NCMP],
                               start=(m == 0), stop=(m == 1))
            mm.then_inc(kc_done, 1)
            pe.wait_ge(hc_ready, 4)
            pe.wait_ge(gate_ready, QB)
            for g in range(2):
                for m in range(2):
                    mm = pe.matmul(bank[0:NCMP, 4, g * HD:(g + 1) * HD], hc[:, 1, m, g * NCMP:(g + 1) * NCMP],
                                   w2_s[:, 1, m, :], start=(m == 0), stop=(m == 1))
            mm.then_inc(vc_done, 1)
            pe.wait_ge(kc2_ready, 1)
            pe.matmul(bank[0:HD, 7, 0:2 * NCMP], perm[0:HD, 0:HD], kc2[:, :, :].rearrange("p g c -> p (g c)"),
                      start=True, stop=True).then_inc(kcrot_done, 1)

            def c_scores(i):
                if i == 0:
                    pe.wait_ge(kcm_dup, 1)
                    pe.wait_ge(rope_done, 6)
                    pe.wait_ge(hc_ready, 4)
                    pe.wait_ge(mask_ready, 3)
                if i >= 2:
                    pe.wait_ge(c_sub, i - 1)
                for e in range(2):
                    b_ = 2 * (i % 2) + e
                    pe.matmul(bank[:, b_, 0:P], ident_b[:, :], cmask_b[:, i, :], start=True, stop=False)
                    for m in range(4):
                        mm = pe.matmul(bank[:, b_, m * 32:(m + 1) * 32], qT[HD * e:HD * e + HD, m, i * P:(i + 1) * P],
                                       kcm[HD * e:HD * e + HD, m // 2, :], start=False, stop=(m == 3))
                mm.then_inc(j_s, 1)

            def c_turn(i):
                pe.wait_ge(j_exp, i + 1)
                if i == 0:
                    pe.wait_ge(vblk_ready, 4)
                    pe.wait_ge(cstd_ready, 1)
                if i >= 2:
                    pe.wait_ge(j_pta, i - 1)
                for e in range(2):
                    mm = pe.transpose(bank[:, 4 + i % 2, e * P:(e + 1) * P], e_c[:, i % 2, e * P:(e + 1) * P], ident[:, :])
                mm.then_inc(j_t, 1)

            def c_values(i):
                pe.wait_ge(j_pta, i + 1)
                if i == 0:
                    pe.wait_ge(kc_rope, 3)
                if i >= 2:
                    pe.wait_ge(j_o, i - 1)
                for e in range(2):
                    mm = pe.matmul(bank[:, 6 + i % 2, e * 4 * HD:(e + 1) * 4 * HD], pt_c[:, i % 2, e * P:(e + 1) * P],
                                   vblk[:, :], start=True, stop=True)
                mm.then_inc(j_pv, 1)

            for t in range(QB + 2):
                if t < QB:
                    c_scores(t)
                if 0 <= t - 1 < QB:
                    c_turn(t - 1)
                if t >= 2:
                    c_values(t - 2)

            def scores(j):
                i, hd = j // 8, j % 8
                m, e, g = hd // 2, hd % 2, hd // 4
                n = (i + 1) * P
                if j == 0:
                    pe.wait_ge(kx_ready, 4)
                if j < 2:
                    pe.wait_ge(c_sub, QB)
                else:
                    pe.wait_ge(j_exp, QB + 2 * (j - 1))
                for br in range(2):
                    b_ = 2 * (j % 2) + br
                    pe.matmul(bank[:, b_, 0:n], qT[HD * e:HD * e + HD, m, i * P:(i + 1) * P],
                              key_rows(kT, kTx, e, g)[:, br, 0:n], start=True, stop=False)
                    mm = pe.matmul(bank[:, b_, i * P:n], ident_b[:, :], mask_b[:, P:2 * P], start=False, stop=True)
                mm.then_inc(j_s, 1)

            def turn(j):
                i = j // 8
                pe.wait_ge(j_exp, QB + 2 * (j + 1))
                if j == 0:
                    pe.wait_ge(j_pta, QB)
                else:
                    pe.wait_ge(j_pta, QB + j)
                    pe.wait_ge(j_ptd, j)
                for br in range(2):
                    for k in range(i + 1):
                        mm = pe.transpose(bank[:, 4 + br, k * P:(k + 1) * P], prob[:, j % 2, br, k * P:(k + 1) * P], ident[:, :])
                mm.then_inc(j_t, 1)

            def values(j):
                i, g = j // 8, j % 8 // 4
                pe.wait_ge(j_pta, QB + j + 1)
                pe.wait_ge(j_ptd, j + 1)
                if j < 2:
                    pe.wait_ge(j_o, QB)
                else:
                    pe.wait_ge(j_o, QB + 2 * (j - 1))
                for br in range(2):
                    for k in range(i + 1):
                        mm = pe.matmul(bank[:, 6 + j % 2, br * HD:(br + 1) * HD], probT[:, j % 2, br, k * P:(k + 1) * P],
                                       vtok[:, k, br * P + g * HD:br * P + (g + 1) * HD], start=(k == 0), stop=(k == i))
                mm.then_inc(j_pv, 1)

            for t in range(JOBS + 2):
                if t < JOBS:
                    scores(t)
                if 0 <= t - 1 < JOBS:
                    turn(t - 1)
                if t >= 2:
                    values(t - 2)

            pe.wait_ge(j_exp, QB + 2 * JOBS)
            for b_ in range(QB):
                pe.wait_ge(ao_n, b_ + 1)
                for m in range(4):
                    mm = pe.transpose(bank[:, b_, m * P:(m + 1) * P], o_all[:, b_, m * P:(m + 1) * P], ident[:, :])
                mm.then_inc(ao_t, 1)
            pe.wait_ge(j_o, QB)
            pe.wait_ge(j_o, QB + 2 * JOBS)
            stat_columns(pe, NORM_MEM, 2)
            stat_rows(pe, NORM_MEM, MEM)

            def mixed(k):
                pe.wait_ge(mix_lo, k + 1)
            pe.wait_ge(mix_lo, 8)
            linear_wide(pe, [Unit(U_OUT + s) for s in range(3)], mixed)
            linear(pe, Unit(U_OUT + 3))
            stat_rows_after_std(pe, NORM_MIXP)

        def stat_rows_after_std(pe, n):
            pe.wait_ge(std_ready, n)
            stat_rows(pe, n)

        def mixer1_act(act):
            act.dma_start(gains[:, :], pack).then_inc(const_in, 16)
            for k in range(0, DT, 2):
                act.dma_start(h[:, k:k + 2, :], x[:, k * T:(k + 2) * T].rearrange("p (k t) -> p k t", k=2)).then_inc(x_in[k // 2], 16)
            act.dma_start(ident[:, :], tables[:, 0:P]).then_inc(const_in, 16)
            act.dma_start(perm[:, :], tables[:, P:2 * P]).then_inc(const_in, 16)
            act.dma_start(pos_i[:, :], pos.to_broadcast([P, T])).then_inc(pos_in, 16)
            act.dma_start(stage[:, 0:6 * P], cmask).then_inc(tab_in, 16)
            act.dma_start(w2_s[:, :, :, :].rearrange("p a m d -> p (a m d)"), w2).then_inc(tab_in, 16)
            act.dma_start(wg_s[:, :], wg).then_inc(tab_in, 16)
            split_hi(act, Unit(0))
            act.wait_ge(const_in, 48)
            for k in range(DT):
                if k % 2 == 0:
                    act.wait_ge(x_in[k // 2], 16)
                pre_norm_hi(act, 0, NORM_MIX, k, "mix_pre")
                if k in (0, 1):
                    split_hi(act, Unit(1 + k))
            act.wait_ge(const_ready, 2)
            std_rows(act, NORM_MIX)
            std_columns(act, 0, QB)
            act.wait_ge(tab_in, 48)
            act.activation(ident_b[:, :], ident[:, :], ACT.Copy).then_inc(mask_ready, 1)
            act.activation(mask_b[:, :], stage[:, 0:2 * P], ACT.Copy).then_inc(mask_ready, 1)
            act.activation(cmask_b[:, :, :].rearrange("p b c -> p (b c)"), stage[:, 2 * P:6 * P], ACT.Copy).then_inc(mask_ready, 1)
            act.activation(wg_hi[:, :], wg_s[:, :], ACT.Copy).then_inc(wg_hi_ready, 1)
            act.wait_ge(trig_step, 8)
            act.wait_ge(const_ready, 2)
            act.activation(sinT[:, :], ctmp[:, 1, :], ACT.Sin).then_inc(sin_ready, 1)
            act.activation(cosT[:, :], ctmp[:, 1, :], ACT.Abs).then_inc(sin_ready, 1)
            act.wait_ge(sin_ready, 2)
            act.activation(cosT[:, :], cosT[:, :], ACT.Sin, bias=eps_c[:, 2:3], scale=-1.0).then_inc(sin_ready, 1)
            for j in range(9):
                split_hi(act, Unit(U_IN + j + 3))
            act.wait_ge(proj_ready, 18)
            for kv in range(2):
                for g in range(2):
                    for par in range(2):
                        for half in range(2):
                            v = kvc[g * HD:(g + 1) * HD, kv, 16 * half:16 * half + 16 * NCMP]\
                                .rearrange("p (c j q) -> p j c q", j=8, q=2)[:, :, :, par]
                            act.activation(xf[par * HD:(par + 1) * HD, kv, 8 * half:8 * half + 8, g * NCMP:(g + 1) * NCMP],
                                           v, ACT.Copy).then_inc(xf_ready, 1)
                pe_col = gains[:, _cols["pe_v" if kv else "pe_k"][0]:][:, 0:16]
                act.activation(xf[:, kv, :, 2 * NCMP:64], pe_col.unsqueeze(2).to_broadcast([P, 16, 2]), ACT.Copy).then_inc(xf_ready, 1)
            act.wait_ge(xf_ready, 18)
            for kv in range(2):
                act.activation(xc_hi[:, kv, :, :], xf[:, kv, :, :], ACT.Copy).then_inc(xc_hi_ready, 1)
            split_hi(act, Unit(U_IN + 12))
            act.wait_ge(unit_done, U_IN + 11)
            act.wait_ge(rcol_ready, 1)
            for b_ in range(QB):
                act.activation(vtok[:, b_, :], bank[:, 2 + b_ // 2, b_ % 2 * 2 * P:(b_ % 2 + 1) * 2 * P], ACT.Copy,
                               scale=rcol[:, b_:b_ + 1]).then_inc(vtok_ready, 1)
            split_hi(act, Unit(U_IN + 13))
            act.wait_ge(gate_done, 1)
            for b_ in range(QB):
                act.activation(gate[:, b_, :], bank[:, 4, b_ * 24:(b_ + 1) * 24], ACT.Sigmoid,
                               scale=rcol[:, b_:b_ + 1]).then_inc(gate_ready, 1)
            for r in range(2):
                act.wait_ge(rope_done, 5 + r)
                act.activation(kTx[0:HD, r, :], kT[HD:P, r, :], ACT.Copy).then_inc(kx_ready, 1)
                act.activation(kTx[HD:P, r, :], kT[0:HD, r, :], ACT.Copy).then_inc(kx_ready, 1)
            split_hi(act, Unit(U_IN + 14))
            for m in range(4):
                act.wait_ge(conv_step, 12 + m + 1)
                act.activation(z[:, m, :], cv[:, m, :], ACT.Square).then_inc(csq_ready, 1)
            for u in range(U_W1 + 1, U_W1 + 4):
                split_hi(act, Unit(u + 3))
            act.wait_ge(cstat_done, 1)
            act.activation(ctmp[:, 0, :], bank[:, 5, :], ACT.Sqrt, bias=eps_c[:, 0:1], scale=1.0 / 512).then_inc(cstd_ready, 1)
            for kv in range(2):
                act.wait_ge(unit_done, U_W1 + 2 * kv + 2)
                for m in range(2):
                    act.activation(pecol[:, kv, m:m + 1], bank[:, 2 * kv + m, 2 * NCMP:2 * NCMP + 1], ACT.Copy).then_inc(pecol_ready, 1)
                for m in range(2):
                    act.wait_ge(pecol_ready, 2 * kv + m + 1)
                    act.activation(hc[:, kv, m, :], bank[:, 2 * kv + m, 0:64], ACT.Silu, bias=pecol[:, kv, m:m + 1]).then_inc(hc_ready, 1)
            act.wait_ge(kc_done, 1)
            act.activation(kc2[:, :, :].rearrange("p g c -> p (g c)"), bank[0:HD, 6, 0:2 * NCMP], ACT.Copy).then_inc(kc2_ready, 1)
            act.wait_ge(vc_done, 1)
            act.wait_ge(vblk_zero, 1)
            for m in range(4):
                act.activation(vblk[m * 32:m * 32 + NCMP, m * HD:(m + 1) * HD], bank[0:NCMP, 4, (m // 2) * HD:(m // 2 + 1) * HD],
                               ACT.Copy).then_inc(vblk_ready, 1)
            act.wait_ge(kcm_ready, 1)
            act.activation(kcm[HD:P, :, :], kcm[0:HD, :, :], ACT.Copy).then_inc(kcm_dup, 1)
            act.wait_ge(gate_done, 1)
            for m in range(4):
                act.wait_ge(cn_ready, m + 1)
                act.activation(x_hi[:, m, :], cv[:, m, :], ACT.Copy, scale=col("conv_out", m)).then_inc(mix_hi, 1)

            def c_e(i):
                act.wait_ge(c_sub, i + 1)
                act.activation(e_c[:, i % 2, :], e_c[:, i % 2, :], ACT.Exp).then_inc(j_exp, 1)

            def c_copy(i):
                act.wait_ge(j_t, i + 1)
                if i >= 2:
                    act.wait_ge(j_pv, i - 1)
                act.activation(pt_c[:, i % 2, :], bank[:, 4 + i % 2, 0:2 * P], ACT.Copy).then_inc(j_pta, 1)

            for t in range(QB + 1):
                if t < QB:
                    c_e(t)
                if t >= 1:
                    c_copy(t - 1)

            def exps(j):
                n = (j // 8 + 1) * P
                act.wait_ge(j_neg, QB + j + 1)
                if j >= 2:
                    act.wait_ge(j_t, QB + j - 1)
                if j >= 4:
                    act.wait_ge(j_rec, j - 3)
                for br in range(2):
                    act.activation(prob[:, j % 2, br, 0:n], bank[:, 2 * (j % 2) + br, 0:n], ACT.Exp,
                                   bias=jsm(j, 2, br), accum_out=jsm(j, 4, br)).then_inc(j_exp, 1)

            def copy_turned(j):
                n = (j // 8 + 1) * P
                act.wait_ge(j_t, QB + j + 1)
                if j >= 2:
                    act.wait_ge(j_pv, QB + j - 1)
                act.activation(probT[:, j % 2, 0, 0:n], bank[:, 4, 0:n], ACT.Copy).then_inc(j_pta, 1)

            act.wait_ge(unit_done, U_OUT)
            for t in range(JOBS + 1):
                if t < JOBS:
                    exps(t)
                if t >= 1:
                    copy_turned(t - 1)

            act.dma_start(memT[:, :, :].rearrange("p k t -> p (k t)"), mem).then_inc(mem_in, 16)
            act.wait_ge(j_pv, QB + JOBS)
            for b_ in range(QB):
                act.wait_ge(j_o, QB + 2 * 8 * (b_ + 1))
                if b_ >= 2:
                    act.wait_ge(ao_sq, b_ - 1)
                act.activation(probT[:, b_ % 2, 0, :], o_all[:, b_, :], ACT.Square, accum_out=small[:, 32 + b_:33 + b_]).then_inc(ao_sq, 1)
            act.wait_ge(ao_sq, QB)
            act.activation(small[:, 36:40], small[:, 32:36], ACT.Sqrt, bias=eps_c[:, 0:1], scale=1.0 / 512).then_inc(ao_std, 1)
            act.wait_ge(mem_in, 16)
            for k in range(DT):
                act.activation(m_hi[:, k, :], memT[:, k, :], ACT.Copy, scale=col("mem", k)).then_inc(mem_hi, 1)
                square(act, NORM_MEM, k, memT[:, k, :], MEM)
            act.wait_ge(ao_t, QB)
            for m in range(4):
                act.activation(x_hi[:, 4 + m, :].rearrange("p (b t) -> p b t", b=QB), bank[:, 0:QB, m * P:(m + 1) * P],
                               ACT.Copy, scale=col("attn_out", m)).then_inc(mix_hi, 1)
            std_columns(act, 1, 2)
            std_rows_after(act, NORM_MEM, MEM)

        def std_rows_after(act, n, width=T):
            act.wait_ge(r_ready, n)
            std_rows(act, n, width)

        def jsm(j, a_, br=None):
            c = 16 * (j % 4) + a_
            return jcol[:, c:c + 2] if br is None else jcol[:, c + br:c + br + 1]

        def mixer1_dve(dve):
            split_lo(dve, Unit(0))
            for k in range(DT):
                pre_norm_lo(dve, 0, k, "mix_pre")
                if k in (0, 1):
                    split_lo(dve, Unit(1 + k))
            ang, red = ctmp[:, 0, :], ctmp[:, 1, :]
            dve.wait_ge(pos_in, 16)
            dve.tensor_copy(red, pos_i[:, :]).then_inc(trig_step, 1)
            dve.wait_ge(trig_step, 1)
            dve.tensor_scalar(ang, red, col("inv"), None, ALU.mult).then_inc(trig_step, 1)
            dve.wait_ge(trig_step, 2)
            dve.tensor_scalar(sinT[:, :], ang, 1 / (2 * np.pi), ROUNDER, ALU.mult, ALU.add).then_inc(trig_step, 1)
            dve.wait_ge(trig_step, 3)
            dve.tensor_scalar(sinT[:, :], sinT[:, :], -ROUNDER, None, ALU.add).then_inc(trig_step, 1)
            for n, c in enumerate((C1, C2, C3)):
                dve.wait_ge(trig_step, 4 + n)
                dve.scalar_tensor_tensor(out=red, in0=sinT[:, :], scalar=-c, in1=ang if n == 0 else red,
                                         op0=ALU.mult, op1=ALU.add).then_inc(trig_step, 1)
            dve.wait_ge(trig_step, 7)
            dve.tensor_scalar(red, red, float(np.float32(3.1415925)), -float(np.float32(3.1415925)), ALU.min, ALU.max).then_inc(trig_step, 1)
            inv_rows(dve, NORM_MIX)
            dve.wait_ge(r_ready, NORM_MIX + 1)
            inv_columns(dve, 0, QB)
            dve.wait_ge(wg_hi_ready, 1)
            dve.tensor_tensor(wg_lo[:, :], wg_s[:, :], wg_hi[:, :], ALU.subtract).then_inc(wg_lo_ready, 1)

            for j in range(10):
                u = Unit(U_IN + j)
                dve.wait_ge(unit_done, u.n + 1)
                for m in range(2):
                    src, k = bank[:, 2 * u.slot + m, :], 2 * (j % 2) + m
                    if j < 2:
                        dve.tensor_tensor(bg[:, k, :], src, rbc[:, :], ALU.mult).then_inc(proj_ready, 1)
                    elif j < 4:
                        dve.tensor_tensor(z[:, k, :], src, rbc[:, :], ALU.mult).then_inc(proj_ready, 1)
                    elif j < 6:
                        dve.tensor_tensor(src, src, rbc[:, :], ALU.mult).then_inc(xin_scaled, 1)
                    elif j < 8:
                        dve.scalar_tensor_tensor(out=qT[:, k, :], in0=src, scalar=HD ** -0.5, in1=rbc[:, :],
                                                 op0=ALU.mult, op1=ALU.mult).then_inc(proj_ready, 1)
                    else:
                        dve.tensor_tensor((kvc if j == 8 else kT)[:, m, :], src, rbc[:, :], ALU.mult).then_inc(proj_ready, 1)
                if j in (4, 5):
                    for m in range(2):
                        k = 2 * (j % 2) + m
                        dve.wait_ge(xin_scaled, k + 1)
                        dve.tensor_tensor(z[:, k, :], z[:, k, :], bank[:, 2 * u.slot + m, :], ALU.mult).then_inc(proj_ready, 1)
                split_lo(dve, Unit(U_IN + j + 3))
                for r in {8: (0, 1), 9: (2, 3)}.get(j, ()):
                    rope_dve(dve, r)
            dve.wait_ge(xc_hi_ready, 2)
            dve.tensor_tensor(xc_lo[:, :, :, :].rearrange("p v j c -> p (v j c)"), xf[:, :, :, :].rearrange("p v j c -> p (v j c)"),
                              xc_hi[:, :, :, :].rearrange("p v j c -> p (v j c)"), ALU.subtract).then_inc(xc_lo_ready, 1)
            split_lo(dve, Unit(U_IN + 13))
            rope_dve(dve, 4)
            rope_dve(dve, 5)
            for step in range(4):
                for m in range(4):
                    if step:
                        dve.wait_ge(conv_step, 4 * (step - 1) + m + 1)
                    else:
                        dve.wait_ge(proj_ready, 12)
                        dve.wait_ge(mask_ready, 3)
                    wk = lambda k: col("conv_w", 3 * m + k)
                    if step == 0:
                        ins = dve.tensor_scalar(cv[:, m, :], z[:, m, :], wk(2), None, ALU.mult)
                    elif step < 3:
                        ins = dve.scalar_tensor_tensor(out=cv[:, m, step:T], in0=z[:, m, 0:T - step], scalar=wk(2 - step),
                                                       in1=cv[:, m, step:T], op0=ALU.mult, op1=ALU.add)
                    else:
                        ins = dve.tensor_tensor(cv[:, m, :], cv[:, m, :], bg[:, m, :], ALU.mult)
                    ins.then_inc(conv_step, 1)
            for j in range(14, 18):
                split_lo(dve, Unit(j))
            dve.wait_ge(cstd_ready, 1)
            dve.reciprocal(ctmp[:, 0, :], ctmp[:, 0, :]).then_inc(cinv_ready, 1)
            dve.wait_ge(cinv_ready, 1)
            for m in range(4):
                dve.tensor_tensor(cv[:, m, :], cv[:, m, :], ctmp[:, 0, :], ALU.mult).then_inc(cn_ready, 1)
            ends = slice(31, T, 16)
            dve.wait_ge(kc2_ready, 1)
            dve.wait_ge(kcrot_done, 1)
            rot = bank[0:HD, 7, 0:2 * NCMP].rearrange("p (g c) -> p g c", g=2)
            dve.tensor_tensor(rot, rot, sinT[0:HD, ends].unsqueeze(1).to_broadcast([HD, 2, NCMP]), ALU.mult).then_inc(kc_rope, 1)
            dve.tensor_tensor(kc2[:, :, :], kc2[:, :, :], cosT[0:HD, ends].unsqueeze(1).to_broadcast([HD, 2, NCMP]), ALU.mult).then_inc(kc_rope, 1)
            dve.wait_ge(kc_rope, 2)
            dve.tensor_tensor(kc2[:, :, :], kc2[:, :, :], rot, ALU.add).then_inc(kc_rope, 1)
            dve.wait_ge(kc_rope, 3)
            dve.wait_ge(vblk_zero, 1)
            dve.tensor_copy(kcm[0:HD, :, 0:NCMP], kc2[:, :, :]).then_inc(kcm_ready, 1)
            for m in range(4):
                dve.wait_ge(mix_hi, m + 1)
                dve.scalar_tensor_tensor(out=x_lo[:, m, :], in0=cv[:, m, :], scalar=col("conv_out", m), in1=x_hi[:, m, :],
                                         op0=ALU.mult, op1=ALU.subtract).then_inc(mix_lo, 1)

            def csm(i, a_):
                return small[:, 32 * (i % 2) + a_:32 * (i % 2) + a_ + 8]

            def c_softmax(i):
                s = bank[:, 2 * (i % 2):2 * (i % 2) + 2, 0:P].rearrange("p e (m c) -> p e m c", c=32)
                v = lambda t: t.rearrange("p (e m) -> p e m", e=2)
                dve.wait_ge(j_s, i + 1)
                if i >= 2:
                    dve.wait_ge(j_t, i - 1)
                dve.tensor_reduce(v(csm(i, 0)), s, AX, ALU.max).then_inc(j_max, 1)
                dve.wait_ge(j_max, i + 1)
                dve.tensor_scalar(csm(i, 8), csm(i, 0), LOW, -1.0, ALU.max, ALU.mult).then_inc(j_neg, 1)
                dve.wait_ge(j_neg, i + 1)
                dve.tensor_tensor(e_c[:, i % 2, :].rearrange("p (e m c) -> p e m c", e=2, m=4), s,
                                  v(csm(i, 8)).unsqueeze(3).to_broadcast([P, 2, 4, 32]), ALU.add).then_inc(c_sub, 1)

            def c_weights(i):
                dve.wait_ge(j_exp, i + 1)
                dve.tensor_reduce(csm(i, 16), e_c[:, i % 2, :].rearrange("p (h c) -> p h c", c=32), AX, ALU.add).then_inc(c_sum, 1)
                dve.wait_ge(c_sum, i + 1)
                dve.tensor_scalar(csm(i, 16), csm(i, 16), 1e-30, None, ALU.max).then_inc(c_w, 1)
                dve.wait_ge(c_w, 3 * i + 1)
                dve.reciprocal(csm(i, 16), csm(i, 16)).then_inc(c_w, 1)
                dve.wait_ge(c_w, 3 * i + 2)
                g0 = gate[:, i, :].rearrange("p (m e b) -> p e m b", e=2, b=3)[:, :, :, 0]
                dve.tensor_tensor(csm(i, 24).rearrange("p (e m) -> p e m", e=2), csm(i, 16).rearrange("p (e m) -> p e m", e=2),
                                  g0, ALU.mult).then_inc(c_w, 1)

            def c_combine(i):
                dve.wait_ge(j_pv, i + 1)
                dve.wait_ge(c_w, 3 * i + 3)
                dve.tensor_tensor(o_all[:, i, :].rearrange("p (m e d) -> p e m d", e=2, d=HD),
                                  bank[:, 6 + i % 2, :].rearrange("p (e m d) -> p e m d", e=2, d=HD),
                                  csm(i, 24).rearrange("p (e m) -> p e m", e=2).unsqueeze(3).to_broadcast([P, 2, 4, HD]),
                                  ALU.mult).then_inc(j_o, 1)

            dve.wait_ge(gate_ready, QB)
            for t in range(QB + 2):
                if t < QB:
                    c_softmax(t)
                if 0 <= t - 1 < QB:
                    c_weights(t - 1)
                if t >= 2:
                    c_combine(t - 2)

            def maxima(j):
                n = (j // 8 + 1) * P
                dve.wait_ge(j_s, QB + j + 1)
                if j >= 4:
                    dve.wait_ge(j_exp, QB + 2 * (j - 3))
                dve.tensor_reduce(jsm(j, 0), bank[:, 2 * (j % 2):2 * (j % 2) + 2, 0:n], AX, ALU.max).then_inc(j_max, 1)
                dve.wait_ge(j_max, QB + j + 1)
                dve.tensor_scalar(jsm(j, 2), jsm(j, 0), LOW, -1.0, ALU.max, ALU.mult).then_inc(j_neg, 1)

            def copy_turned(j):
                n = (j // 8 + 1) * P
                dve.wait_ge(j_t, QB + j + 1)
                if j >= 2:
                    dve.wait_ge(j_pv, QB + j - 1)
                dve.tensor_copy(probT[:, j % 2, 1, 0:n], bank[:, 5, 0:n]).then_inc(j_ptd, 1)

            def combine(j):
                i, hd = j // 8, j % 8
                dve.wait_ge(j_exp, QB + 2 * (j + 1))
                dve.reciprocal(jsm(j, 6), jsm(j, 4)).then_inc(j_rec, 1)
                dve.wait_ge(j_rec, j + 1)
                dve.tensor_tensor(jsm(j, 8), jsm(j, 6), gate[:, i, 3 * hd + 1:3 * hd + 3], ALU.mult).then_inc(j_w, 1)
                dve.wait_ge(j_w, j + 1)
                dve.wait_ge(j_pv, QB + j + 1)
                o = o_all[:, i, hd * HD:(hd + 1) * HD]
                for br in range(2):
                    if br:
                        dve.wait_ge(j_o, QB + 2 * j + 1)
                    else:
                        dve.wait_ge(j_o, i + 1)
                    dve.scalar_tensor_tensor(out=o, in0=bank[:, 6 + j % 2, br * HD:(br + 1) * HD], scalar=jsm(j, 8, br), in1=o,
                                             op0=ALU.mult, op1=ALU.add).then_inc(j_o, 1)

            for t in range(JOBS + 2):
                if t < JOBS:
                    maxima(t)
                if 0 <= t - 1 < JOBS:
                    copy_turned(t - 1)
                if t >= 2:
                    combine(t - 2)

            dve.wait_ge(ao_std, 1)
            dve.reciprocal(small[:, 36:40], small[:, 36:40]).then_inc(ao_inv, 1)
            dve.wait_ge(ao_inv, 1)
            for b_ in range(QB):
                dve.tensor_scalar(o_all[:, b_, :], o_all[:, b_, :], small[:, 36 + b_:37 + b_], None, ALU.mult).then_inc(ao_n, 1)
            for k in range(DT):
                dve.wait_ge(mem_hi, k + 1)
                dve.scalar_tensor_tensor(out=m_lo[:, k, :], in0=memT[:, k, :], scalar=col("mem", k), in1=m_hi[:, k, :],
                                         op0=ALU.mult, op1=ALU.subtract).then_inc(mem_lo, 1)
            dve.wait_ge(mix_hi, 8)
            for m in range(4):
                dve.scalar_tensor_tensor(out=x_lo[:, 4 + m, :].rearrange("p (b t) -> p b t", b=QB), in0=bank[:, 0:QB, m * P:(m + 1) * P],
                                         scalar=col("attn_out", m), in1=x_hi[:, 4 + m, :].rearrange("p (b t) -> p b t", b=QB),
                                         op0=ALU.mult, op1=ALU.subtract).then_inc(mix_lo, 1)
            inv_columns(dve, 1, 2)
            dve.wait_ge(std_ready, NORM_MEM + 1)
            dve.reciprocal(rmem[:, :], rbc[:, 0:MEM]).then_inc(r_ready, 1)

        kx_done, vx_done, qx_done = sem("kx_done"), sem("vx_done"), sem("qx_done")
        x_back, ox_hi, ox_lo = sem("x_back"), sem("ox_hi"), sem("ox_lo")
        X_1, X_2, X_REC = QB + JOBS, QB + 2 * JOBS, JOBS
        XJOBS = QB * 2

        def xsm(j, a_, e=None):
            c = 8 * (j % 4) + a_
            return small[:, c:c + 2] if e is None else small[:, c + e:c + e + 1]

        def cross_pe(pe):
            pe.wait_ge(mem_lo, DT)
            for j in range(4):
                linear(pe, Unit(U_KV + j), m_hi, m_lo, MEM)
            for j in range(4, 8):
                u = Unit(U_KV + j)
                pe.wait_ge(lo_ready, u.n + 1)
                tokens_major(pe, u, m_hi, m_lo, 2, 0, 2 * P, lambda b_: (2 * u.slot + b_, 0)).then_inc(unit_done, 1)
            linear_wide(pe, [Unit(U_QX + s) for s in range(3)], lambda k: pe.wait_ge(pre_lo, 8 + k + 1))
            stat_rows_after_std(pe, NORM_X)
            linear(pe, Unit(U_QX + 3))

            def scores(j):
                i, hp = j // 2, j % 2
                if j == 0:
                    pe.wait_ge(qx_done, DT)
                    pe.wait_ge(kx_done, DT)
                if j >= 2:
                    pe.wait_ge(j_exp, X_2 + 2 * (j - 1))
                for e in range(2):
                    for d in range(2):
                        tile = 4 * hp + 2 * e + d
                        mm = pe.matmul(bank[:, j % 2, e * MEM:(e + 1) * MEM], qx[:, tile, i * P:(i + 1) * P], kx[:, tile, :],
                                       start=(d == 0), stop=(d == 1))
                mm.then_inc(j_s, 1)

            def turn(j):
                pe.wait_ge(j_exp, X_2 + 2 * (j + 1))
                if j >= 2:
                    pe.wait_ge(j_pta, X_1 + j - 1)
                for c in range(4):
                    mm = pe.transpose(bank[:, 2 + j % 2, c * P:(c + 1) * P],
                                      xprob[:, j % 2, c // 2, c % 2 * P:(c % 2 + 1) * P], ident[:, :])
                mm.then_inc(j_t, 1)

            def values(j):
                hp = j % 2
                pe.wait_ge(j_pta, X_1 + j + 1)
                pe.wait_ge(vx_done, 8)
                if j >= 2:
                    pe.wait_ge(j_o, X_2 + j - 1)
                for e in range(2):
                    for c in range(2):
                        mm = pe.matmul(bank[:, 4 + j % 2, e * MEM:(e + 1) * MEM], xprobT[:, j % 2, 2 * e + c, :],
                                       vx[:, c, (2 * hp + e) * 256:(2 * hp + e + 1) * 256], start=(c == 0), stop=(c == 1))
                mm.then_inc(j_pv, 1)

            def back(j):
                pe.wait_ge(j_o, X_2 + j + 1)
                pe.wait_ge(r_ready, NORM_X + 1)
                if j >= 2:
                    pe.wait_ge(ox_lo, j - 1)
                for c in range(4):
                    mm = pe.transpose(bank[:, 6 + j % 2, c * P:(c + 1) * P], xo[:, j % 2, c * P:(c + 1) * P], ident[:, :])
                mm.then_inc(x_back, 1)

            for t in range(XJOBS + 3):
                if t < XJOBS:
                    scores(t)
                if 0 <= t - 1 < XJOBS:
                    turn(t - 1)
                if 0 <= t - 2 < XJOBS:
                    values(t - 2)
                if t >= 3:
                    back(t - 3)
            pe.wait_ge(ox_lo, XJOBS)
            for j in range(4):
                linear(pe, Unit(U_OX + j))
            stat_rows_after_std(pe, NORM_XP)
            ffn_pe(pe, U_GU, 2, NORM_F, 0, None)
            stat_rows_after_std(pe, NORM_FP)

        def out_evac_act(act, first, n, y, base):
            for j in range(4):
                u = Unit(first + j)
                act.wait_ge(unit_done, u.n + 1)
                for m in range(2):
                    k = 2 * j + m
                    src = bank[:, 2 * u.slot + m, :]
                    act.activation(y[:, k, :], src, ACT.Copy).then_inc(y_ready, 1)
                    square(act, n, k, src)
                split_hi(act, Unit(u.n0 + 3))

        def post_norm_dve(dve, q, n, y, gain, pre, pre_gain):
            inv_rows(dve, n)
            dve.wait_ge(r_ready, n + 1)
            for k in range(DT + 2):
                if k < DT:
                    dve.wait_ge(y_ready, 8 * q + k + 1)
                    dve.tensor_tensor(y[:, k, :], y[:, k, :], rbc[:, :], ALU.mult).then_inc(t_ready, 1)
                if 0 <= k - 1 < DT:
                    dve.wait_ge(t_ready, 8 * q + k)
                    dve.scalar_tensor_tensor(out=h[:, k - 1, :], in0=y[:, k - 1, :], scalar=col(gain, k - 1), in1=h[:, k - 1, :],
                                             op0=ALU.mult, op1=ALU.add).then_inc(h_ready, 1)
                if k >= 2 and pre is not None:
                    dve.wait_ge(h_ready, 8 * q + k - 1)
                    pre_norm_lo(dve, pre, k - 2, pre_gain)

        def cross_act(act):
            out_evac_act(act, U_OUT, NORM_MIXP, yb, 0)
            std_rows_after(act, NORM_MIXP)
            for k in range(DT):
                act.wait_ge(h_ready, k + 1)
                pre_norm_hi(act, 1, NORM_X, k, "x_pre")
            for j in range(8):
                u = Unit(U_KV + j)
                if j >= 4:
                    act.wait_ge(unit_done, u.n + 1)
                    for b_ in range(2):
                        act.activation(vx[:, b_, (j - 4) * 256:(j - 3) * 256], bank[:, 2 * u.slot + b_, 0:2 * P], ACT.Copy,
                                       scale=rcol[:, b_:b_ + 1]).then_inc(vx_done, 1)
                split_hi(act, Unit(u.n0 + 3))
            std_rows_after(act, NORM_X)
            for j in range(4):
                split_hi(act, Unit(U_QX + j + 3))

            def exps(j):
                act.wait_ge(j_neg, X_1 + j + 1)
                if j >= 2:
                    act.wait_ge(j_t, X_1 + j - 1)
                for e in range(2):
                    act.activation(xprob[:, j % 2, e, :], bank[:, j % 2, e * MEM:(e + 1) * MEM], ACT.Exp, bias=xsm(j, 2, e),
                                   accum_out=xsm(j, 4, e)).then_inc(j_exp, 1)

            def copy_turned(j):
                act.wait_ge(j_t, X_1 + j + 1)
                if j >= 2:
                    act.wait_ge(j_pv, X_1 + j - 1)
                act.activation(xprobT[:, j % 2, :, :].rearrange("p c t -> p (c t)"), bank[:, 2 + j % 2, :], ACT.Copy)\
                   .then_inc(j_pta, 1)

            def split_back(j):
                i, hp = j // 2, j % 2
                act.wait_ge(x_back, j + 1)
                act.activation(x_hi[:, 4 * hp:4 * hp + 4, i * P:(i + 1) * P], bank[:, 6 + j % 2, :].rearrange("p (c t) -> p c t", c=4),
                               ACT.Copy).then_inc(ox_hi, 1)

            for t in range(XJOBS + 3):
                if t < XJOBS:
                    exps(t)
                if 0 <= t - 1 < XJOBS:
                    copy_turned(t - 1)
                if t >= 3:
                    split_back(t - 3)
            out_evac_act(act, U_OX, NORM_XP, yb, 1)
            std_rows_after(act, NORM_XP)
            for k in range(DT):
                act.wait_ge(h_ready, 8 + k + 1)
                pre_norm_hi(act, 2, NORM_F, k, "ffn_pre")
            std_rows_after(act, NORM_F)
            ffn_up_act(act, U_GU, 0, None)
            for g in range(4):
                for part in range(3):
                    u = Unit(U_DN + 3 * g + part)
                    act.wait_ge(unit_done, u.n + 1)
                    if part == 2:
                        for m in range(2):
                            k, src = 2 * g + m, bank[:, 2 * (g % 2) + m, :]
                            act.activation(y_ffn[:, k, :], src, ACT.Copy).then_inc(y_ready, 1)
                            square(act, NORM_FP, k, src)
                    if g < 3:
                        split_hi(act, Unit(u.n0 + 3))
            std_rows_after(act, NORM_FP)

        def cross_dve(dve):
            for j in range(4):
                split_lo(dve, Unit(U_OUT + j + 3))
            post_norm_dve(dve, 0, NORM_MIXP, yb, "mix_post", 1, "x_pre")
            for j in range(8):
                u = Unit(U_KV + j)
                if j < 4:
                    dve.wait_ge(unit_done, u.n + 1)
                    for m in range(2):
                        dve.tensor_tensor(kx[:, 2 * j + m, :], bank[:, 2 * u.slot + m, 0:MEM], rmem[:, :], ALU.mult).then_inc(kx_done, 1)
                split_lo(dve, Unit(u.n0 + 3))
            inv_rows(dve, NORM_X)
            dve.wait_ge(r_ready, NORM_X + 1)
            for j in range(4):
                u = Unit(U_QX + j)
                dve.wait_ge(unit_done, u.n + 1)
                for m in range(2):
                    dve.scalar_tensor_tensor(out=qx[:, 2 * j + m, :], in0=bank[:, 2 * u.slot + m, :], scalar=256 ** -0.5,
                                             in1=rbc[:, :], op0=ALU.mult, op1=ALU.mult).then_inc(qx_done, 1)
                split_lo(dve, Unit(u.n0 + 3))

            def maxima(j):
                dve.wait_ge(j_s, X_1 + j + 1)
                dve.tensor_reduce(xsm(j, 0), bank[:, j % 2, :].rearrange("p (e c) -> p e c", e=2), AX, ALU.max).then_inc(j_max, 1)
                dve.wait_ge(j_max, X_1 + j + 1)
                dve.tensor_scalar(xsm(j, 2), xsm(j, 0), -1.0, None, ALU.mult).then_inc(j_neg, 1)

            def combine(j):
                dve.wait_ge(j_exp, X_2 + 2 * (j + 1))
                dve.reciprocal(xsm(j, 6), xsm(j, 4)).then_inc(j_rec, 1)
                dve.wait_ge(j_rec, X_REC + j + 1)
                dve.wait_ge(j_pv, X_1 + j + 1)
                if j >= 2:
                    dve.wait_ge(x_back, j - 1)
                dve.tensor_tensor(xo[:, j % 2, :].rearrange("p (e d) -> p e d", e=2), bank[:, 4 + j % 2, :].rearrange("p (e d) -> p e d", e=2),
                                  xsm(j, 6).unsqueeze(2).to_broadcast([P, 2, MEM]), ALU.mult).then_inc(j_o, 1)

            def split_back(j):
                i, hp = j // 2, j % 2
                dst = (slice(None), slice(4 * hp, 4 * hp + 4), slice(i * P, (i + 1) * P))
                dve.wait_ge(ox_hi, j + 1)
                dve.tensor_tensor(x_lo[dst], bank[:, 6 + j % 2, :].rearrange("p (c t) -> p c t", c=4), x_hi[dst],
                                  ALU.subtract).then_inc(ox_lo, 1)

            for t in range(XJOBS + 3):
                if t < XJOBS:
                    maxima(t)
                if 0 <= t - 2 < XJOBS:
                    combine(t - 2)
                if t >= 3:
                    split_back(t - 3)
            for j in range(4):
                split_lo(dve, Unit(U_OX + j + 3))
            post_norm_dve(dve, 1, NORM_XP, yb, "x_post", 2, "ffn_pre")
            inv_rows(dve, NORM_F)
            ffn_up_dve(dve, U_GU, NORM_F, 0, None)
            for j in range(9):
                split_lo(dve, Unit(U_DN + j + 3))
            post_norm_dve(dve, 2, NORM_FP, y_ffn, "ffn_post", None, None)

        tab2_in, pad_ready = sem("tab2_in"), sem("pad_ready")
        l_u, l_ugs, l_sig, l_a, l_tap, l_q, l_v = (sem("l_" + n) for n in ("u", "ug_scaled", "sigmoid", "a", "tap", "q", "v"))
        q_sq, q_ss, q_std, q_inv, q_n, q_rot, q_cos, q_sin, q_rope, l_kx = (sem("l_" + n) for n in (
            "q_sq", "q_ss", "q_std", "q_inv", "q_n", "q_rot", "q_cos", "q_sin", "q_rope", "kx"))
        l_gs, l_g = sem("l_gates_scaled"), sem("l_gates")
        ln_sum, ln_mu, ln_c, ln_sq, ln_ss, ln_std, ln_inv, ln_n, ln_y, ln_hi, ln_lo = (sem("ln_" + n) for n in (
            "sum", "mu", "centred", "squares", "ss", "std", "inv", "normed", "silu", "hi", "lo"))
        co_done, co_ready, mg_sum, mg_hi, mg_lo = (sem("l_" + n) for n in ("co_done", "co_ready", "mg_sum", "mg_hi", "mg_lo"))
        A = {n: sem("a_" + n) for n in ("scores", "max", "neg", "sinkd", "exp", "sinke", "den", "rec", "turned", "turned_copied",
                                        "pv", "out", "back", "gated")}
        LJ = QB * 8
        UNIT_TAPS = {4: 9, 5: 9, 6: 9, 7: 9, 8: 9, 9: 12, 10: 12, 11: 12, 12: 12, 13: 12, 14: 12, 15: 7}
        assert sum(UNIT_TAPS.values()) == 4 * TAPS
        ROPE_UNITS = range(6, 11)
        AT_CENTRE, AT_SQ, AT_SS, AT_STD, AT_NORM, AT_SILU, AT_LO, AT_CO = 1, 2, 3, 4, 5, 7, 8, 11

        def pairs(p):
            return [t for t in (2 * p, 2 * p + 1) if t < 9]

        def asm(j, a_, e=None):
            c = 16 * (j % 4) + a_
            return small[:, c:c + 2] if e is None else small[:, c + e:c + e + 1]

        def layer_pe(pe, L):
            base = U_L
            norm, pre = L * 2 + NORM_L, L * 2 + 3

            def head_squares(t):
                pe.wait_ge(q_sq, L * 9 + t + 1)
                if t < 2:
                    pe.wait_ge(std_ready, norm + 1)
                    pe.wait_ge(rcol_std, L + 3)
                else:
                    pe.wait_ge(q_rope, L * 9 + t - 1)
                pe.wait_ge(tab2_in, L * 16 + 16)
                pe.matmul(bank[:, STAT + t % 2, :], heads2, lsq[:, t % 2, :], start=True, stop=True).then_inc(q_ss, 1)

            def rotate(t):
                pe.wait_ge(q_n, L * 9 + t + 1)
                pe.matmul(bank[:, STAT + t % 2, :], perm2, lq[:, t, :], start=True, stop=True).then_inc(q_rot, 1)

            linear_wide(pe, [Unit(base + s, L) for s in range(3)], lambda k: pe.wait_ge(pre_lo, pre * 8 + k + 1))
            pe.wait_ge(std_ready, norm)
            stat_columns(pe, norm, QB)
            stat_rows(pe, norm)
            for n in range(3, V_CO):
                u = Unit(base + n, L)
                pe.wait_ge(lo_ready, u.n + 1)
                mm = linear_tile(pe, u, 0)
                if n in ROPE_UNITS:
                    for t in pairs(n - ROPE_UNITS[0]):
                        head_squares(t)
                if n == V_KV:
                    mm = tokens_major(pe, u, x_hi, x_lo, QB, P, P, lambda b_: (2 * u.slot + 1, b_ * P))
                else:
                    mm = linear_tile(pe, u, 1)
                mm.then_inc(unit_done, 1)
                if n in ROPE_UNITS:
                    for t in pairs(n - ROPE_UNITS[0]):
                        rotate(t)

            def scores(j):
                i, tile, g = j // 8, j % 8, j % 8 // 4
                if j == 0:
                    pe.wait_ge(q_rope, L * 9 + 9)
                    pe.wait_ge(l_kx, L * 2 + 2)
                    pe.wait_ge(l_g, L * 16 + 16)
                if j >= 2:
                    pe.wait_ge(A["exp"], L * 2 * LJ + 2 * (j - 1))
                c0, k0 = (P, 0) if i == 0 else (0, (i - 1) * P)
                for e in range(2):
                    dst = bank[:, 2 * (j % 2) + e, c0:2 * P]
                    keys = key_rows(lq[:, 8, :], lkx[:, :], e, g)[:, k0:(i + 1) * P]
                    pe.matmul(dst, lq[HD * e:HD * e + HD, tile, i * P:(i + 1) * P], keys, start=True, stop=False)
                    mm = pe.matmul(dst, ident_b[:, :], mask_b[:, c0:2 * P], start=False, stop=True)
                mm.then_inc(A["scores"], 1)

            def turn(j):
                first = 1 if j // 8 == 0 else 0
                pe.wait_ge(A["exp"], L * 2 * LJ + 2 * (j + 1))
                if j:
                    pe.wait_ge(A["turned_copied"], L * LJ + j)
                for e in range(2):
                    for c in range(first, 2):
                        mm = pe.transpose(bank[:, 4, (2 * e + c) * P:(2 * e + c + 1) * P], lprob[:, j % 2, e, c * P:(c + 1) * P], ident[:, :])
                mm.then_inc(A["turned"], 1)

            def values(j):
                i, g = j // 8, j % 8 // 4
                first = 1 if i == 0 else 0
                pe.wait_ge(A["turned_copied"], L * LJ + j + 1)
                if j:
                    pe.wait_ge(A["out"], L * LJ + j)
                for e in range(2):
                    for c in range(first, 2):
                        mm = pe.matmul(bank[:, 6, e * HD:(e + 1) * HD], lprobT[:, j % 2, 2 * e + c, :],
                                       lv[:, i - 1 + c, g * HD:(g + 1) * HD], start=(c == first), stop=(c == 1))
                mm.then_inc(A["pv"], 1)

            def back(j):
                pe.wait_ge(A["out"], L * LJ + j + 1)
                if j:
                    pe.wait_ge(A["gated"], L * LJ + j)
                pe.transpose(bank[:, 7, 0:P], lo_s[:, j % 2, :], ident[:, :]).then_inc(A["back"], 1)

            def conv_project(k):
                u = Unit(base + V_CO + k // 4, L)
                if k % 4 == 0:
                    pe.wait_ge(lo_ready, u.n + 1)
                if k == 0:
                    pe.wait_ge(ln_lo, L * 4 + 4)
                    pe.wait_ge(ln_std, L + 1)
                else:
                    pe.wait_ge(co_ready, L * 8 + k)
                wh = w_hi[:, u.slot, :].rearrange("p (k c) -> p k c", k=4)[:, :, (k % 4) * P:(k % 4 + 1) * P]
                wl = w_lo[:, u.slot, :].rearrange("p (k c) -> p k c", k=4)[:, :, (k % 4) * P:(k % 4 + 1) * P]
                for c in range(4):
                    pe.matmul(bank[:, 5, :], wh[:, c, :], x_hi[:, c, :], start=(c == 0), stop=False)
                    pe.matmul(bank[:, 5, :], wh[:, c, :], x_lo[:, c, :], start=False, stop=False)
                    mm = pe.matmul(bank[:, 5, :], wl[:, c, :], x_hi[:, c, :], start=False, stop=(c == 3))
                mm.then_inc(unit_done if k % 4 == 3 else co_done, 1)

            for t in range(LJ + 3):
                if t < LJ:
                    scores(t)
                if 0 <= t - 1 < LJ:
                    turn(t - 1)
                if 0 <= t - 2 < LJ:
                    values(t - 2)
                if t >= 3:
                    back(t - 3)
                if t == 0:
                    pe.wait_ge(l_tap, L * 4 * TAPS + 4 * TAPS)
                    for m in range(4):
                        mm = pe.matmul(bank[:, 5, :], ones[:, :], cy[:, m, :], start=(m == 0), stop=(m == 3))
                    mm.then_inc(ln_sum, 1)
                if t == AT_SS:
                    for m in range(4):
                        if m == 0:
                            pe.wait_ge(ln_mu, L + 1)
                        pe.wait_ge(ln_sq, L * 4 + m + 1)
                        mm = pe.matmul(bank[:, 5, :], ones[:, :], sgb_free(m), start=(m == 0), stop=(m == 3))
                    mm.then_inc(ln_ss, 1)
                if AT_CO <= t < AT_CO + 8:
                    conv_project(t - AT_CO)

            def merged(k):
                pe.wait_ge(mg_lo, L * 8 + k + 1)
            linear_wide(pe, [Unit(base + V_OUT + s, L) for s in range(3)], merged)
            linear(pe, Unit(base + V_OUT + 3, L))
            ffn_pe(pe, base + V_GU, L * 2 + 4, norm + 1, L + 1, L)

        def sgb_free(m):
            return la[:, m, PAD:PAD + T]

        def layer_act(act, L):
            base = U_L
            norm, pre = L * 2 + NORM_L, L * 2 + 3
            act.wait_ge(h_ready, L * 16 + 24)
            act.dma_start(tab2[:, :], rope2).then_inc(tab2_in, 16)
            for k in range(DT):
                if k < 3:
                    split_hi(act, Unit(base + k, L))
                pre_norm_hi(act, pre, norm, k, "norm_mix", L)
            act.wait_ge(r_ready, norm)
            std_rows(act, norm)
            std_columns(act, L + 2, QB)

            def roots(p):
                for t in pairs(p):
                    act.wait_ge(q_ss, L * 9 + t + 1)
                    if t < 2:
                        act.wait_ge(l_u, L * 4 + 4)
                    else:
                        act.wait_ge(q_n, L * 9 + t - 1)
                    act.activation(lrq[:, t % 2, :], bank[:, STAT + t % 2, :], ACT.Sqrt, bias=eps_c[:, 1:2] if t < 8 else eps_c[:, 0:1],
                                   scale=1.0 if t < 8 else 1.0 / HD).then_inc(q_std, 1)

            for n in range(V_CO):
                u = Unit(base + n, L)
                if V_UG <= n < V_Q:
                    for m in range(2):
                        k, src = 2 * (n - V_UG) + m, bank[:, 2 * u.slot + m, :]
                        act.wait_ge(l_ugs, L * 4 + k + 1)
                        act.activation(src, src, ACT.Sigmoid).then_inc(l_sig, 1)
                if n == V_KV:
                    act.wait_ge(unit_done, u.n + 1)
                    act.wait_ge(rcol_ready, L + 3)
                    for b_ in range(QB):
                        act.activation(lv[:, b_, :], bank[:, 2 * u.slot + 1, b_ * P:(b_ + 1) * P], ACT.Copy,
                                       scale=rcol[:, b_:b_ + 1]).then_inc(l_v, 1)
                if n >= V_GA:
                    for m in range(2):
                        k, src = 2 * (n - V_GA) + m, bank[:, 2 * u.slot + m, :]
                        act.wait_ge(l_gs, L * 16 + k + 1)
                        act.activation((sga if k < 8 else sgb)[:, k % 8, :], src, ACT.Sigmoid).then_inc(l_g, 1)
                split_hi(act, Unit(base + n + 3, L))
                if n + 1 in ROPE_UNITS:
                    roots(n + 1 - ROPE_UNITS[0])
                if V_Q <= n <= V_KV:
                    for t in pairs(n - V_Q):
                        act.wait_ge(l_q, L * 9 + t + 1)
                        if t >= 2:
                            act.wait_ge(q_ss, L * 9 + t - 1)
                        act.activation(lsq[:, t % 2, :], lq[:, t, :], ACT.Square).then_inc(q_sq, 1)
                if n == 12:
                    act.wait_ge(q_rope, L * 9 + 9)
                    act.activation(lkx[0:HD, :], lq[HD:P, 8, :], ACT.Copy).then_inc(l_kx, 1)
                    act.activation(lkx[HD:P, :], lq[0:HD, 8, :], ACT.Copy).then_inc(l_kx, 1)

            def exps(j):
                c0 = P if j // 8 == 0 else 0
                act.wait_ge(A["neg"], L * LJ + j + 1)
                if j >= 2:
                    act.wait_ge(A["turned"], L * LJ + j - 1)
                for e in range(2):
                    act.activation(lprob[:, j % 2, e, c0:2 * P], bank[:, 2 * (j % 2) + e, c0:2 * P], ACT.Exp, bias=asm(j, 2, e),
                                   accum_out=asm(j, 4, e)).then_inc(A["exp"], 1)
                act.wait_ge(A["sinkd"], L * LJ + j + 1)
                act.activation(asm(j, 8), asm(j, 6), ACT.Exp).then_inc(A["sinke"], 1)

            def copy_turned(j):
                act.wait_ge(A["turned"], L * LJ + j + 1)
                if j >= 2:
                    act.wait_ge(A["pv"], L * LJ + j - 1)
                first = 1 if j // 8 == 0 else 0
                act.activation(lprobT[:, j % 2, :, :].rearrange("p (e c) t -> p e c t", e=2)[:, :, first:, :],
                               bank[:, 4, :].rearrange("p (e c t) -> p e c t", e=2, c=2)[:, :, first:, :], ACT.Copy)\
                   .then_inc(A["turned_copied"], 1)

            for t in range(LJ + 1):
                if t < LJ:
                    exps(t)
                if t >= 1:
                    copy_turned(t - 1)
                if t == AT_SQ:
                    for m in range(4):
                        act.wait_ge(ln_c, L * 4 + m + 1)
                        act.activation(sgb_free(m), cy[:, m, :], ACT.Square).then_inc(ln_sq, 1)
                if t == AT_STD:
                    act.wait_ge(ln_ss, L + 1)
                    act.activation(acc[:, :], bank[:, 5, :], ACT.Sqrt, bias=eps_c[:, 0:1], scale=1.0 / 512).then_inc(ln_std, 1)
                if t == AT_SILU:
                    act.wait_ge(unit_done, L * V_N + base + V_CO)
                    for m in range(4):
                        act.wait_ge(ln_n, L * 4 + m + 1)
                        act.activation(cy[:, m, :], cy[:, m, :], ACT.Silu, bias=col("ln_b", m, L), scale=col("ln_g", m, L)).then_inc(ln_y, 1)
                    for m in range(4):
                        act.wait_ge(ln_y, L * 4 + m + 1)
                        act.activation(x_hi[:, m, :], cy[:, m, :], ACT.Copy).then_inc(ln_hi, 1)
                if t == AT_CO + 5:
                    split_hi(act, Unit(base + V_CO + 3, L))
                if t == AT_CO + 9:
                    split_hi(act, Unit(base + V_CO + 4, L))

            act.wait_ge(unit_done, L * V_N + base + V_CO + 2)
            for k in range(DT):
                act.wait_ge(mg_sum, L * 8 + k + 1)
                act.activation(x_hi[:, k, :], sgb[:, k, :], ACT.Copy).then_inc(mg_hi, 1)
            for j in range(4):
                split_hi(act, Unit(base + V_OUT + j + 3, L))
            for k in range(DT):
                act.wait_ge(h_ready, L * 16 + 24 + k + 1)
                pre_norm_hi(act, pre + 1, norm + 1, k, "norm_ffn", L)
            act.wait_ge(r_ready, norm + 1)
            std_rows(act, norm + 1)
            ffn_up_act(act, base + V_GU, L + 1, L)
            for j in range(9):
                split_hi(act, Unit(base + V_DN + j + 3, L))

        def layer_dve(dve, L):
            base = U_L
            norm, pre = L * 2 + NORM_L, L * 2 + 3
            for k in range(DT):
                if k < 3:
                    split_lo(dve, Unit(base + k, L))
                pre_norm_lo(dve, pre, k, "norm_mix", L)
            inv_rows(dve, norm)
            dve.wait_ge(r_ready, norm + 1)
            inv_columns(dve, L + 2, QB)
            done = [0]

            def taps(count):
                for s in range(done[0], done[0] + count):
                    tap, m = s // 4, s % 4
                    src, wt = la[:, m, tap:tap + T], col("taps", m * TAPS + tap, L)
                    if tap == 0:
                        dve.wait_ge(l_a, L * 4 + m + 1)
                        dve.wait_ge(pad_ready, L + 1)
                        dve.tensor_scalar(cy[:, m, :], src, wt, col("conv_b", m, L), ALU.mult, ALU.add).then_inc(l_tap, 1)
                    else:
                        dve.wait_ge(l_tap, L * 4 * TAPS + s - 3)
                        dve.scalar_tensor_tensor(out=cy[:, m, :], in0=src, scalar=wt, in1=cy[:, m, :],
                                                 op0=ALU.mult, op1=ALU.add).then_inc(l_tap, 1)
                done[0] += count

            def normed(p):
                for t in pairs(p):
                    rq = lrq[:, t % 2, :]
                    dve.wait_ge(q_std, L * 9 + t + 1)
                    dve.reciprocal(rq, rq).then_inc(q_inv, 1)
                    dve.wait_ge(q_inv, L * 9 + t + 1)
                    dve.scalar_tensor_tensor(out=lq[:, t, :], in0=lq[:, t, :], scalar=col("q_norm" if t < 8 else "k_norm", 0, L),
                                             in1=rq, op0=ALU.mult, op1=ALU.mult).then_inc(q_n, 1)

            def roped(p):
                for t in pairs(p):
                    rot = bank[:, STAT + t % 2, :]
                    dve.wait_ge(q_rot, L * 9 + t + 1)
                    dve.tensor_tensor(rot, rot, sin2, ALU.mult).then_inc(q_sin, 1)
                    dve.wait_ge(q_sin, L * 9 + t + 1)
                    dve.wait_ge(q_cos, L * 9 + t + 1)
                    dve.tensor_tensor(lq[:, t, :], lcos[:, t % 2, :], rot, ALU.add).then_inc(q_rope, 1)

            for n in range(V_CO):
                u = Unit(base + n, L)
                dve.wait_ge(unit_done, u.n + 1)
                for m in range(2):
                    src = bank[:, 2 * u.slot + m, :]
                    if n < V_UG:
                        dve.tensor_tensor(la[:, 2 * n + m, PAD:PAD + T], src, rbc[:, :], ALU.mult).then_inc(l_u, 1)
                    elif n < V_Q:
                        dve.tensor_tensor(src, src, rbc[:, :], ALU.mult).then_inc(l_ugs, 1)
                    elif n <= V_KV:
                        if n < V_KV or m == 0:
                            dve.tensor_tensor(lq[:, 2 * (n - V_Q) + m, :], src, rbc[:, :], ALU.mult).then_inc(l_q, 1)
                    else:
                        dve.tensor_tensor(src, src, rbc[:, :], ALU.mult).then_inc(l_gs, 1)
                if V_UG <= n < V_Q:
                    for m in range(2):
                        k = 2 * (n - V_UG) + m
                        dst = la[:, k, PAD:PAD + T]
                        dve.wait_ge(l_sig, L * 4 + k + 1)
                        dve.wait_ge(l_u, L * 4 + k + 1)
                        dve.tensor_tensor(dst, dst, bank[:, 2 * u.slot + m, :], ALU.mult).then_inc(l_a, 1)
                split_lo(dve, Unit(base + n + 3, L))
                if n in ROPE_UNITS:
                    roped(n - ROPE_UNITS[0])
                taps(UNIT_TAPS.get(n, 0))
                if n + 1 in ROPE_UNITS:
                    normed(n + 1 - ROPE_UNITS[0])

            def maxima(j):
                c0 = P if j // 8 == 0 else 0
                tile = j % 8
                dve.wait_ge(A["scores"], L * LJ + j + 1)
                dve.tensor_reduce(asm(j, 0), bank[:, 2 * (j % 2):2 * (j % 2) + 2, c0:2 * P], AX, ALU.max).then_inc(A["max"], 1)
                dve.wait_ge(A["max"], L * LJ + j + 1)
                sink = gains[:, bass.ds(L * LAYER_W + (_cols["sinks"][0] + 2 * tile), 2)]
                nsink = neg_sink[:, bass.ds(L, 1), 2 * tile:2 * tile + 2].rearrange("p o c -> p (o c)")
                dve.scalar_tensor_tensor(out=asm(j, 2), in0=asm(j, 0), scalar=-1.0, in1=nsink, op0=ALU.mult, op1=ALU.min).then_inc(A["neg"], 1)
                dve.wait_ge(A["neg"], L * LJ + j + 1)
                dve.tensor_tensor(asm(j, 6), asm(j, 2), sink, ALU.add).then_inc(A["sinkd"], 1)

            def combine(j):
                dve.wait_ge(A["exp"], L * 2 * LJ + 2 * (j + 1))
                dve.wait_ge(A["sinke"], L * LJ + j + 1)
                dve.tensor_tensor(asm(j, 10), asm(j, 4), asm(j, 8), ALU.add).then_inc(A["den"], 1)
                dve.wait_ge(A["den"], L * LJ + j + 1)
                dve.reciprocal(asm(j, 12), asm(j, 10)).then_inc(A["rec"], 1)
                dve.wait_ge(A["rec"], L * LJ + j + 1)
                dve.wait_ge(A["pv"], L * LJ + j + 1)
                if j >= 2:
                    dve.wait_ge(A["back"], L * LJ + j - 1)
                dve.tensor_tensor(lo_s[:, j % 2, :].rearrange("p (e d) -> p e d", e=2), bank[:, 6, 0:P].rearrange("p (e d) -> p e d", e=2),
                                  asm(j, 12).unsqueeze(2).to_broadcast([P, 2, HD]), ALU.mult).then_inc(A["out"], 1)

            def gated(j):
                i, tile = j // 8, j % 8
                dst = sga[:, tile, i * P:(i + 1) * P]
                dve.wait_ge(A["back"], L * LJ + j + 1)
                if j == 0:
                    dve.wait_ge(l_g, L * 16 + 16)
                dve.tensor_tensor(dst, dst, bank[:, 7, 0:P], ALU.mult).then_inc(A["gated"], 1)

            for t in range(LJ + 3):
                if t < LJ:
                    maxima(t)
                if 0 <= t - 2 < LJ:
                    combine(t - 2)
                if t >= 3:
                    gated(t - 3)
                if t == AT_CENTRE:
                    dve.wait_ge(ln_sum, L + 1)
                    dve.tensor_scalar(rbc[:, :], bank[:, 5, :], 1.0 / 512, None, ALU.mult).then_inc(ln_mu, 1)
                    dve.wait_ge(ln_mu, L + 1)
                    for m in range(4):
                        dve.tensor_tensor(cy[:, m, :], cy[:, m, :], rbc[:, :], ALU.subtract).then_inc(ln_c, 1)
                if t == AT_NORM:
                    dve.wait_ge(ln_std, L + 1)
                    dve.reciprocal(acc[:, :], acc[:, :]).then_inc(ln_inv, 1)
                    dve.wait_ge(ln_inv, L + 1)
                    for m in range(4):
                        dve.tensor_tensor(cy[:, m, :], cy[:, m, :], acc[:, :], ALU.mult).then_inc(ln_n, 1)
                if t == AT_LO:
                    for m in range(4):
                        dve.wait_ge(ln_hi, L * 4 + m + 1)
                        dve.tensor_tensor(x_lo[:, m, :], cy[:, m, :], x_hi[:, m, :], ALU.subtract).then_inc(ln_lo, 1)
                if AT_CO <= t < AT_CO + 8:
                    k = t - AT_CO
                    if k % 4 == 3:
                        dve.wait_ge(unit_done, L * V_N + base + V_CO + k // 4 + 1)
                    else:
                        dve.wait_ge(co_done, L * 6 + k - k // 4 + 1)
                    dve.tensor_tensor(sgb[:, k, :], sgb[:, k, :], bank[:, 5, :], ALU.mult).then_inc(co_ready, 1)
                if t == AT_CO + 6:
                    split_lo(dve, Unit(base + V_CO + 3, L))
                if t == AT_CO + 10:
                    split_lo(dve, Unit(base + V_CO + 4, L))

            for k in range(DT):
                dve.wait_ge(mg_hi, L * 8 + k + 1)
                dve.tensor_tensor(x_lo[:, k, :], sgb[:, k, :], x_hi[:, k, :], ALU.subtract).then_inc(mg_lo, 1)

            def residual(k, src):
                dve.tensor_tensor(h[:, k, :], h[:, k, :], src, ALU.add).then_inc(h_ready, 1)

            for j in range(4):
                u = Unit(base + V_OUT + j, L)
                dve.wait_ge(unit_done, u.n + 1)
                for m in range(2):
                    residual(2 * j + m, bank[:, 2 * u.slot + m, :])
                split_lo(dve, Unit(u.n0 + 3, L))
            for k in range(DT):
                pre_norm_lo(dve, pre + 1, k, "norm_ffn", L)
            inv_rows(dve, norm + 1)
            ffn_up_dve(dve, base + V_GU, norm + 1, L + 1, L)
            for g in range(4):
                for part in range(3):
                    u = Unit(base + V_DN + 3 * g + part, L)
                    if part == 2:
                        dve.wait_ge(unit_done, u.n + 1)
                        for m in range(2):
                            residual(2 * g + m, bank[:, 2 * (g % 2) + m, :])
                    if g < 3:
                        split_lo(dve, Unit(u.n0 + 3, L))

        @block.tensor
        def _(pe):
            mixer1_pe(pe)
            cross_pe(pe)
            with pe.Fori(0, LAYERS) as L:
                layer_pe(pe, L)

        @block.scalar
        def _(act):
            mixer1_act(act)
            cross_act(act)
            with act.Fori(0, LAYERS) as L:
                layer_act(act, L)

        @block.vector
        def _(dve):
            mixer1_dve(dve)
            cross_dve(dve)
            dve.tensor_scalar(neg_sink[:, :, :].rearrange("p l c -> p (l c)").rearrange("p (l c) -> p l c", l=LAYERS),
                              gains[:, LAYER_BASE:].rearrange("p (l c) -> p l c", l=LAYERS)[:, :, _cols["sinks"][0] - LAYER_BASE:
                                                                                          _cols["sinks"][0] - LAYER_BASE + 16],
                              -1.0, None, ALU.mult).then_inc(neg_sink_ready, 1)
            dve.wait_ge(neg_sink_ready, 1)
            with dve.Fori(0, LAYERS) as L:
                layer_dve(dve, L)

        @block.gpsimd
        def _(pool):
            pool.memset(ones[:, :], 1.0).then_inc(const_ready, 1)
            pool.memset(eps_c[:, 0:1], EPS)
            pool.memset(eps_c[:, 1:2], HD * EPS)
            pool.memset(eps_c[:, 2:3], float(np.pi / 2)).then_inc(const_ready, 1)
            pool.memset(kcm[:, :, :], 0.0)
            pool.memset(vblk[:, :], 0.0).then_inc(vblk_zero, 1)
            sum_squares(pool, NORM_MIX)
            for r in range(6):
                rope_pool(pool, r)
            sum_squares(pool, NORM_MEM, MEM)
            for n in range(NORM_MIXP, NORM_L):
                sum_squares(pool, n)
            ones_pad = ones[:, 0:PAD].unsqueeze(1).to_broadcast([P, 4, PAD])
            with pool.Fori(0, LAYERS) as L:
                pool.wait_ge(h_ready, L * 16 + 24)
                pool.tensor_tensor(la[:, :, 0:PAD], ones_pad, ones_pad, ALU.subtract).then_inc(pad_ready, 1)
                sum_squares(pool, L * 2 + NORM_L)
                pool.wait_ge(tab2_in, L * 16 + 16)
                for t in range(9):
                    pool.wait_ge(q_n, L * 9 + t + 1)
                    if t >= 2:
                        pool.wait_ge(q_rope, L * 9 + t - 1)
                    pool.tensor_tensor(lcos[:, t % 2, :], lq[:, t, :], cos2, ALU.mult).then_inc(q_cos, 1)
                for k in range(DT):
                    pool.wait_ge(A["gated"], L * LJ + 3 * 8 + k + 1)
                    pool.wait_ge(co_ready, L * 8 + k + 1)
                    pool.tensor_tensor(sgb[:, k, :], sgb[:, k, :], sga[:, k, :], ALU.add).then_inc(mg_sum, 1)
                sum_squares(pool, L * 2 + NORM_L + 1)


def unit_pack(weight, cols, rows=8):
    k = weight.shape[0] // P
    part = weight[:, cols].reshape(k, P, len(cols)).transpose(1, 0, 2)
    out = []
    for c in range(0, k, rows):
        u = np.zeros((P, rows, UNIT // rows), np.float32)
        m = min(rows, k - c)
        u[:, :m, :len(cols)] = part[:, c:c + m]
        out.append(u.reshape(P, UNIT))
    return out


def spans(weight, lo, hi, rows=8, order=None):
    step = UNIT // rows
    cols = np.arange(lo, hi) if order is None else np.asarray(order)
    return [u for c in range(0, len(cols), step) for u in unit_pack(weight, cols[c:c + step], rows)]


def ffn_units(gate_up, down):
    out = []
    for j in range(FT):
        out += unit_pack(gate_up, np.r_[j * P:(j + 1) * P, FF + j * P:FF + (j + 1) * P])
    return out + spans(down, 0, D)


def tiles(v):
    v = np.asarray(v)
    return v.reshape(-1, P).T


def feature_major(a):
    return np.ascontiguousarray(a.T.reshape(-1, P, a.shape[0]).transpose(1, 0, 2).reshape(P, -1))


def rotation(half, width):
    m = np.zeros((P, P), np.float32)
    for head in range(0, P, HD):
        for i in range(half):
            m[head + half + i, head + i] = -1.0
            m[head + i, head + half + i] = 1.0
    return m


def kernel(**inputs):
    import concourse.bacc as bacc
    from concourse.bass_utils import run_bass_kernel_spmd

    g = {k: np.asarray(v) for k, v in inputs.items()}
    win = g["w_in"]
    c = 3 * 512
    kvb = c + 512
    stream = spans(win, 0, kvb) + spans(win, kvb, kvb + 256)
    stream += spans(win, 0, 0, order=np.r_[kvb + 256:kvb + 384, kvb + 512:kvb + 640])
    stream += spans(win, 0, 0, order=np.r_[kvb + 384:kvb + 512, kvb + 640:kvb + 768])
    stream += spans(g["w1_kc"], 0, 256) + spans(g["w1_vc"], 0, 256)
    stream += spans(g["w_out"], 0, D) + spans(g["w_kv_x"], 0, 2 * D) + spans(g["w_q_x"], 0, D) + spans(g["w_o_x"], 0, D)
    stream += ffn_units(g["w_gate_up"], g["w_down"])
    for l in range(LAYERS):
        wl = g["w_in_2"][l]
        q, kv, u, ug, ga = 0, 1024, 1280, 1792, 2304
        stream += spans(wl, u, u + 512) + spans(wl, ug, ug + 512) + spans(wl, q, q + 1024) + spans(wl, kv, kv + 256)
        stream += spans(wl, ga, ga + 2048) + spans(g["w_conv_out_2"][l], 0, D, rows=4) + spans(g["w_out_2"][l], 0, D)
        stream += ffn_units(g["w_gate_up_2"][l], g["w_down_2"][l])
    assert len(stream) == UNITS, len(stream)
    w = np.stack(stream)

    def pe_pairs(pe):
        return pe.reshape(16, 2, HD).transpose(1, 2, 0).reshape(P, 16)

    inv = (np.float32(10000.0) ** (-np.arange(32, dtype=np.float32) / np.float32(32))).astype(np.float32)
    cols = [tiles(g["norm_mix_pre"]), tiles(g["norm_mix_post"]), tiles(g["norm_x_pre"]), tiles(g["norm_mem"]),
            tiles(g["norm_x_post"]), tiles(g["norm_ffn_pre"]), tiles(g["norm_ffn_post"]), tiles(g["norm_conv_out"]),
            tiles(g["norm_attn_out"]), g["conv_w"].reshape(3, 4, P).transpose(2, 1, 0).reshape(P, 12),
            np.tile(inv, 4)[:, None], pe_pairs(g["pe_kc"]), pe_pairs(g["pe_vc"])]
    for l in range(LAYERS):
        cols += [tiles(g["norm_mix_2"][l]), tiles(g["norm_ffn_2"][l]), np.tile(g["q_norm_2"][l], 2)[:, None],
                 np.tile(g["k_norm_2"][l], 2)[:, None], np.broadcast_to(g["sinks_2"][l], (P, 16)),
                 g["conv_w_2"][l].reshape(TAPS, 4, P).transpose(2, 1, 0).reshape(P, 4 * TAPS), tiles(g["conv_b_2"][l]),
                 tiles(g["conv_ln_g_2"][l]), tiles(g["conv_ln_b_2"][l])]
    pack = np.ascontiguousarray(np.concatenate(cols, axis=1).astype(np.float32))
    assert pack.shape == (P, PACK_W)

    r, s = np.arange(P)[:, None], np.arange(P)[None, :]
    masks = [np.where(s > r, 0, NEG), np.where(s <= r, 0, NEG)]
    for b in range(QB):
        j = np.arange(32)[None, :]
        seen = (j < NCMP) & (16 * j + 31 <= b * P + r)
        masks.append(np.tile(np.where(seen, 0, NEG), (1, 4)))
    cmask = np.ascontiguousarray(np.concatenate(masks, axis=1).astype(np.float32))
    tables = np.concatenate([np.eye(P, dtype=np.float32), rotation(32, HD)], axis=1)
    f2 = (np.float32(500000.0) ** (-np.arange(0, 16, 2, dtype=np.float32) / np.float32(16))).astype(np.float32)
    ang = (np.arange(T, dtype=np.float32)[None, :] * f2[:, None]).astype(np.float32).astype(np.float64)
    cos_h, sin_h = np.ones((HD, T)), np.zeros((HD, T))
    cos_h[0:8], cos_h[8:16], sin_h[0:8], sin_h[8:16] = np.cos(ang), np.cos(ang), np.sin(ang), np.sin(ang)
    heads = np.kron(np.eye(2), np.ones((HD, HD)))
    rope2 = np.concatenate([np.tile(cos_h, (2, 1)), np.tile(sin_h, (2, 1)), rotation(8, HD), heads], axis=1).astype(np.float32)

    w2 = np.stack([g["w2_kc"], g["w2_vc"]]).reshape(2, 2, P, HD).transpose(2, 0, 1, 3).reshape(P, -1)
    wg = win[:, kvb + 768:].reshape(8, P, 24).transpose(1, 0, 2).reshape(P, -1)
    arrays = {
        "w": w, "x": feature_major(g["x"][0]), "mem": feature_major(g["mem"][0]), "pos": g["positions"].astype(np.int32),
        "pack": pack, "tables": tables, "cmask": cmask, "w2": np.ascontiguousarray(w2), "wg": np.ascontiguousarray(wg),
        "rope2": np.ascontiguousarray(rope2),
    }
    nc = bacc.Bacc("TRN2", target_bir_lowering=False, num_devices=1, dynamic_dma_scratch_size=1024)
    aps = {n: nc.dram_tensor(n + "_d", a.shape, mybir.dt.from_np(a.dtype), kind="ExternalInput").ap() for n, a in arrays.items()}
    out = nc.dram_tensor("out_d", (P, DT * T), F32, kind="ExternalOutput").ap()
    build(nc, out=out.rearrange("p (k t) -> p k t", k=DT), **aps)
    res = run_bass_kernel_spmd(nc, [{n + "_d": a for n, a in arrays.items()}], core_ids=[0])
    y = res.results[0]["out_d"].reshape(P, DT, T).transpose(2, 1, 0).reshape(1, T, D)
    return np.ascontiguousarray(y)
```

```python
from contextlib import ExitStack

import concourse.bass as bass
from concourse import mybir
import numpy as np

F32 = mybir.dt.float32
F32R = mybir.dt.float32r
BF16 = mybir.dt.bfloat16
I32 = mybir.dt.int32
ALU = mybir.AluOpType
ACT = mybir.ActivationFunctionType
AX = mybir.AxisListType.X

P = 128
T = 512
D = 1024
DT = D // P
QB = T // P
MEM = 256
FF = 2816
FT = FF // P
HD = 64
EPS = 1e-6
LAYERS = 2
NCMP = (T - 32) // 16 + 1
WINDOWS = 2 * NCMP
TAPS = 31
PAD = TAPS - 1
NEG = -1e30
LOW = -1e20
SLOTS = 3
UNIT = 2048

U_IN, U_W1, U_OUT, U_KV, U_QX, U_OX, U_GU, U_DN, U_L = 0, 11, 15, 19, 27, 31, 35, 57, 69
V_U, V_UG, V_Q, V_KV, V_GA, V_CO, V_OUT, V_GU, V_DN, V_N = 0, 2, 4, 8, 9, 17, 19, 23, 45, 57
UNITS = U_L + LAYERS * V_N
assert U_L % SLOTS == 0 and V_N % SLOTS == 0

_cols = {}


def _column(name, n):
    _cols[name] = (sum(c for _, c in _cols.values()), n)


for _n, _c in [("mix_pre", 8), ("mix_post", 8), ("x_pre", 8), ("mem", 8), ("x_post", 8), ("ffn_pre", 8),
               ("ffn_post", 8), ("conv_out", 4), ("attn_out", 4), ("conv_w", 12), ("inv", 1), ("pe_k", 16), ("pe_v", 16)]:
    _column(_n, _c)
LAYER_COLS = [("norm_mix", 8), ("norm_ffn", 8), ("q_norm", 1), ("k_norm", 1), ("sinks", 16),
              ("taps", 4 * TAPS), ("conv_b", 4), ("ln_g", 4), ("ln_b", 4)]
LAYER_BASE = sum(c for _, c in _cols.values())
_at = LAYER_BASE
for _n, _c in LAYER_COLS:
    _cols[_n] = (_at, _c)
    _at += _c
LAYER_W = _at - LAYER_BASE
PACK_W = LAYER_BASE + LAYERS * LAYER_W

C1 = 6.28125
C2 = float(np.round((2 * np.pi - C1) * 2 ** 22) / 2 ** 22)
C3 = float(2 * np.pi - C1 - C2)
ROUNDER = float(1.5 * 2 ** 23)


class Unit:

    def __init__(self, n0, layer=None, turn=None):
        self.n0, self.slot, self.n, self.round = n0, n0 % SLOTS, n0, n0 // SLOTS
        self.first = n0 < SLOTS and turn is None
        if layer is not None:
            self.n = layer * V_N + self.n
            self.round = layer * (V_N // SLOTS) + self.round
        if turn is not None:
            self.n = turn * SLOTS + self.n
            self.round = turn + self.round


def build(nc, w, x, mem, pos, pack, tables, cmask, w2, wg, rope2, out):
    ctx = ExitStack()
    with ctx:
        def sem(name):
            return ctx.enter_context(nc.semaphore(name))

        where = [(nc.sbuf_base + 63) // 64 * 64]

        def place(name, shape, dt=F32, cursor=where):
            size = int(np.prod(shape[1:])) * (2 if dt == BF16 else 4)
            t = nc.alloc_sbuf_tensor_at(name, shape, dt, offset=cursor[0])
            cursor[0] += (size + 31) // 32 * 32
            assert cursor[0] <= nc.sbuf_usable_end, (name, cursor[0])
            return t

        w_raw = place("w_raw", [P, SLOTS, UNIT])
        w_hi = place("w_hi", [P, SLOTS, UNIT], F32R)
        w_lo = place("w_lo", [P, SLOTS, UNIT], F32R)
        h = place("h", [P, DT, T])
        act_at = [where[0]]
        y_ffn = place("y_ffn", [P, DT, T], F32, act_at)
        x_hi = place("x_hi", [P, DT, T], F32R)
        x_lo = place("x_lo", [P, DT, T], F32R)
        rbc = place("rbc", [P, T])
        acc = place("acc", [P, T])
        sq = place("sq", [P, 2, T])
        gains = place("gains", [P, PACK_W])
        ident = place("ident", [P, P])
        ones = place("ones", [P, P])
        ident_b = place("ident_b", [P, P], BF16)
        mask_b = place("mask_b", [P, 2 * P], BF16)
        eps_c = place("eps_c", [P, 3])
        rcol, rcol_mem = place("rcol", [P, QB]), place("rcol_mem", [P, 2])
        rcol_c, rcol_ln = place("rcol_c", [P, QB]), place("rcol_ln", [P, QB])
        rcol_head = place("rcol_head", [P, 9 * QB * 2])
        neg_sink = place("neg_sink", [P, LAYERS, 16])
        small = place("small", [P, 64])
        jcol = place("jcol", [P, 64])
        scope = where[0]

        a = [scope]
        f_hi = place("f_hi", [P, FT, T], F32R, a)
        f_lo = place("f_lo", [P, FT, T], F32R, a)
        silu = place("silu", [P, T], F32, a)

        a = [scope]
        bg = place("bg", [P, 4, T], F32, a)
        z = place("z", [P, 4, T], F32, a)
        cv = place("cv", [P, 4, T], F32, a)
        qT = place("qT", [P, 4, T], F32, a)
        kT = place("kT", [P, 2, T], F32, a)
        kTx = place("kTx", [P, 2, T], F32, a)
        b = [a[0]]
        e_c = place("e_c", [P, 2, 2 * P], F32, b)
        pt_c = place("pt_c", [P, 2, 2 * P], F32, b)
        kvc = place("kvc", [P, 2, T], F32, a)
        vtok = place("vtok", [P, QB, 2 * P], F32, a)
        cosT = place("cosT", [P, T], F32, a)
        sinT = place("sinT", [P, T], F32, a)
        ctmp = place("ctmp", [P, 2, T], F32, a)
        b = [a[0]]
        xf = place("xf", [P, 2, 16, WINDOWS], F32, b)
        o_all = place("o_all", [P, QB, T], F32, a)
        gate = place("gate", [P, QB, 24], F32, a)
        perm = place("perm", [P, P], F32, a)
        wg_s = place("wg_s", [P, 8 * 24], F32, a)
        wg_hi = place("wg_hi", [P, 8 * 24], F32R, a)
        wg_lo = place("wg_lo", [P, 8 * 24], F32R, a)
        w2_s = place("w2_s", [P, 2, 2, HD], F32, a)
        hc = place("hc", [P, 2, 2, WINDOWS], F32, a)
        hid = place("hid", [WINDOWS, 2, 2 * P], F32, a)
        kc2 = place("kc2", [HD, 2, NCMP], F32, a)
        kcm = place("kcm", [P, 2, 32], F32, a)
        vblk = place("vblk", [P, 4 * HD], F32, a)
        cmask_b = place("cmask_b", [P, QB, P], BF16, a)
        b = [a[0]]
        xc_hi = place("xc_hi", [P, 2, 16, WINDOWS], F32R, b)
        xc_lo = place("xc_lo", [P, 2, 16, WINDOWS], F32R, b)
        b = [a[0]]
        prob = place("prob", [P, 2, 2, T], F32, b)
        probT = place("probT", [P, 2, 2, T], F32, b)
        stage = nc.alloc_sbuf_tensor_at("stage", [P, 4 * P + QB * P], F32, offset=scope + 16 * 1024)
        pos_i = nc.alloc_sbuf_tensor_at("pos_i", [P, T], I32, offset=scope + 16 * 1024 + 4096)

        a = [scope]
        memT = place("memT", [P, DT, MEM], F32, a)
        m_hi = place("m_hi", [P, DT, MEM], F32R, a)
        m_lo = place("m_lo", [P, DT, MEM], F32R, a)
        kx = place("kx", [P, DT, MEM], F32, a)
        vx = place("vx", [P, 2, D], F32, a)
        qx = place("qx", [P, DT, T], F32, a)
        yb = place("yb", [P, DT, T], F32, a)
        xprob = place("xprob", [P, 2, 2, MEM], F32, a)
        xprobT = place("xprobT", [P, 2, 4, P], F32, a)
        xo = place("xo", [P, 2, T], F32, a)
        rmem = place("rmem", [P, MEM], F32, a)

        a = [scope]
        lq = place("lq", [P, 9, T], F32, a)
        lkx = place("lkx", [P, T], F32, a)
        lv = place("lv", [P, QB, P], F32, a)
        la = place("la", [P, 4, PAD + T], F32, a)
        cy = place("cy", [P, 4, T], F32, a)
        sga = place("sga", [P, DT, T], F32, a)
        sgb = place("sgb", [P, DT, T], F32, a)
        tab2 = place("tab2", [P, 2 * T + 2 * P], F32, a)
        cos2, sin2 = tab2[:, 0:T], tab2[:, T:2 * T]
        perm2, heads2 = tab2[:, 2 * T:2 * T + P], tab2[:, 2 * T + P:]
        lsm = place("lsm", [P, 2, 16], F32, a)
        b = [a[0]]
        lsq = place("lsq", [P, 2, T], F32, b)
        lcos = place("lcos", [P, 2, T], F32, b)
        lwide = place("lwide", [P, 2, QB * P], F32, b)
        b = [a[0]]
        lprob = place("lprob", [P, 2, 2, MEM], F32, b)
        lprobT = place("lprobT", [P, 2, 4, P], F32, b)
        lo_s = place("lo_s", [P, 2, P], F32, b)

        bank = ctx.enter_context(nc.psum_tensor("bank", [P, 8, T], F32))
        STAT, AUX = 6, 7

        def col(name, k=0, layer=None):
            c = _cols[name][0] + k
            if layer is None:
                return gains[:, c:c + 1]
            return gains[:, bass.ds(layer * LAYER_W + c, 1)]

        def ki(t, slot):
            return t[:, slot, :].rearrange("p (k c) -> p k c", k=8)

        raw_in = [sem(f"raw_in{s}") for s in range(SLOTS)]
        hi_ready, lo_ready, unit_done = sem("hi_ready"), sem("lo_ready"), sem("unit_done")
        x_in = [sem(f"x_in{k}") for k in range(4)]
        gains_in, pos_in, tab_in, out_done = (sem(n) for n in ("gains_in", "pos_in", "tab_in", "out_done"))
        const_ready, mask_ready, neg_sink_ready = sem("const_ready"), sem("mask_ready"), sem("neg_sink_ready")
        sq_ready, acc_ready, stat_done, std_ready, inv_ready, row_done, r_ready = (sem(n) for n in (
            "sq_ready", "acc_ready", "stat_done", "std_ready", "inv_ready", "row_done", "r_ready"))
        mem_hi, mem_lo = sem("mem_hi"), sem("mem_lo")
        pre_hi, pre_lo, h_ready, t_ready, y_ready = (sem(n) for n in (
            "pre_hi", "pre_lo", "h_ready", "t_ready", "y_ready"))
        NORM_MIX, NORM_MEM, NORM_MIXP, NORM_X, NORM_XP, NORM_F, NORM_FP, NORM_L = range(8)

        def split_hi(act, u):
            act.wait_ge(raw_in[u.slot], (u.round + 1) * 16)
            if not u.first:
                act.wait_ge(unit_done, u.n - 2)
            act.activation(w_hi[:, u.slot, :], w_raw[:, u.slot, :], ACT.Copy).then_inc(hi_ready, 1)

        def split_lo(dve, u):
            dve.wait_ge(hi_ready, u.n + 1)
            dve.tensor_tensor(w_lo[:, u.slot, :], w_raw[:, u.slot, :], w_hi[:, u.slot, :],
                              ALU.subtract).then_inc(lo_ready, 1)

        def square(act, n, k, src, width=T):
            if not isinstance(n, int) or n * 7 + k >= 2:
                act.wait_ge(acc_ready, n * 7 + (0, 0, 1, 1, 2, 3, 4, 5)[k])
            act.activation(sq[:, k % 2, 0:width], src, ACT.Square).then_inc(sq_ready, 1)

        def sum_squares(pool, n, width=T):
            for k in range(1, 8):
                pool.wait_ge(sq_ready, n * 8 + k + 1)
                if k > 1:
                    pool.wait_ge(acc_ready, n * 7 + k - 1)
                elif not isinstance(n, int) or n > 0:
                    pool.wait_ge(stat_done, n)
                pool.tensor_tensor(acc[:, 0:width], sq[:, 0, 0:width] if k == 1 else acc[:, 0:width], sq[:, k % 2, 0:width],
                                   ALU.add).then_inc(acc_ready, 1)

        def column_sums(pe, dst, *srcs):
            for b_ in range(srcs[0].shape[1] // P):
                for i, src in enumerate(srcs):
                    mm = pe.matmul(dst[:, b_:b_ + 1], src[:, b_ * P:(b_ + 1) * P], ones[:, 0:1],
                                   start=(i == 0), stop=(i == len(srcs) - 1))
            return mm

        def spread(pe, dst, src):
            for b_ in range(src.shape[1]):
                mm = pe.transpose(dst[:, b_ * P:(b_ + 1) * P], src[:, b_:b_ + 1].to_broadcast([P, P]), ident[:, :])
            return mm

        def stat_columns(pe, n, width=T):
            pe.wait_ge(acc_ready, n * 7 + 7)
            if not isinstance(n, int) or n > 0:
                pe.wait_ge(std_ready, n)
            column_sums(pe, bank[:, AUX, 0:width // P], acc[:, 0:width]).then_inc(stat_done, 1)

        def stat_rows(pe, n, src=rcol):
            pe.wait_ge(inv_ready, n + 1)
            if not isinstance(n, int) or n > 0:
                pe.wait_ge(r_ready, n)
            spread(pe, bank[:, STAT, :], src).then_inc(row_done, 1)

        def std_columns(act, n, dst=rcol):
            act.wait_ge(stat_done, n + 1)
            act.activation(dst[:, :], bank[:, AUX, 0:dst.shape[1]], ACT.Sqrt, bias=eps_c[:, 0:1], scale=1.0 / D).then_inc(std_ready, 1)

        def inv_columns(dve, n, dst=rcol):
            dve.wait_ge(std_ready, n + 1)
            dve.reciprocal(dst[:, :], dst[:, :]).then_inc(inv_ready, 1)

        def take_rows(act, n, dst=rbc):
            act.wait_ge(row_done, n + 1)
            act.activation(dst[:, :], bank[:, STAT, 0:dst.shape[1]], ACT.Copy).then_inc(r_ready, 1)

        def pre_norm_hi(act, i, n, k, gain, layer=None):
            act.activation(x_hi[:, k, :], h[:, k, :], ACT.Copy, scale=col(gain, k, layer)).then_inc(pre_hi, 1)
            square(act, n, k, h[:, k, :])

        def pre_norm_lo(dve, i, k, gain, layer=None):
            dve.wait_ge(pre_hi, i * 8 + k + 1)
            dve.scalar_tensor_tensor(out=x_lo[:, k, :], in0=h[:, k, :], scalar=col(gain, k, layer),
                                     in1=x_hi[:, k, :], op0=ALU.mult, op1=ALU.subtract).then_inc(pre_lo, 1)

        def products(pe, u, m, k, kx_, pair, start, stop, hi, lo, width=T, chunks=8):
            wh = w_hi[:, u.slot, :].rearrange("p (k c) -> p k c", k=chunks)
            wl = w_lo[:, u.slot, :].rearrange("p (k c) -> p k c", k=chunks)
            cols = slice(m * P, (m + 1) * P)
            dst = bank[:, 2 * pair + m, 0:width]
            pe.matmul(dst, wh[:, k, cols], hi[:, kx_, 0:width], start=start, stop=False)
            pe.matmul(dst, wh[:, k, cols], lo[:, kx_, 0:width], start=False, stop=False)
            return pe.matmul(dst, wl[:, k, cols], hi[:, kx_, 0:width], start=False, stop=stop)

        def linear_tile(pe, u, m, hi=x_hi, lo=x_lo, width=T):
            for k in range(8):
                mm = products(pe, u, m, k, k, u.slot, k == 0, k == 7, hi, lo, width)
            return mm

        def linear(pe, u, hi=x_hi, lo=x_lo, width=T):
            pe.wait_ge(lo_ready, u.n + 1)
            for m in range(2):
                mm = linear_tile(pe, u, m, hi, lo, width)
            mm.then_inc(unit_done, 1)

        def linear_start(pe, us, chunk_ready, norm=None):
            for i, u in enumerate(us):
                pe.wait_ge(lo_ready, u.n + 1)
                if i == 0:
                    for k in range(8):
                        chunk_ready(k)
                        for m in range(2):
                            mm = products(pe, u, m, k, k, u.slot, k == 0, k == 7, x_hi, x_lo)
                else:
                    linear_tile(pe, u, 0)
                    if norm is not None:
                        stat_columns(pe, norm)
                    for k in range(8):
                        if k == 4 and norm is not None:
                            stat_rows(pe, norm)
                        mm = products(pe, u, 1, k, k, u.slot, k == 0, k == 7, x_hi, x_lo)
                mm.then_inc(unit_done, 1)

        def tokens_major(pe, u, hi, lo, blocks, c0, n, bank_of):
            wh, wl = ki(w_hi, u.slot), ki(w_lo, u.slot)
            for b_ in range(blocks):
                bk, at = bank_of(b_)
                dst = bank[:, bk, at:at + n]
                for k in range(8):
                    xh, xl = hi[:, k, b_ * P:(b_ + 1) * P], lo[:, k, b_ * P:(b_ + 1) * P]
                    pe.matmul(dst, xh, wh[:, k, c0:c0 + n], start=(k == 0), stop=False)
                    pe.matmul(dst, xl, wh[:, k, c0:c0 + n], start=False, stop=False)
                    mm = pe.matmul(dst, xh, wl[:, k, c0:c0 + n], start=False, stop=(k == 7))
            return mm

        def units(eng, first, count, layer, body):
            turns = count // SLOTS
            if turns >= 2:
                with eng.Fori(0, turns) as i:
                    for s in range(SLOTS):
                        body(Unit(first + s, layer, i), s, i)
            else:
                turns = 0
            for j in range(turns * SLOTS, count):
                body(Unit(first + j, layer), j, None)

        gu_scaled, silu_done, f_ready, f_hi_done, f_lo_done = (sem(n) for n in (
            "gate_up_scaled", "silu_done", "f_ready", "f_hi_done", "f_lo_done"))

        def tile_of(j, i):
            return j if i is None else i * SLOTS + j

        def pick(t, j, i):
            return t[:, j, :] if i is None else t[:, bass.ds(i * SLOTS + j, 1), :].rearrange("p o t -> p (o t)")

        def ffn_up_act(act, first, call, layer):
            def body(u, j, i):
                n = tile_of(j, i) + call * FT
                g, up = bank[:, 2 * u.slot, :], bank[:, 2 * u.slot + 1, :]
                act.wait_ge(gu_scaled, n * 2 + 1)
                act.activation(silu[:, :], g, ACT.Silu).then_inc(silu_done, 1)
                act.wait_ge(f_ready, n + 1)
                act.activation(pick(f_hi, j, i), up, ACT.Copy).then_inc(f_hi_done, 1)
                split_hi(act, Unit(u.n0 + SLOTS, layer, i))
            units(act, first, FT, layer, body)

        def ffn_up_dve(dve, first, norm, call, layer):
            def body(u, j, i):
                n = tile_of(j, i) + call * FT
                g, up = bank[:, 2 * u.slot, :], bank[:, 2 * u.slot + 1, :]
                dve.wait_ge(unit_done, u.n + 1)
                dve.wait_ge(r_ready, norm + 1)
                dve.tensor_tensor(g, g, rbc[:, :], ALU.mult).then_inc(gu_scaled, 1)
                dve.tensor_tensor(up, up, rbc[:, :], ALU.mult).then_inc(gu_scaled, 1)
                dve.wait_ge(gu_scaled, n * 2 + 2)
                dve.wait_ge(silu_done, n + 1)
                dve.tensor_tensor(up, up, silu[:, :], ALU.mult).then_inc(f_ready, 1)
                dve.wait_ge(f_hi_done, n + 1)
                dve.tensor_tensor(pick(f_lo, j, i), up, pick(f_hi, j, i), ALU.subtract).then_inc(f_lo_done, 1)
                split_lo(dve, Unit(u.n0 + SLOTS, layer, i))
            units(dve, first, FT, layer, body)

        def ffn_pe(pe, first, pre, norm, call, layer):
            linear_start(pe, [Unit(first + s, layer) for s in range(2)],
                         lambda k: pe.wait_ge(pre_lo, pre * 8 + k + 1), norm)
            linear(pe, Unit(first + 2, layer))
            units(pe, first + 3, FT - 3, layer, lambda u, j, i: linear(pe, u))
            down = first + FT
            with pe.Fori(0, 2) as i:
                for g in range(2):
                    for part in range(3):
                        u = Unit(down + g * 3 + part, layer)
                        n = i * 6 + u.n
                        if g == part == 0:
                            pe.wait_ge(f_lo_done, (call + 1) * FT)
                        pe.wait_ge(lo_ready, n + 1)
                        ks = range(8 * part, min(8 * part + 8, FT))
                        for m in range(2):
                            for k in ks:
                                mm = products(pe, u, m, k - 8 * part, k, g, k == 0, k == FT - 1, f_hi, f_lo)
                        mm.then_inc(unit_done, 1)

        block = ctx.enter_context(nc.Block())

        @block.sync
        def _(sp):
            for s in range(SLOTS):
                if s == 1:
                    sp.wait_ge(x_in[DT // 2 - 1], 16)
                sp.dma_start(w_raw[:, s, :], w[s]).then_inc(raw_in[s], 16)
            with sp.Fori(1, UNITS // SLOTS) as i:
                for s in range(SLOTS):
                    sp.wait_ge(lo_ready, i * SLOTS + (s - 2))
                    sp.dma_start(w_raw[:, s, :], w[bass.ds(i * SLOTS + s, 1)].rearrange("o p c -> (o p) c"))\
                      .then_inc(raw_in[s], 16)
            sp.wait_ge(h_ready, 24 + 16 * LAYERS)
            sp.dma_start(out, h[:, :, :]).then_inc(out_done, 16)
            sp.wait_ge(out_done, 16)

        proj_ready, xin_scaled, vtok_ready, gate_done, gate_copied, gate_turned, gate_ready = (sem(n) for n in (
            "proj_ready", "xin_scaled", "vtok_ready", "gate_done", "gate_copied", "gate_turned", "gate_ready"))
        trig_step, sin_ready, wg_lo_ready = sem("trig_step"), sem("sin_ready"), sem("wg_lo_ready")
        rot_done, rope_cos, rope_sin, rope_done, kx_ready = (sem(n) for n in (
            "rot_done", "rope_cos", "rope_sin", "rope_done", "kx_ready"))
        xf_ready, xc_hi_ready, xc_lo_ready, xf_pe, hid_ready, hid_turned, hc_ready = (sem(n) for n in (
            "xf_ready", "xc_hi_ready", "xc_lo_ready", "xf_pe", "hid_ready", "hid_turned", "hc_ready"))
        kc_done, vc_done, kc2_ready, kcrot_done, kc_rope, kcm_ready, kcm_dup, vblk_zero, vblk_ready = (
            sem(n) for n in ("kc_done", "vc_done", "kc2_ready", "kcrot_done", "kc_rope", "kcm_ready", "kcm_dup",
                             "vblk_zero", "vblk_ready"))
        conv_step, csq_ready, cstat_done, cstd_ready, cinv_ready, crow_done, cn_ready, mix_hi, mix_lo = (sem(n) for n in (
            "conv_step", "csq_ready", "cstat_done", "cstd_ready", "cinv_ready", "crow_done", "cn_ready", "mix_hi", "mix_lo"))
        c_sub, c_sum, c_w = sem("cmp_sub"), sem("cmp_sum"), sem("cmp_weight")
        j_s, j_max, j_neg, j_exp, j_rec, j_w, j_t, j_pta, j_ptd, j_pv, j_o = (sem("job_" + n) for n in (
            "scores", "max", "neg", "exp", "recip", "weight", "turned", "turned_copied_act",
            "turned_copied_dve", "pv", "out"))
        ao_sq, ao_std, ao_inv, ao_n, ao_t = (sem("attn_norm_" + n) for n in ("squares", "std", "inv", "scaled", "turned"))
        JOBS = QB * 8
        LAG_TURN, LAG_VALUES, LAG_BACK = 2, 3, 4
        MEM_FROM = 10

        def rope_tile(r):
            return qT[:, r, :] if r < 4 else kT[:, r - 4, :]

        def rot_pe(pe, r):
            pe.wait_ge(proj_ready, 12 + r + 1 if r < 4 else 18 + (r - 4) + 1)
            if r >= 2:
                pe.wait_ge(rope_done, r - 1)
            else:
                pe.wait_ge(r_ready, 1)
            pe.matmul(bank[:, STAT + r % 2, :], perm[:, :], rope_tile(r), start=True, stop=True).then_inc(rot_done, 1)

        def rope_pool(pool, r):
            pool.wait_ge(proj_ready, 12 + r + 1 if r < 4 else 18 + (r - 4) + 1)
            pool.wait_ge(sin_ready, 3)
            if r >= 2:
                pool.wait_ge(rope_done, r - 1)
            pool.tensor_tensor(ctmp[:, r % 2, :], rope_tile(r), cosT[:, :], ALU.mult).then_inc(rope_cos, 1)

        def rope_dve(dve, r):
            rot = bank[:, STAT + r % 2, :]
            dve.wait_ge(rot_done, r + 1)
            dve.wait_ge(sin_ready, 3)
            dve.tensor_tensor(rot, rot, sinT[:, :], ALU.mult).then_inc(rope_sin, 1)
            dve.wait_ge(rope_sin, r + 1)
            dve.wait_ge(rope_cos, r + 1)
            dve.tensor_tensor(rope_tile(r), ctmp[:, r % 2, :], rot, ALU.add).then_inc(rope_done, 1)

        def key_rows(t, tx, e, g):
            return (t if g == e else tx)[HD * e:HD * e + HD]

        def mixer1_pe(pe):
            pe.wait_ge(const_ready, 1)
            pe.wait_ge(tab_in, 80)
            linear_start(pe, [Unit(U_IN + s) for s in range(2)], lambda k: pe.wait_ge(pre_lo, k + 1), NORM_MIX)
            for j in range(2, 10):
                linear(pe, Unit(U_IN + j))
                for r in {7: (0, 1), 8: (2, 3)}.get(j, ()):
                    rot_pe(pe, r)
            u = Unit(U_IN + 10)
            pe.wait_ge(lo_ready, u.n + 1)
            tokens_major(pe, u, x_hi, x_lo, QB, 0, 2 * P, lambda b_: (2 * u.slot + b_ // 2, b_ % 2 * 2 * P))\
                .then_inc(unit_done, 1)
            pe.wait_ge(wg_lo_ready, 1)
            pe.wait_ge(proj_ready, 18)
            for k in range(8):
                wh, wl = wg_hi[:, k * 24:(k + 1) * 24], wg_lo[:, k * 24:(k + 1) * 24]
                dst = bank[0:24, 4, :]
                pe.matmul(dst, wh, x_hi[:, k, :], start=(k == 0), stop=False)
                pe.matmul(dst, wh, x_lo[:, k, :], start=False, stop=False)
                mm = pe.matmul(dst, wl, x_hi[:, k, :], start=False, stop=(k == 7))
            mm.then_inc(gate_done, 1)
            rot_pe(pe, 4)
            rot_pe(pe, 5)
            pe.wait_ge(gate_copied, 1)
            for b_ in range(QB):
                mm = pe.transpose(bank[:, 4, b_ * 24:(b_ + 1) * 24], sq[0:24, 0, b_ * P:(b_ + 1) * P], ident[0:24, 0:24])
            mm.then_inc(gate_turned, 1)
            pe.wait_ge(proj_ready, 20)
            pe.wait_ge(xc_lo_ready, 1)
            for kv in range(2):
                if kv == 1:
                    pe.wait_ge(vtok_ready, QB)
                for part in range(2):
                    u = Unit(U_W1 + 2 * kv + part)
                    pe.wait_ge(lo_ready, u.n + 1)
                    for k in range(8):
                        c, dst = 8 * part + k, bank[0:WINDOWS, 2 * kv, 0:2 * P]
                        wh, wl = ki(w_hi, u.slot)[:, k, :], ki(w_lo, u.slot)[:, k, :]
                        pe.matmul(dst, xc_hi[:, kv, c, :], wh, start=(c == 0), stop=False)
                        pe.matmul(dst, xc_hi[:, kv, c, :], wl, start=False, stop=False)
                        mm = pe.matmul(dst, xc_lo[:, kv, c, :], wh, start=False, stop=(c == 15))
                    mm.then_inc(unit_done, 1)
            pe.wait_ge(csq_ready, 4)
            column_sums(pe, bank[:, 5, 0:QB], *(z[:, m, :] for m in range(4))).then_inc(cstat_done, 1)
            for kv in range(2):
                pe.wait_ge(hid_ready, kv + 1)
                for m in range(2):
                    mm = pe.transpose(bank[:, 2 * kv + 1, m * WINDOWS:(m + 1) * WINDOWS], hid[:, kv, m * P:(m + 1) * P],
                                      ident[0:WINDOWS, 0:WINDOWS])
                mm.then_inc(hid_turned, 1)
            pe.wait_ge(hc_ready, 1)
            pe.wait_ge(rope_done, 6)
            for m in range(2):
                mm = pe.matmul(bank[0:HD, 6, 0:2 * NCMP], w2_s[:, 0, m, :], hc[:, 0, m, :],
                               start=(m == 0), stop=(m == 1))
            mm.then_inc(kc_done, 1)
            pe.wait_ge(cinv_ready, 1)
            spread(pe, bank[:, 5, :], rcol_c).then_inc(crow_done, 1)
            pe.wait_ge(hc_ready, 2)
            pe.wait_ge(gate_ready, QB)
            for g in range(2):
                for m in range(2):
                    mm = pe.matmul(bank[0:NCMP, 4, g * HD:(g + 1) * HD], hc[:, 1, m, g * NCMP:(g + 1) * NCMP],
                                   w2_s[:, 1, m, :], start=(m == 0), stop=(m == 1))
            mm.then_inc(vc_done, 1)
            pe.wait_ge(kc2_ready, 1)
            pe.matmul(bank[0:HD, 7, 0:2 * NCMP], perm[0:HD, 0:HD], kc2[:, :, :].rearrange("p g c -> p (g c)"),
                      start=True, stop=True).then_inc(kcrot_done, 1)

            def c_scores(i):
                if i == 0:
                    pe.wait_ge(kcm_dup, 1)
                    pe.wait_ge(rope_done, 6)
                    pe.wait_ge(hc_ready, 2)
                    pe.wait_ge(mask_ready, 3)
                if i >= 2:
                    pe.wait_ge(c_sub, i - 1)
                for e in range(2):
                    b_ = 2 * (i % 2) + e
                    pe.matmul(bank[:, b_, 0:P], ident_b[:, :], cmask_b[:, i, :], start=True, stop=False)
                    for m in range(4):
                        mm = pe.matmul(bank[:, b_, m * 32:(m + 1) * 32], qT[HD * e:HD * e + HD, m, i * P:(i + 1) * P],
                                       kcm[HD * e:HD * e + HD, m // 2, :], start=False, stop=(m == 3))
                mm.then_inc(j_s, 1)

            def c_turn(i):
                pe.wait_ge(j_exp, i + 1)
                if i == 0:
                    pe.wait_ge(vblk_ready, 4)
                    pe.wait_ge(cn_ready, 4)
                if i >= 2:
                    pe.wait_ge(j_pta, i - 1)
                for e in range(2):
                    mm = pe.transpose(bank[:, 4 + i % 2, e * P:(e + 1) * P], e_c[:, i % 2, e * P:(e + 1) * P], ident[:, :])
                mm.then_inc(j_t, 1)

            def c_values(i):
                pe.wait_ge(j_pta, i + 1)
                if i == 0:
                    pe.wait_ge(kc_rope, 3)
                if i >= 2:
                    pe.wait_ge(j_o, i - 1)
                for e in range(2):
                    mm = pe.matmul(bank[:, 6 + i % 2, e * 4 * HD:(e + 1) * 4 * HD], pt_c[:, i % 2, e * P:(e + 1) * P],
                                   vblk[:, :], start=True, stop=True)
                mm.then_inc(j_pv, 1)

            for t in range(QB + 2):
                if t < QB:
                    c_scores(t)
                if 0 <= t - 1 < QB:
                    c_turn(t - 1)
                if t >= 2:
                    c_values(t - 2)

            def scores(j):
                i, hd = j // 8, j % 8
                m, e, g = hd // 2, hd % 2, hd // 4
                n = (i + 1) * P
                if j == 0:
                    pe.wait_ge(kx_ready, 4)
                if j < 2:
                    pe.wait_ge(c_sub, QB)
                else:
                    pe.wait_ge(j_exp, QB + 2 * (j - 1))
                for br in range(2):
                    b_ = 2 * (j % 2) + br
                    pe.matmul(bank[:, b_, 0:n], qT[HD * e:HD * e + HD, m, i * P:(i + 1) * P],
                              key_rows(kT, kTx, e, g)[:, br, 0:n], start=True, stop=False)
                    mm = pe.matmul(bank[:, b_, i * P:n], ident_b[:, :], mask_b[:, P:2 * P], start=False, stop=True)
                mm.then_inc(j_s, 1)

            def turn(j):
                i = j // 8
                pe.wait_ge(j_exp, QB + 2 * (j + 1))
                if j == 0:
                    pe.wait_ge(j_pta, QB)
                else:
                    pe.wait_ge(j_pta, QB + j)
                    pe.wait_ge(j_ptd, j)
                for br in range(2):
                    for k in range(i + 1):
                        mm = pe.transpose(bank[:, 4 + br, k * P:(k + 1) * P], prob[:, j % 2, br, k * P:(k + 1) * P], ident[:, :])
                mm.then_inc(j_t, 1)

            def values(j):
                i, g = j // 8, j % 8 // 4
                pe.wait_ge(j_pta, QB + j + 1)
                pe.wait_ge(j_ptd, j + 1)
                if j < 2:
                    pe.wait_ge(j_o, QB)
                else:
                    pe.wait_ge(j_o, QB + 2 * (j - 1))
                for br in range(2):
                    for k in range(i + 1):
                        mm = pe.matmul(bank[:, 6 + j % 2, br * HD:(br + 1) * HD], probT[:, j % 2, br, k * P:(k + 1) * P],
                                       vtok[:, k, br * P + g * HD:br * P + (g + 1) * HD], start=(k == 0), stop=(k == i))
                mm.then_inc(j_pv, 1)

            for t in range(JOBS + LAG_VALUES):
                if t < JOBS:
                    scores(t)
                if 0 <= t - LAG_TURN < JOBS:
                    turn(t - LAG_TURN)
                if t >= LAG_VALUES:
                    values(t - LAG_VALUES)

            pe.wait_ge(j_exp, QB + 2 * JOBS)
            for b_ in range(QB):
                pe.wait_ge(ao_n, b_ + 1)
                for m in range(4):
                    mm = pe.transpose(bank[:, b_, m * P:(m + 1) * P], o_all[:, b_, m * P:(m + 1) * P], ident[:, :])
                mm.then_inc(ao_t, 1)
            pe.wait_ge(j_o, QB)
            pe.wait_ge(j_o, QB + 2 * JOBS)
            stat_columns(pe, NORM_MEM, MEM)
            stat_rows(pe, NORM_MEM, rcol_mem)

            def mixed(k):
                pe.wait_ge(mix_lo, k + 1)
            pe.wait_ge(mix_lo, 8)
            linear_start(pe, [Unit(U_OUT + s) for s in range(2)], mixed)
            for j in range(2, 4):
                linear(pe, Unit(U_OUT + j))

        def mixer1_act(act):
            act.dma_start(gains[:, :], pack).then_inc(gains_in, 16)
            for k in range(0, DT, 2):
                act.dma_start(h[:, k:k + 2, :], x[:, k * T:(k + 2) * T].rearrange("p (k t) -> p k t", k=2)).then_inc(x_in[k // 2], 16)
            act.dma_start(ident[:, :], tables[:, 0:P]).then_inc(tab_in, 16)
            act.dma_start(perm[:, :], tables[:, P:2 * P]).then_inc(tab_in, 16)
            act.dma_start(pos_i[:, :], pos.to_broadcast([P, T])).then_inc(pos_in, 16)
            act.dma_start(stage[:, 0:6 * P], cmask).then_inc(tab_in, 16)
            act.dma_start(w2_s[:, :, :, :].rearrange("p a m d -> p (a m d)"), w2).then_inc(tab_in, 16)
            act.dma_start(wg_s[:, :], wg).then_inc(tab_in, 16)
            split_hi(act, Unit(0))
            act.wait_ge(gains_in, 16)
            for k in range(DT):
                if k % 2 == 0:
                    act.wait_ge(x_in[k // 2], 16)
                pre_norm_hi(act, 0, NORM_MIX, k, "mix_pre")
            for s in (1, 2):
                split_hi(act, Unit(s))
            act.wait_ge(const_ready, 2)
            std_columns(act, NORM_MIX)
            take_rows(act, NORM_MIX)
            act.wait_ge(tab_in, 80)
            act.activation(ident_b[:, :], ident[:, :], ACT.Copy).then_inc(mask_ready, 1)
            act.activation(mask_b[:, :], stage[:, 0:2 * P], ACT.Copy).then_inc(mask_ready, 1)
            act.activation(cmask_b[:, :, :].rearrange("p b c -> p (b c)"), stage[:, 2 * P:6 * P], ACT.Copy).then_inc(mask_ready, 1)
            act.activation(wg_hi[:, :], wg_s[:, :], ACT.Copy).then_inc(mask_ready, 1)
            act.wait_ge(trig_step, 8)
            act.wait_ge(const_ready, 2)
            act.activation(sinT[:, :], ctmp[:, 1, :], ACT.Sin).then_inc(sin_ready, 1)
            act.activation(cosT[:, :], ctmp[:, 1, :], ACT.Abs).then_inc(sin_ready, 1)
            act.wait_ge(sin_ready, 2)
            act.activation(cosT[:, :], cosT[:, :], ACT.Sin, bias=eps_c[:, 2:3], scale=-1.0).then_inc(sin_ready, 1)
            for j in range(9):
                split_hi(act, Unit(U_IN + j + 3))
            act.wait_ge(proj_ready, 18)
            for kv in range(2):
                for g in range(2):
                    for par in range(2):
                        for half in range(2):
                            v = kvc[g * HD:(g + 1) * HD, kv, 16 * half:16 * half + 16 * NCMP]\
                                .rearrange("p (c j q) -> p j c q", j=8, q=2)[:, :, :, par]
                            act.activation(xf[par * HD:(par + 1) * HD, kv, 8 * half:8 * half + 8, g * NCMP:(g + 1) * NCMP],
                                           v, ACT.Copy).then_inc(xf_ready, 1)
            split_hi(act, Unit(U_IN + 12))
            act.wait_ge(xf_pe, 2)
            for kv in range(2):
                act.activation(xc_hi[:, kv, :, :], xf[:, kv, :, :], ACT.Copy).then_inc(xc_hi_ready, 1)
            act.wait_ge(unit_done, U_IN + 11)
            act.wait_ge(inv_ready, 1)
            for b_ in range(QB):
                act.activation(vtok[:, b_, :], bank[:, 2 + b_ // 2, b_ % 2 * 2 * P:(b_ % 2 + 1) * 2 * P], ACT.Copy,
                               scale=rcol[:, b_:b_ + 1]).then_inc(vtok_ready, 1)
            split_hi(act, Unit(U_IN + 13))
            act.wait_ge(gate_done, 1)
            act.activation(sq[0:24, 0, :], bank[0:24, 4, :], ACT.Copy).then_inc(gate_copied, 1)
            act.wait_ge(gate_turned, 1)
            for b_ in range(QB):
                act.activation(gate[:, b_, :], bank[:, 4, b_ * 24:(b_ + 1) * 24], ACT.Sigmoid,
                               scale=rcol[:, b_:b_ + 1]).then_inc(gate_ready, 1)
            for r in range(2):
                act.wait_ge(rope_done, 5 + r)
                act.activation(kTx[0:HD, r, :], kT[HD:P, r, :], ACT.Copy).then_inc(kx_ready, 1)
                act.activation(kTx[HD:P, r, :], kT[0:HD, r, :], ACT.Copy).then_inc(kx_ready, 1)
            split_hi(act, Unit(U_IN + 14))
            for m in range(4):
                act.wait_ge(conv_step, 12 + m + 1)
                act.activation(z[:, m, :], cv[:, m, :], ACT.Square).then_inc(csq_ready, 1)
            for u in range(U_W1 + 1, U_W1 + 4):
                split_hi(act, Unit(u + 3))
            act.wait_ge(cstat_done, 1)
            act.activation(rcol_c[:, :], bank[:, 5, 0:QB], ACT.Sqrt, bias=eps_c[:, 0:1], scale=1.0 / 512).then_inc(cstd_ready, 1)
            for kv in range(2):
                act.wait_ge(unit_done, U_W1 + 2 * kv + 2)
                act.activation(hid[:, kv, :], bank[0:WINDOWS, 2 * kv, 0:2 * P], ACT.Silu).then_inc(hid_ready, 1)
            for kv in range(2):
                act.wait_ge(hid_turned, kv + 1)
                act.activation(hc[:, kv, :, :].rearrange("p m c -> p (m c)"), bank[:, 2 * kv + 1, 0:2 * WINDOWS], ACT.Copy).then_inc(hc_ready, 1)
            act.wait_ge(kc_done, 1)
            act.activation(kc2[:, :, :].rearrange("p g c -> p (g c)"), bank[0:HD, 6, 0:2 * NCMP], ACT.Copy).then_inc(kc2_ready, 1)
            act.wait_ge(vc_done, 1)
            act.wait_ge(vblk_zero, 1)
            for m in range(4):
                act.activation(vblk[m * 32:m * 32 + NCMP, m * HD:(m + 1) * HD], bank[0:NCMP, 4, (m // 2) * HD:(m // 2 + 1) * HD],
                               ACT.Copy).then_inc(vblk_ready, 1)
            act.wait_ge(kcm_ready, 1)
            act.activation(kcm[HD:P, :, :], kcm[0:HD, :, :], ACT.Copy).then_inc(kcm_dup, 1)
            act.wait_ge(gate_done, 1)
            for m in range(4):
                act.wait_ge(cn_ready, m + 1)
                act.activation(x_hi[:, m, :], cv[:, m, :], ACT.Copy, scale=col("conv_out", m)).then_inc(mix_hi, 1)

            def c_e(i):
                act.wait_ge(c_sub, i + 1)
                act.activation(e_c[:, i % 2, :], e_c[:, i % 2, :], ACT.Exp).then_inc(j_exp, 1)

            def c_copy(i):
                act.wait_ge(j_t, i + 1)
                if i >= 2:
                    act.wait_ge(j_pv, i - 1)
                act.activation(pt_c[:, i % 2, :], bank[:, 4 + i % 2, 0:2 * P], ACT.Copy).then_inc(j_pta, 1)

            for t in range(QB + 1):
                if t < QB:
                    c_e(t)
                if t >= 1:
                    c_copy(t - 1)

            def exps(j):
                n = (j // 8 + 1) * P
                act.wait_ge(j_neg, QB + j + 1)
                if j >= 2:
                    act.wait_ge(j_t, QB + j - 1)
                if j >= 4:
                    act.wait_ge(j_rec, j - 3)
                for br in range(2):
                    act.activation(prob[:, j % 2, br, 0:n], bank[:, 2 * (j % 2) + br, 0:n], ACT.Exp,
                                   bias=jsm(j, 2, br), accum_out=jsm(j, 4, br)).then_inc(j_exp, 1)

            def copy_turned(j):
                n = (j // 8 + 1) * P
                act.wait_ge(j_t, QB + j + 1)
                if j >= 2:
                    act.wait_ge(j_pv, QB + j - 1)
                act.activation(probT[:, j % 2, 0, 0:n], bank[:, 4, 0:n], ACT.Copy).then_inc(j_pta, 1)

            act.wait_ge(unit_done, U_OUT)
            def squares_of_block(b_):
                act.wait_ge(j_o, QB + 2 * 8 * (b_ + 1))
                if b_ >= 2:
                    act.wait_ge(ao_sq, b_ - 1)
                act.activation(ctmp[:, b_ % 2, :], o_all[:, b_, :], ACT.Square, accum_out=small[:, 32 + b_:33 + b_]).then_inc(ao_sq, 1)

            act.dma_start(memT[:, :, :].rearrange("p k t -> p (k t)"), mem).then_inc(tab_in, 16)
            for t in range(JOBS + LAG_TURN):
                if t < JOBS:
                    exps(t)
                if t >= LAG_TURN:
                    copy_turned(t - LAG_TURN)
                if MEM_FROM <= t < MEM_FROM + DT:
                    k = t - MEM_FROM
                    act.wait_ge(tab_in, 96)
                    act.activation(m_hi[:, k, :], memT[:, k, :], ACT.Copy, scale=col("mem", k)).then_inc(mem_hi, 1)
                    square(act, NORM_MEM, k, memT[:, k, :], MEM)
                if t % 8 == 5 and 8 < t:
                    squares_of_block(t // 8 - 1)

            squares_of_block(QB - 1)
            act.wait_ge(ao_sq, QB)
            act.activation(small[:, 36:40], small[:, 32:36], ACT.Sqrt, bias=eps_c[:, 0:1], scale=1.0 / 512).then_inc(ao_std, 1)
            act.wait_ge(ao_t, QB)
            for m in range(4):
                act.activation(x_hi[:, 4 + m, :].rearrange("p (b t) -> p b t", b=QB), bank[:, 0:QB, m * P:(m + 1) * P],
                               ACT.Copy, scale=col("attn_out", m)).then_inc(mix_hi, 1)
            std_columns(act, NORM_MEM, rcol_mem)
            take_rows(act, NORM_MEM, rmem)

        def jsm(j, a_, br=None):
            c = 16 * (j % 4) + a_
            return jcol[:, c:c + 2] if br is None else jcol[:, c + br:c + br + 1]

        def mixer1_dve(dve):
            split_lo(dve, Unit(0))
            for k in range(DT):
                pre_norm_lo(dve, 0, k, "mix_pre")
            for s in (1, 2):
                split_lo(dve, Unit(s))
            ang, red = ctmp[:, 0, :], ctmp[:, 1, :]
            dve.wait_ge(pos_in, 16)
            dve.tensor_copy(red, pos_i[:, :]).then_inc(trig_step, 1)
            dve.wait_ge(trig_step, 1)
            dve.tensor_scalar(ang, red, col("inv"), None, ALU.mult).then_inc(trig_step, 1)
            dve.wait_ge(trig_step, 2)
            dve.tensor_scalar(sinT[:, :], ang, 1 / (2 * np.pi), ROUNDER, ALU.mult, ALU.add).then_inc(trig_step, 1)
            dve.wait_ge(trig_step, 3)
            dve.tensor_scalar(sinT[:, :], sinT[:, :], -ROUNDER, None, ALU.add).then_inc(trig_step, 1)
            for n, c in enumerate((C1, C2, C3)):
                dve.wait_ge(trig_step, 4 + n)
                dve.scalar_tensor_tensor(out=red, in0=sinT[:, :], scalar=-c, in1=ang if n == 0 else red,
                                         op0=ALU.mult, op1=ALU.add).then_inc(trig_step, 1)
            dve.wait_ge(trig_step, 7)
            dve.tensor_scalar(red, red, float(np.float32(3.1415925)), -float(np.float32(3.1415925)), ALU.min, ALU.max).then_inc(trig_step, 1)
            inv_columns(dve, NORM_MIX)
            dve.wait_ge(r_ready, NORM_MIX + 1)
            dve.wait_ge(mask_ready, 4)
            dve.tensor_tensor(wg_lo[:, :], wg_s[:, :], wg_hi[:, :], ALU.subtract).then_inc(wg_lo_ready, 1)

            for j in range(10):
                u = Unit(U_IN + j)
                dve.wait_ge(unit_done, u.n + 1)
                for m in range(2):
                    src, k = bank[:, 2 * u.slot + m, :], 2 * (j % 2) + m
                    if j < 2:
                        dve.tensor_tensor(bg[:, k, :], src, rbc[:, :], ALU.mult).then_inc(proj_ready, 1)
                    elif j < 4:
                        dve.tensor_tensor(z[:, k, :], src, rbc[:, :], ALU.mult).then_inc(proj_ready, 1)
                    elif j < 6:
                        dve.tensor_tensor(src, src, rbc[:, :], ALU.mult).then_inc(xin_scaled, 1)
                    elif j < 8:
                        dve.scalar_tensor_tensor(out=qT[:, k, :], in0=src, scalar=HD ** -0.5, in1=rbc[:, :],
                                                 op0=ALU.mult, op1=ALU.mult).then_inc(proj_ready, 1)
                    else:
                        dve.tensor_tensor((kvc if j == 8 else kT)[:, m, :], src, rbc[:, :], ALU.mult).then_inc(proj_ready, 1)
                if j in (4, 5):
                    for m in range(2):
                        k = 2 * (j % 2) + m
                        dve.wait_ge(xin_scaled, k + 1)
                        dve.tensor_tensor(z[:, k, :], z[:, k, :], bank[:, 2 * u.slot + m, :], ALU.mult).then_inc(proj_ready, 1)
                split_lo(dve, Unit(U_IN + j + 3))
                for r in {8: (0, 1), 9: (2, 3)}.get(j, ()):
                    rope_dve(dve, r)
            dve.wait_ge(xf_ready, 16)
            for kv in range(2):
                pe_col = gains[:, _cols["pe_v" if kv else "pe_k"][0]:][:, 0:16]
                dve.tensor_tensor(xf[:, kv, :, :], xf[:, kv, :, :], pe_col.unsqueeze(2).to_broadcast([P, 16, WINDOWS]), ALU.add).then_inc(xf_pe, 1)
            dve.wait_ge(xc_hi_ready, 2)
            dve.tensor_tensor(xc_lo[:, :, :, :].rearrange("p v j c -> p (v j c)"), xf[:, :, :, :].rearrange("p v j c -> p (v j c)"),
                              xc_hi[:, :, :, :].rearrange("p v j c -> p (v j c)"), ALU.subtract).then_inc(xc_lo_ready, 1)
            split_lo(dve, Unit(U_IN + 13))
            rope_dve(dve, 4)
            rope_dve(dve, 5)
            for step in range(4):
                for m in range(4):
                    if step:
                        dve.wait_ge(conv_step, 4 * (step - 1) + m + 1)
                    else:
                        dve.wait_ge(proj_ready, 12)
                        dve.wait_ge(mask_ready, 3)
                    wk = lambda k: col("conv_w", 3 * m + k)
                    if step == 0:
                        ins = dve.tensor_scalar(cv[:, m, :], z[:, m, :], wk(2), None, ALU.mult)
                    elif step < 3:
                        ins = dve.scalar_tensor_tensor(out=cv[:, m, step:T], in0=z[:, m, 0:T - step], scalar=wk(2 - step),
                                                       in1=cv[:, m, step:T], op0=ALU.mult, op1=ALU.add)
                    else:
                        ins = dve.tensor_tensor(cv[:, m, :], cv[:, m, :], bg[:, m, :], ALU.mult)
                    ins.then_inc(conv_step, 1)
            for j in range(14, 18):
                split_lo(dve, Unit(j))
            dve.wait_ge(cstd_ready, 1)
            dve.reciprocal(rcol_c[:, :], rcol_c[:, :]).then_inc(cinv_ready, 1)
            dve.wait_ge(crow_done, 1)
            for m in range(4):
                dve.tensor_tensor(cv[:, m, :], cv[:, m, :], bank[:, 5, :], ALU.mult).then_inc(cn_ready, 1)
            ends = slice(31, T, 16)
            dve.wait_ge(kc2_ready, 1)
            dve.wait_ge(kcrot_done, 1)
            rot = bank[0:HD, 7, 0:2 * NCMP].rearrange("p (g c) -> p g c", g=2)
            dve.tensor_tensor(rot, rot, sinT[0:HD, ends].unsqueeze(1).to_broadcast([HD, 2, NCMP]), ALU.mult).then_inc(kc_rope, 1)
            dve.tensor_tensor(kc2[:, :, :], kc2[:, :, :], cosT[0:HD, ends].unsqueeze(1).to_broadcast([HD, 2, NCMP]), ALU.mult).then_inc(kc_rope, 1)
            dve.wait_ge(kc_rope, 2)
            dve.tensor_tensor(kc2[:, :, :], kc2[:, :, :], rot, ALU.add).then_inc(kc_rope, 1)
            dve.wait_ge(kc_rope, 3)
            dve.wait_ge(vblk_zero, 1)
            dve.tensor_copy(kcm[0:HD, :, 0:NCMP], kc2[:, :, :]).then_inc(kcm_ready, 1)
            for m in range(4):
                dve.wait_ge(mix_hi, m + 1)
                dve.scalar_tensor_tensor(out=x_lo[:, m, :], in0=cv[:, m, :], scalar=col("conv_out", m), in1=x_hi[:, m, :],
                                         op0=ALU.mult, op1=ALU.subtract).then_inc(mix_lo, 1)

            def csm(i, a_):
                return small[:, 32 * (i % 2) + a_:32 * (i % 2) + a_ + 8]

            def c_softmax(i):
                s = bank[:, 2 * (i % 2):2 * (i % 2) + 2, 0:P].rearrange("p e (m c) -> p e m c", c=32)
                v = lambda t: t.rearrange("p (e m) -> p e m", e=2)
                dve.wait_ge(j_s, i + 1)
                if i >= 2:
                    dve.wait_ge(j_t, i - 1)
                dve.tensor_reduce(v(csm(i, 0)), s, AX, ALU.max).then_inc(j_max, 1)
                dve.wait_ge(j_max, i + 1)
                dve.tensor_scalar(csm(i, 8), csm(i, 0), LOW, -1.0, ALU.max, ALU.mult).then_inc(j_neg, 1)
                dve.wait_ge(j_neg, i + 1)
                dve.tensor_tensor(e_c[:, i % 2, :].rearrange("p (e m c) -> p e m c", e=2, m=4), s,
                                  v(csm(i, 8)).unsqueeze(3).to_broadcast([P, 2, 4, 32]), ALU.add).then_inc(c_sub, 1)

            def c_weights(i):
                dve.wait_ge(j_exp, i + 1)
                dve.tensor_reduce(csm(i, 16), e_c[:, i % 2, :].rearrange("p (h c) -> p h c", c=32), AX, ALU.add).then_inc(c_sum, 1)
                dve.wait_ge(c_sum, i + 1)
                dve.tensor_scalar(csm(i, 16), csm(i, 16), 1e-30, None, ALU.max).then_inc(c_w, 1)
                dve.wait_ge(c_w, 3 * i + 1)
                dve.reciprocal(csm(i, 16), csm(i, 16)).then_inc(c_w, 1)
                dve.wait_ge(c_w, 3 * i + 2)
                g0 = gate[:, i, :].rearrange("p (m e b) -> p e m b", e=2, b=3)[:, :, :, 0]
                dve.tensor_tensor(csm(i, 24).rearrange("p (e m) -> p e m", e=2), csm(i, 16).rearrange("p (e m) -> p e m", e=2),
                                  g0, ALU.mult).then_inc(c_w, 1)

            def c_combine(i):
                dve.wait_ge(j_pv, i + 1)
                dve.wait_ge(c_w, 3 * i + 3)
                dve.tensor_tensor(o_all[:, i, :].rearrange("p (m e d) -> p e m d", e=2, d=HD),
                                  bank[:, 6 + i % 2, :].rearrange("p (e m d) -> p e m d", e=2, d=HD),
                                  csm(i, 24).rearrange("p (e m) -> p e m", e=2).unsqueeze(3).to_broadcast([P, 2, 4, HD]),
                                  ALU.mult).then_inc(j_o, 1)

            dve.wait_ge(gate_ready, QB)
            for t in range(QB + 2):
                if t < QB:
                    c_softmax(t)
                if 0 <= t - 1 < QB:
                    c_weights(t - 1)
                if t >= 2:
                    c_combine(t - 2)

            def maxima(j):
                n = (j // 8 + 1) * P
                dve.wait_ge(j_s, QB + j + 1)
                if j >= 4:
                    dve.wait_ge(j_exp, QB + 2 * (j - 3))
                dve.tensor_reduce(jsm(j, 0), bank[:, 2 * (j % 2):2 * (j % 2) + 2, 0:n], AX, ALU.max).then_inc(j_max, 1)
                dve.wait_ge(j_max, QB + j + 1)
                dve.tensor_scalar(jsm(j, 2), jsm(j, 0), LOW, -1.0, ALU.max, ALU.mult).then_inc(j_neg, 1)

            def copy_turned(j):
                n = (j // 8 + 1) * P
                dve.wait_ge(j_t, QB + j + 1)
                if j >= 2:
                    dve.wait_ge(j_pv, QB + j - 1)
                dve.tensor_copy(probT[:, j % 2, 1, 0:n], bank[:, 5, 0:n]).then_inc(j_ptd, 1)

            def combine(j):
                i, hd = j // 8, j % 8
                dve.wait_ge(j_exp, QB + 2 * (j + 1))
                dve.reciprocal(jsm(j, 6), jsm(j, 4)).then_inc(j_rec, 1)
                dve.wait_ge(j_rec, j + 1)
                dve.tensor_tensor(jsm(j, 8), jsm(j, 6), gate[:, i, 3 * hd + 1:3 * hd + 3], ALU.mult).then_inc(j_w, 1)
                dve.wait_ge(j_w, j + 1)
                dve.wait_ge(j_pv, QB + j + 1)
                o = o_all[:, i, hd * HD:(hd + 1) * HD]
                for br in range(2):
                    if br:
                        dve.wait_ge(j_o, QB + 2 * j + 1)
                    else:
                        dve.wait_ge(j_o, i + 1)
                    dve.scalar_tensor_tensor(out=o, in0=bank[:, 6 + j % 2, br * HD:(br + 1) * HD], scalar=jsm(j, 8, br), in1=o,
                                             op0=ALU.mult, op1=ALU.add).then_inc(j_o, 1)

            def memory_lo(k):
                dve.wait_ge(mem_hi, k + 1)
                dve.scalar_tensor_tensor(out=m_lo[:, k, :], in0=memT[:, k, :], scalar=col("mem", k), in1=m_hi[:, k, :],
                                         op0=ALU.mult, op1=ALU.subtract).then_inc(mem_lo, 1)

            for t in range(JOBS + LAG_VALUES):
                if t < JOBS:
                    maxima(t)
                if 0 <= t - LAG_TURN < JOBS:
                    copy_turned(t - LAG_TURN)
                if t >= LAG_VALUES:
                    combine(t - LAG_VALUES)
                if MEM_FROM <= t < MEM_FROM + DT:
                    memory_lo(t - MEM_FROM)

            dve.wait_ge(ao_std, 1)
            dve.reciprocal(small[:, 36:40], small[:, 36:40]).then_inc(ao_inv, 1)
            dve.wait_ge(ao_inv, 1)
            for b_ in range(QB):
                dve.tensor_scalar(o_all[:, b_, :], o_all[:, b_, :], small[:, 36 + b_:37 + b_], None, ALU.mult).then_inc(ao_n, 1)
            dve.wait_ge(mix_hi, 8)
            for m in range(4):
                dve.scalar_tensor_tensor(out=x_lo[:, 4 + m, :].rearrange("p (b t) -> p b t", b=QB), in0=bank[:, 0:QB, m * P:(m + 1) * P],
                                         scalar=col("attn_out", m), in1=x_hi[:, 4 + m, :].rearrange("p (b t) -> p b t", b=QB),
                                         op0=ALU.mult, op1=ALU.subtract).then_inc(mix_lo, 1)
            inv_columns(dve, NORM_MEM, rcol_mem)

        kx_done, vx_done, qx_done = sem("kx_done"), sem("vx_done"), sem("qx_done")
        x_back, ox_hi, ox_lo = sem("x_back"), sem("ox_hi"), sem("ox_lo")
        X_1, X_2, X_REC = QB + JOBS, QB + 2 * JOBS, JOBS
        XJOBS = QB * 2
        KV_AT = [3, 6]

        def xsm(j, a_, e=None):
            c = 8 * (j % 4) + a_
            return small[:, c:c + 2] if e is None else small[:, c + e:c + e + 1]

        def cross_pe(pe):
            pe.wait_ge(mem_lo, DT)
            for j in range(4):
                linear(pe, Unit(U_KV + j), m_hi, m_lo, MEM)
                if j == 0:
                    stat_columns(pe, NORM_MIXP)
                if j == 1:
                    stat_rows(pe, NORM_MIXP)
            for j in range(4, 8):
                u = Unit(U_KV + j)
                pe.wait_ge(lo_ready, u.n + 1)
                tokens_major(pe, u, m_hi, m_lo, 2, 0, 2 * P, lambda b_: (2 * u.slot + b_, 0)).then_inc(unit_done, 1)
            linear_start(pe, [Unit(U_QX + s) for s in range(2)], lambda k: pe.wait_ge(pre_lo, 8 + k + 1), NORM_X)
            for j in range(2, 4):
                linear(pe, Unit(U_QX + j))

            def scores(j):
                i, hp = j // 2, j % 2
                if j == 0:
                    pe.wait_ge(qx_done, DT)
                    pe.wait_ge(kx_done, DT)
                if j >= 2:
                    pe.wait_ge(j_exp, X_2 + 2 * (j - 1))
                for e in range(2):
                    for d in range(2):
                        tile = 4 * hp + 2 * e + d
                        mm = pe.matmul(bank[:, j % 2, e * MEM:(e + 1) * MEM], qx[:, tile, i * P:(i + 1) * P], kx[:, tile, :],
                                       start=(d == 0), stop=(d == 1))
                mm.then_inc(j_s, 1)

            def turn(j):
                pe.wait_ge(j_exp, X_2 + 2 * (j + 1))
                if j >= 2:
                    pe.wait_ge(j_pta, X_1 + j - 1)
                for c in range(4):
                    mm = pe.transpose(bank[:, 2 + j % 2, c * P:(c + 1) * P],
                                      xprob[:, j % 2, c // 2, c % 2 * P:(c % 2 + 1) * P], ident[:, :])
                mm.then_inc(j_t, 1)

            def values(j):
                hp = j % 2
                pe.wait_ge(j_pta, X_1 + j + 1)
                pe.wait_ge(vx_done, 8)
                if j >= 2:
                    pe.wait_ge(j_o, X_2 + j - 1)
                for e in range(2):
                    for c in range(2):
                        mm = pe.matmul(bank[:, 4 + j % 2, e * MEM:(e + 1) * MEM], xprobT[:, j % 2, 2 * e + c, :],
                                       vx[:, c, (2 * hp + e) * 256:(2 * hp + e + 1) * 256], start=(c == 0), stop=(c == 1))
                mm.then_inc(j_pv, 1)

            def back(j):
                pe.wait_ge(j_o, X_2 + j + 1)
                pe.wait_ge(r_ready, NORM_X + 1)
                if j >= 2:
                    pe.wait_ge(ox_lo, j - 1)
                for c in range(4):
                    mm = pe.transpose(bank[:, 6 + j % 2, c * P:(c + 1) * P], xo[:, j % 2, c * P:(c + 1) * P], ident[:, :])
                mm.then_inc(x_back, 1)

            for t in range(XJOBS + LAG_BACK):
                if t < XJOBS:
                    scores(t)
                if 0 <= t - LAG_TURN < XJOBS:
                    turn(t - LAG_TURN)
                if 0 <= t - LAG_VALUES < XJOBS:
                    values(t - LAG_VALUES)
                if t >= LAG_BACK:
                    back(t - LAG_BACK)
            pe.wait_ge(ox_lo, XJOBS)
            for j in range(4):
                linear(pe, Unit(U_OX + j))
            stat_columns(pe, NORM_XP)
            stat_rows(pe, NORM_XP)
            ffn_pe(pe, U_GU, 2, NORM_F, 0, None)
            stat_columns(pe, NORM_FP)
            stat_rows(pe, NORM_FP)

        def out_evac_act(act, first, n, y, base):
            for j in range(4):
                u = Unit(first + j)
                act.wait_ge(unit_done, u.n + 1)
                for m in range(2):
                    k = 2 * j + m
                    src = bank[:, 2 * u.slot + m, :]
                    act.activation(y[:, k, :], src, ACT.Copy).then_inc(y_ready, 1)
                    square(act, n, k, src)
                split_hi(act, Unit(u.n0 + 3))

        def post_norm_dve(dve, q, n, y, gain, pre, pre_gain, between=lambda k: None):
            inv_columns(dve, n)
            dve.wait_ge(r_ready, n + 1)
            for k in range(DT + 2):
                if k < DT:
                    dve.wait_ge(y_ready, 8 * q + k + 1)
                    dve.tensor_tensor(y[:, k, :], y[:, k, :], rbc[:, :], ALU.mult).then_inc(t_ready, 1)
                if 0 <= k - 1 < DT:
                    dve.wait_ge(t_ready, 8 * q + k)
                    dve.scalar_tensor_tensor(out=h[:, k - 1, :], in0=y[:, k - 1, :], scalar=col(gain, k - 1), in1=h[:, k - 1, :],
                                             op0=ALU.mult, op1=ALU.add).then_inc(h_ready, 1)
                if k >= 2 and pre is not None:
                    dve.wait_ge(h_ready, 8 * q + k - 1)
                    pre_norm_lo(dve, pre, k - 2, pre_gain)
                between(k)

        def cross_act(act):
            out_evac_act(act, U_OUT, NORM_MIXP, yb, 0)
            std_columns(act, NORM_MIXP)
            take_rows(act, NORM_MIXP)
            for k in range(DT):
                act.wait_ge(h_ready, k + 1)
                pre_norm_hi(act, 1, NORM_X, k, "x_pre")
                if k + 1 in KV_AT:
                    split_hi(act, Unit(U_KV + KV_AT.index(k + 1) + 3))
            for j in range(len(KV_AT), 8):
                u = Unit(U_KV + j)
                if j >= 4:
                    act.wait_ge(unit_done, u.n + 1)
                    act.wait_ge(inv_ready, NORM_MEM + 1)
                    for b_ in range(2):
                        act.activation(vx[:, b_, (j - 4) * 256:(j - 3) * 256], bank[:, 2 * u.slot + b_, 0:2 * P], ACT.Copy,
                                       scale=rcol_mem[:, b_:b_ + 1]).then_inc(vx_done, 1)
                split_hi(act, Unit(u.n0 + 3))
            std_columns(act, NORM_X)
            take_rows(act, NORM_X)
            for j in range(4):
                split_hi(act, Unit(U_QX + j + 3))

            def exps(j):
                act.wait_ge(j_neg, X_1 + j + 1)
                if j >= 2:
                    act.wait_ge(j_t, X_1 + j - 1)
                for e in range(2):
                    act.activation(xprob[:, j % 2, e, :], bank[:, j % 2, e * MEM:(e + 1) * MEM], ACT.Exp, bias=xsm(j, 2, e),
                                   accum_out=xsm(j, 4, e)).then_inc(j_exp, 1)

            def copy_turned(j):
                act.wait_ge(j_t, X_1 + j + 1)
                if j >= 2:
                    act.wait_ge(j_pv, X_1 + j - 1)
                act.activation(xprobT[:, j % 2, :, :].rearrange("p c t -> p (c t)"), bank[:, 2 + j % 2, :], ACT.Copy)\
                   .then_inc(j_pta, 1)

            def split_back(j):
                i, hp = j // 2, j % 2
                act.wait_ge(x_back, j + 1)
                act.activation(x_hi[:, 4 * hp:4 * hp + 4, i * P:(i + 1) * P], bank[:, 6 + j % 2, :].rearrange("p (c t) -> p c t", c=4),
                               ACT.Copy).then_inc(ox_hi, 1)

            for t in range(XJOBS + LAG_BACK):
                if t < XJOBS:
                    exps(t)
                if 0 <= t - LAG_TURN < XJOBS:
                    copy_turned(t - LAG_TURN)
                if t >= LAG_BACK:
                    split_back(t - LAG_BACK)
            out_evac_act(act, U_OX, NORM_XP, yb, 1)
            std_columns(act, NORM_XP)
            take_rows(act, NORM_XP)
            for k in range(DT):
                act.wait_ge(h_ready, 8 + k + 1)
                pre_norm_hi(act, 2, NORM_F, k, "ffn_pre")
            std_columns(act, NORM_F)
            take_rows(act, NORM_F)
            ffn_up_act(act, U_GU, 0, None)
            for g in range(4):
                for part in range(3):
                    u = Unit(U_DN + 3 * g + part)
                    act.wait_ge(unit_done, u.n + 1)
                    if part == 2:
                        for m in range(2):
                            k, src = 2 * g + m, bank[:, 2 * (g % 2) + m, :]
                            act.activation(y_ffn[:, k, :], src, ACT.Copy).then_inc(y_ready, 1)
                            square(act, NORM_FP, k, src)
                    if g < 3:
                        split_hi(act, Unit(u.n0 + 3))
            std_columns(act, NORM_FP)
            take_rows(act, NORM_FP)

        def cross_dve(dve):
            for j in range(4):
                split_lo(dve, Unit(U_OUT + j + 3))

            def keys_unit(j):
                u = Unit(U_KV + j)
                if j < 4:
                    dve.wait_ge(unit_done, u.n + 1)
                    dve.wait_ge(r_ready, NORM_MEM + 1)
                    for m in range(2):
                        dve.tensor_tensor(kx[:, 2 * j + m, :], bank[:, 2 * u.slot + m, 0:MEM], rmem[:, :], ALU.mult).then_inc(kx_done, 1)
                split_lo(dve, Unit(u.n0 + 3))

            post_norm_dve(dve, 0, NORM_MIXP, yb, "mix_post", 1, "x_pre",
                          lambda k: keys_unit(KV_AT.index(k)) if k in KV_AT else None)
            for j in range(len(KV_AT), 8):
                keys_unit(j)
            inv_columns(dve, NORM_X)
            dve.wait_ge(r_ready, NORM_X + 1)
            for j in range(4):
                u = Unit(U_QX + j)
                dve.wait_ge(unit_done, u.n + 1)
                for m in range(2):
                    dve.scalar_tensor_tensor(out=qx[:, 2 * j + m, :], in0=bank[:, 2 * u.slot + m, :], scalar=256 ** -0.5,
                                             in1=rbc[:, :], op0=ALU.mult, op1=ALU.mult).then_inc(qx_done, 1)
                split_lo(dve, Unit(u.n0 + 3))

            def maxima(j):
                dve.wait_ge(j_s, X_1 + j + 1)
                dve.tensor_reduce(xsm(j, 0), bank[:, j % 2, :].rearrange("p (e c) -> p e c", e=2), AX, ALU.max).then_inc(j_max, 1)
                dve.wait_ge(j_max, X_1 + j + 1)
                dve.tensor_scalar(xsm(j, 2), xsm(j, 0), -1.0, None, ALU.mult).then_inc(j_neg, 1)

            def combine(j):
                dve.wait_ge(j_exp, X_2 + 2 * (j + 1))
                dve.reciprocal(xsm(j, 6), xsm(j, 4)).then_inc(j_rec, 1)
                dve.wait_ge(j_rec, X_REC + j + 1)
                dve.wait_ge(j_pv, X_1 + j + 1)
                if j >= 2:
                    dve.wait_ge(x_back, j - 1)
                dve.tensor_tensor(xo[:, j % 2, :].rearrange("p (e d) -> p e d", e=2), bank[:, 4 + j % 2, :].rearrange("p (e d) -> p e d", e=2),
                                  xsm(j, 6).unsqueeze(2).to_broadcast([P, 2, MEM]), ALU.mult).then_inc(j_o, 1)

            def split_back(j):
                i, hp = j // 2, j % 2
                dst = (slice(None), slice(4 * hp, 4 * hp + 4), slice(i * P, (i + 1) * P))
                dve.wait_ge(ox_hi, j + 1)
                dve.tensor_tensor(x_lo[dst], bank[:, 6 + j % 2, :].rearrange("p (c t) -> p c t", c=4), x_hi[dst],
                                  ALU.subtract).then_inc(ox_lo, 1)

            for t in range(XJOBS + LAG_BACK):
                if t < XJOBS:
                    maxima(t)
                if 0 <= t - LAG_VALUES < XJOBS:
                    combine(t - LAG_VALUES)
                if t >= LAG_BACK:
                    split_back(t - LAG_BACK)
            for j in range(4):
                split_lo(dve, Unit(U_OX + j + 3))
            post_norm_dve(dve, 1, NORM_XP, yb, "x_post", 2, "ffn_pre")
            inv_columns(dve, NORM_F)
            ffn_up_dve(dve, U_GU, NORM_F, 0, None)
            for j in range(9):
                split_lo(dve, Unit(U_DN + j + 3))
            post_norm_dve(dve, 2, NORM_FP, y_ffn, "ffn_post", None, None)

        tab2_in, pad_ready = sem("tab2_in"), sem("pad_ready")
        l_u, l_ugs, l_sig, l_a, l_tap, l_q, l_vt, l_v_turned, l_v = (sem("l_" + n) for n in (
            "u", "ug_scaled", "sigmoid", "a", "tap", "q", "v_raw", "v_turned", "v"))
        q_sq, q_ss, q_std, q_inv, q_wide, q_row, q_n, q_rot, q_cos, q_sin, q_rope, l_kx = (sem("l_" + n) for n in (
            "q_sq", "q_ss", "q_std", "q_inv", "q_wide", "q_row", "q_n", "q_rot", "q_cos", "q_sin", "q_rope", "kx"))
        l_gs, l_g = sem("l_gates_scaled"), sem("l_gates")
        ln_sum, ln_mu, ln_c, ln_sq, ln_ss, ln_std, ln_inv, ln_row, ln_n, ln_y, ln_hi, ln_lo = (sem("ln_" + n) for n in (
            "sum", "mu", "centred", "squares", "ss", "std", "inv", "rows", "normed", "silu", "hi", "lo"))
        co_done, co_ready, mg_sum, mg_hi, mg_lo = (sem("l_" + n) for n in ("co_done", "co_ready", "mg_sum", "mg_hi", "mg_lo"))
        A = {n: sem("a_" + n) for n in ("scores", "max", "neg", "sinkd", "exp", "den", "rec", "turned", "turned_copied",
                                        "pv", "out", "back", "gated")}
        LJ = QB * 8
        UNIT_TAPS = {4: 10, 5: 9, 6: 9, 7: 9, 8: 11, 9: 11, 10: 3, 11: 3, 12: 3, 13: 3, 14: 5, 15: 9, 16: 2}
        JOB_TAPS = [3, 3, 3, 2, 4, 4, 4, 4, 4, 3, 3]
        assert sum(UNIT_TAPS.values()) + sum(JOB_TAPS) == 4 * TAPS
        ROPE_UNITS = range(10, 15)
        AT_SUM = len(JOB_TAPS)
        AT_MEAN, AT_CENTRE, AT_SQ, AT_SS, AT_INV, AT_ROWS, AT_NORM, AT_SILU, AT_HI, AT_LO, AT_CO = (
            AT_SUM + s for s in (1, 2, 2, 4, 5, 6, 7, 9, 10, 10, 12))
        AT_LAST_IN = 3
        AT_OUT = {AT_CO + 5: V_CO + 3, AT_CO + 9: V_CO + 4}
        STEPS = max(LJ + LAG_BACK, AT_CO + 10)

        def by_two(t, start):
            return range(2 * (t - start), 2 * (t - start) + 2) if start <= t < start + 2 else ()

        def conv_bank(k):
            return 4 if k % 2 and AT_CO + k > LJ + LAG_VALUES else 5

        def block_of(j):
            return (j // 8 + 1) % QB

        def pairs(p):
            return [t for t in (2 * p, 2 * p + 1) if t < 9]

        def asm(j, a_, e=None):
            c = 16 * (j % 4) + a_
            return small[:, c:c + 2] if e is None else small[:, c + e:c + e + 1]

        def layer_pe(pe, L):
            base = U_L
            norm, pre = L * 2 + NORM_L, L * 2 + 3

            def head_columns(t):
                pe.wait_ge(q_sq, L * 9 + t + 1)
                if t == 0:
                    pe.wait_ge(r_ready, norm + 1)
                    pe.wait_ge(tab2_in, L * 16 + 16)
                for b_ in range(QB):
                    c = (t * QB + b_) * 2
                    mm = pe.matmul(bank[:, STAT, c:c + 2], lsq[:, t % 2, b_ * P:(b_ + 1) * P], heads2[:, 0:P:HD],
                                   start=True, stop=True)
                mm.then_inc(q_ss, 1)

            def head_rows(t):
                pe.wait_ge(q_wide, L * 9 + t + 1)
                if t == 1:
                    pe.wait_ge(l_v, L * 4 + 4)
                if t >= 2:
                    pe.wait_ge(q_rope, L * 9 + t - 1)
                for b_ in range(QB):
                    mm = pe.transpose(bank[:, STAT + t % 2, b_ * P:(b_ + 1) * P], lwide[:, t % 2, b_ * P:(b_ + 1) * P], ident[:, :])
                mm.then_inc(q_row, 1)

            def rotate(t):
                pe.wait_ge(q_n, L * 9 + t + 1)
                pe.matmul(bank[:, STAT + t % 2, :], perm2, lq[:, t, :], start=True, stop=True).then_inc(q_rot, 1)

            linear_start(pe, [Unit(base + s, L) for s in range(2)], lambda k: pe.wait_ge(pre_lo, pre * 8 + k + 1), norm)
            for n in range(2, V_CO):
                u = Unit(base + n, L)
                pe.wait_ge(lo_ready, u.n + 1)
                mm = linear_tile(pe, u, 0)
                if n in ROPE_UNITS:
                    for t in pairs(n - ROPE_UNITS[0]):
                        head_rows(t)
                linear_tile(pe, u, 1).then_inc(unit_done, 1)
                if n == V_KV + 1:
                    pe.wait_ge(l_vt, L + 1)
                    for b_ in range(QB):
                        mm = pe.transpose(bank[:, AUX, b_ * P:(b_ + 1) * P], acc[:, b_ * P:(b_ + 1) * P], ident[:, :])
                    mm.then_inc(l_v_turned, 1)
                if V_Q < n <= V_Q + 5:
                    for t in pairs(n - V_Q - 1):
                        head_columns(t)
                if n in ROPE_UNITS:
                    for t in pairs(n - ROPE_UNITS[0]):
                        rotate(t)

            def scores(j):
                i, tile, g = block_of(j), j % 8, j % 8 // 4
                if j == 0:
                    pe.wait_ge(q_rope, L * 9 + 9)
                    pe.wait_ge(l_kx, L * 2 + 2)
                if j < 2:
                    pe.wait_ge(l_g, L * 16 + 14 + 2 * j)
                if j >= 2:
                    pe.wait_ge(A["exp"], (L * LJ + j - 2) * 3 + 2)
                c0, k0 = (P, 0) if i == 0 else (0, (i - 1) * P)
                for e in range(2):
                    dst = bank[:, 2 * (j % 2) + e, c0:2 * P]
                    keys = key_rows(lq[:, 8, :], lkx[:, :], e, g)[:, k0:(i + 1) * P]
                    pe.matmul(dst, lq[HD * e:HD * e + HD, tile, i * P:(i + 1) * P], keys, start=True, stop=False)
                    mm = pe.matmul(dst, ident_b[:, :], mask_b[:, c0:2 * P], start=False, stop=True)
                mm.then_inc(A["scores"], 1)

            def turn(j):
                first = 1 if block_of(j) == 0 else 0
                pe.wait_ge(A["exp"], (L * LJ + j) * 3 + 2)
                if j == 0:
                    pe.wait_ge(l_g, L * 16 + 12)
                if j:
                    pe.wait_ge(A["turned_copied"], L * LJ + j)
                for e in range(2):
                    for c in range(first, 2):
                        mm = pe.transpose(bank[:, 4, (2 * e + c) * P:(2 * e + c + 1) * P], lprob[:, j % 2, e, c * P:(c + 1) * P], ident[:, :])
                mm.then_inc(A["turned"], 1)

            def values(j):
                i, g = block_of(j), j % 8 // 4
                first = 1 if i == 0 else 0
                pe.wait_ge(A["turned_copied"], L * LJ + j + 1)
                if j:
                    pe.wait_ge(A["out"], L * LJ + j)
                for e in range(2):
                    for c in range(first, 2):
                        mm = pe.matmul(bank[:, 6, e * HD:(e + 1) * HD], lprobT[:, j % 2, 2 * e + c, :],
                                       lv[:, i - 1 + c, g * HD:(g + 1) * HD], start=(c == first), stop=(c == 1))
                mm.then_inc(A["pv"], 1)

            def back(j):
                pe.wait_ge(A["out"], L * LJ + j + 1)
                if j:
                    pe.wait_ge(A["gated"], L * LJ + j)
                pe.transpose(bank[:, 7, 0:P], lo_s[:, j % 2, :], ident[:, :]).then_inc(A["back"], 1)

            def conv_project(k):
                u, dst = Unit(base + V_CO + k // 4, L), bank[:, conv_bank(k), :]
                if k % 4 == 0:
                    pe.wait_ge(lo_ready, u.n + 1)
                if k == 0:
                    pe.wait_ge(ln_lo, L * 4 + 4)
                before = 1 if conv_bank(k) == conv_bank(k - 1) else 2
                if k >= before:
                    pe.wait_ge(co_ready, L * 8 + k - before + 1)
                wh = w_hi[:, u.slot, :].rearrange("p (k c) -> p k c", k=4)[:, :, (k % 4) * P:(k % 4 + 1) * P]
                wl = w_lo[:, u.slot, :].rearrange("p (k c) -> p k c", k=4)[:, :, (k % 4) * P:(k % 4 + 1) * P]
                for c in range(4):
                    pe.matmul(dst, wh[:, c, :], x_hi[:, c, :], start=(c == 0), stop=False)
                    pe.matmul(dst, wh[:, c, :], x_lo[:, c, :], start=False, stop=False)
                    mm = pe.matmul(dst, wl[:, c, :], x_hi[:, c, :], start=False, stop=(c == 3))
                mm.then_inc(unit_done if k % 4 == 3 else co_done, 1)

            for t in range(STEPS):
                if t < LJ:
                    scores(t)
                if 0 <= t - LAG_TURN < LJ:
                    turn(t - LAG_TURN)
                if 0 <= t - LAG_VALUES < LJ:
                    values(t - LAG_VALUES)
                if 0 <= t - LAG_BACK < LJ:
                    back(t - LAG_BACK)
                if t == AT_SUM:
                    pe.wait_ge(l_tap, L * 4 * TAPS + 4 * TAPS)
                    for m in range(4):
                        mm = pe.matmul(bank[:, 5, :], ones[:, :], cy[:, m, :], start=(m == 0), stop=(m == 3))
                    mm.then_inc(ln_sum, 1)
                if t == AT_SS:
                    pe.wait_ge(ln_sq, L * 4 + 4)
                    column_sums(pe, bank[:, 5, 0:QB], *(conv_squares(m) for m in range(4))).then_inc(ln_ss, 1)
                if t == AT_ROWS:
                    pe.wait_ge(ln_inv, L + 1)
                    spread(pe, bank[:, 5, :], rcol_ln).then_inc(ln_row, 1)
                if AT_CO <= t < AT_CO + 8:
                    conv_project(t - AT_CO)

            def merged(k):
                pe.wait_ge(mg_lo, L * 8 + k + 1)
            linear_start(pe, [Unit(base + V_OUT + s, L) for s in range(2)], merged)
            for j in range(2, 4):
                linear(pe, Unit(base + V_OUT + j, L))
            ffn_pe(pe, base + V_GU, L * 2 + 4, norm + 1, L + 1, L)

        def conv_squares(m):
            return la[:, m, PAD:PAD + T]

        def layer_act(act, L):
            base = U_L
            norm, pre = L * 2 + NORM_L, L * 2 + 3
            split_hi(act, Unit(base, L))
            act.wait_ge(unit_done, L * V_N + base)
            act.dma_start(tab2[:, :], rope2).then_inc(tab2_in, 16)
            for k in range(DT):
                act.wait_ge(h_ready, L * 16 + 16 + k + 1)
                pre_norm_hi(act, pre, norm, k, "norm_mix", L)
                if k in (3, 7):
                    split_hi(act, Unit(base + k // 4 + 1, L))
            std_columns(act, norm)
            take_rows(act, norm)

            for n in range(V_CO):
                u = Unit(base + n, L)
                if V_UG <= n < V_Q:
                    for m in range(2):
                        k, src = 2 * (n - V_UG) + m, bank[:, 2 * u.slot + m, :]
                        act.wait_ge(l_ugs, L * 4 + k + 1)
                        act.activation(src, src, ACT.Sigmoid).then_inc(l_sig, 1)
                if n == V_KV:
                    act.wait_ge(unit_done, u.n + 1)
                    act.activation(acc[:, :], bank[:, 2 * u.slot + 1, :], ACT.Copy).then_inc(l_vt, 1)
                if n >= V_GA:
                    for m in range(2):
                        k, src = 2 * (n - V_GA) + m, bank[:, 2 * u.slot + m, :]
                        act.wait_ge(l_gs, L * 16 + k + 1)
                        act.activation((sga if k < 8 else sgb)[:, k % 8, :], src, ACT.Sigmoid).then_inc(l_g, 1)
                if n < V_CO - 1:
                    split_hi(act, Unit(base + n + 3, L))
                if V_Q <= n <= V_KV:
                    for t in pairs(n - V_Q):
                        act.wait_ge(l_q, L * 9 + t + 1)
                        if t >= 2:
                            act.wait_ge(q_ss, L * 9 + t - 1)
                        act.activation(lsq[:, t % 2, :], lq[:, t, :], ACT.Square).then_inc(q_sq, 1)
                if n == V_KV + 1:
                    act.wait_ge(l_v_turned, L + 1)
                    for b_ in range(QB):
                        act.activation(lv[:, b_, :], bank[:, AUX, b_ * P:(b_ + 1) * P], ACT.Copy,
                                       scale=rcol[:, b_:b_ + 1]).then_inc(l_v, 1)
                    act.wait_ge(q_ss, L * 9 + 9)
                    nq = 8 * QB * 2
                    act.activation(rcol_head[:, 0:nq], bank[:, STAT, 0:nq], ACT.Sqrt, bias=eps_c[:, 1:2]).then_inc(q_std, 1)
                    act.activation(rcol_head[:, nq:], bank[:, STAT, nq:9 * QB * 2], ACT.Sqrt, bias=eps_c[:, 0:1],
                                   scale=1.0 / HD).then_inc(q_std, 1)
                if n + 1 in ROPE_UNITS:
                    for t in pairs(n + 1 - ROPE_UNITS[0]):
                        if t == 0:
                            act.wait_ge(q_inv, L + 1)
                        if t >= 2:
                            act.wait_ge(q_row, L * 9 + t - 1)
                        c = t * QB * 2
                        act.activation(lwide[:, t % 2, :].rearrange("p (c d) -> p c d", d=HD),
                                       rcol_head[:, c:c + QB * 2].unsqueeze(2).to_broadcast([P, QB * 2, HD]), ACT.Copy).then_inc(q_wide, 1)
                if n == ROPE_UNITS[-1] + 1:
                    act.wait_ge(q_rope, L * 9 + 9)
                    act.activation(lkx[0:HD, :], lq[HD:P, 8, :], ACT.Copy).then_inc(l_kx, 1)
                    act.activation(lkx[HD:P, :], lq[0:HD, 8, :], ACT.Copy).then_inc(l_kx, 1)

            def exps(j):
                c0 = P if block_of(j) == 0 else 0
                act.wait_ge(A["neg"], L * LJ + j + 1)
                if j >= 2:
                    act.wait_ge(A["turned"], L * LJ + j - 1)
                for e in range(2):
                    act.activation(lprob[:, j % 2, e, c0:2 * P], bank[:, 2 * (j % 2) + e, c0:2 * P], ACT.Exp, bias=asm(j, 2, e),
                                   accum_out=asm(j, 4, e)).then_inc(A["exp"], 1)
                act.wait_ge(A["sinkd"], L * LJ + j + 1)
                act.activation(asm(j, 8), asm(j, 6), ACT.Exp).then_inc(A["exp"], 1)

            def copy_turned(j):
                act.wait_ge(A["turned"], L * LJ + j + 1)
                if j >= 2:
                    act.wait_ge(A["pv"], L * LJ + j - 1)
                first = 1 if block_of(j) == 0 else 0
                act.activation(lprobT[:, j % 2, :, :].rearrange("p (e c) t -> p e c t", e=2)[:, :, first:, :],
                               bank[:, 4, :].rearrange("p (e c t) -> p e c t", e=2, c=2)[:, :, first:, :], ACT.Copy)\
                   .then_inc(A["turned_copied"], 1)

            for t in range(STEPS):
                if t < LJ:
                    exps(t)
                if 0 <= t - LAG_TURN < LJ:
                    copy_turned(t - LAG_TURN)
                if t == AT_LAST_IN:
                    split_hi(act, Unit(base + V_CO + 2, L))
                for m in by_two(t, AT_SQ):
                    act.wait_ge(ln_c, L * 4 + m + 1)
                    act.activation(conv_squares(m), cy[:, m, :], ACT.Square).then_inc(ln_sq, 1)
                if t == AT_SS:
                    act.wait_ge(ln_ss, L + 1)
                    act.activation(rcol_ln[:, :], bank[:, 5, 0:QB], ACT.Sqrt, bias=eps_c[:, 0:1], scale=1.0 / 512).then_inc(ln_std, 1)
                if t == AT_SILU:
                    for m in range(4):
                        act.wait_ge(ln_n, L * 4 + m + 1)
                        act.activation(cy[:, m, :], cy[:, m, :], ACT.Silu, bias=col("ln_b", m, L), scale=col("ln_g", m, L)).then_inc(ln_y, 1)
                for m in by_two(t, AT_HI):
                    if m == 0:
                        act.wait_ge(unit_done, L * V_N + base + V_CO)
                    act.wait_ge(ln_y, L * 4 + m + 1)
                    act.activation(x_hi[:, m, :], cy[:, m, :], ACT.Copy).then_inc(ln_hi, 1)
                if t in AT_OUT:
                    split_hi(act, Unit(base + AT_OUT[t], L))

            act.wait_ge(unit_done, L * V_N + base + V_CO + 2)
            for k in range(DT):
                act.wait_ge(mg_sum, L * 8 + k + 1)
                act.activation(x_hi[:, k, :], sgb[:, k, :], ACT.Copy).then_inc(mg_hi, 1)
            for j in range(4):
                split_hi(act, Unit(base + V_OUT + j + 3, L))
            for k in range(DT):
                act.wait_ge(h_ready, L * 16 + 24 + k + 1)
                pre_norm_hi(act, pre + 1, norm + 1, k, "norm_ffn", L)
            std_columns(act, norm + 1)
            take_rows(act, norm + 1)
            ffn_up_act(act, base + V_GU, L + 1, L)
            for j in range(9):
                split_hi(act, Unit(base + V_DN + j + 3, L))

        def layer_dve(dve, L):
            base = U_L
            norm, pre = L * 2 + NORM_L, L * 2 + 3
            split_lo(dve, Unit(base, L))
            for k in range(DT):
                pre_norm_lo(dve, pre, k, "norm_mix", L)
                if k in (3, 7):
                    split_lo(dve, Unit(base + k // 4 + 1, L))
            inv_columns(dve, norm)
            dve.wait_ge(r_ready, norm + 1)
            done = [0]

            def taps(count):
                for s in range(done[0], done[0] + count):
                    tap, m = s // 4, s % 4
                    src, wt = la[:, m, tap:tap + T], col("taps", m * TAPS + tap, L)
                    if tap == 0:
                        dve.wait_ge(l_a, L * 4 + m + 1)
                        dve.wait_ge(pad_ready, L + 1)
                        dve.tensor_scalar(cy[:, m, :], src, wt, col("conv_b", m, L), ALU.mult, ALU.add).then_inc(l_tap, 1)
                    else:
                        dve.wait_ge(l_tap, L * 4 * TAPS + s - 3)
                        dve.scalar_tensor_tensor(out=cy[:, m, :], in0=src, scalar=wt, in1=cy[:, m, :],
                                                 op0=ALU.mult, op1=ALU.add).then_inc(l_tap, 1)
                done[0] += count

            def normed(p):
                for t in pairs(p):
                    dve.wait_ge(q_row, L * 9 + t + 1)
                    dve.scalar_tensor_tensor(out=lq[:, t, :], in0=lq[:, t, :], scalar=col("q_norm" if t < 8 else "k_norm", 0, L),
                                             in1=bank[:, STAT + t % 2, :], op0=ALU.mult, op1=ALU.mult).then_inc(q_n, 1)

            def roped(p):
                for t in pairs(p):
                    rot = bank[:, STAT + t % 2, :]
                    dve.wait_ge(q_rot, L * 9 + t + 1)
                    dve.tensor_tensor(rot, rot, sin2, ALU.mult).then_inc(q_sin, 1)
                    dve.wait_ge(q_sin, L * 9 + t + 1)
                    dve.wait_ge(q_cos, L * 9 + t + 1)
                    dve.tensor_tensor(lq[:, t, :], lcos[:, t % 2, :], rot, ALU.add).then_inc(q_rope, 1)

            for n in range(V_CO):
                u = Unit(base + n, L)
                dve.wait_ge(unit_done, u.n + 1)
                for m in range(2):
                    src = bank[:, 2 * u.slot + m, :]
                    if n < V_UG:
                        dve.tensor_tensor(la[:, 2 * n + m, PAD:PAD + T], src, rbc[:, :], ALU.mult).then_inc(l_u, 1)
                    elif n < V_Q:
                        dve.tensor_tensor(src, src, rbc[:, :], ALU.mult).then_inc(l_ugs, 1)
                    elif n <= V_KV:
                        if n < V_KV or m == 0:
                            dve.tensor_tensor(lq[:, 2 * (n - V_Q) + m, :], src, rbc[:, :], ALU.mult).then_inc(l_q, 1)
                    else:
                        dve.tensor_tensor(src, src, rbc[:, :], ALU.mult).then_inc(l_gs, 1)
                if V_UG <= n < V_Q:
                    for m in range(2):
                        k = 2 * (n - V_UG) + m
                        dst = la[:, k, PAD:PAD + T]
                        dve.wait_ge(l_sig, L * 4 + k + 1)
                        dve.wait_ge(l_u, L * 4 + k + 1)
                        dve.tensor_tensor(dst, dst, bank[:, 2 * u.slot + m, :], ALU.mult).then_inc(l_a, 1)
                if n < V_CO - 1:
                    split_lo(dve, Unit(base + n + 3, L))
                if n in ROPE_UNITS:
                    roped(n - ROPE_UNITS[0])
                if n == V_KV + 1:
                    dve.wait_ge(q_std, L * 2 + 2)
                    dve.reciprocal(rcol_head[:, :], rcol_head[:, :]).then_inc(q_inv, 1)
                taps(UNIT_TAPS.get(n, 0))
                if n + 1 in ROPE_UNITS:
                    normed(n + 1 - ROPE_UNITS[0])

            def maxima(j):
                c0 = P if block_of(j) == 0 else 0
                tile = j % 8
                dve.wait_ge(A["scores"], L * LJ + j + 1)
                dve.tensor_reduce(asm(j, 0), bank[:, 2 * (j % 2):2 * (j % 2) + 2, c0:2 * P], AX, ALU.max).then_inc(A["max"], 1)
                dve.wait_ge(A["max"], L * LJ + j + 1)
                sink = gains[:, bass.ds(L * LAYER_W + (_cols["sinks"][0] + 2 * tile), 2)]
                nsink = neg_sink[:, bass.ds(L, 1), 2 * tile:2 * tile + 2].rearrange("p o c -> p (o c)")
                dve.scalar_tensor_tensor(out=asm(j, 2), in0=asm(j, 0), scalar=-1.0, in1=nsink, op0=ALU.mult, op1=ALU.min).then_inc(A["neg"], 1)
                dve.wait_ge(A["neg"], L * LJ + j + 1)
                dve.tensor_tensor(asm(j, 6), asm(j, 2), sink, ALU.add).then_inc(A["sinkd"], 1)

            def combine(j):
                dve.wait_ge(A["exp"], (L * LJ + j + 1) * 3)
                dve.tensor_tensor(asm(j, 10), asm(j, 4), asm(j, 8), ALU.add).then_inc(A["den"], 1)
                dve.wait_ge(A["den"], L * LJ + j + 1)
                dve.reciprocal(asm(j, 12), asm(j, 10)).then_inc(A["rec"], 1)
                dve.wait_ge(A["rec"], L * LJ + j + 1)
                dve.wait_ge(A["pv"], L * LJ + j + 1)
                if j >= 2:
                    dve.wait_ge(A["back"], L * LJ + j - 1)
                dve.tensor_tensor(lo_s[:, j % 2, :].rearrange("p (e d) -> p e d", e=2), bank[:, 6, 0:P].rearrange("p (e d) -> p e d", e=2),
                                  asm(j, 12).unsqueeze(2).to_broadcast([P, 2, HD]), ALU.mult).then_inc(A["out"], 1)

            def gated(j):
                i, tile = block_of(j), j % 8
                dst = sga[:, tile, i * P:(i + 1) * P]
                dve.wait_ge(A["back"], L * LJ + j + 1)
                if j == 0:
                    dve.wait_ge(l_g, L * 16 + 16)
                dve.tensor_tensor(dst, dst, bank[:, 7, 0:P], ALU.mult).then_inc(A["gated"], 1)

            for t in range(STEPS):
                if t < LJ:
                    maxima(t)
                if 0 <= t - LAG_VALUES < LJ:
                    combine(t - LAG_VALUES)
                if 0 <= t - LAG_BACK < LJ:
                    gated(t - LAG_BACK)
                if t == AT_LAST_IN:
                    split_lo(dve, Unit(base + V_CO + 2, L))
                if t < AT_SUM:
                    taps(JOB_TAPS[t])
                if t == AT_MEAN:
                    dve.wait_ge(ln_sum, L + 1)
                    dve.tensor_scalar(rbc[:, :], bank[:, 5, :], 1.0 / 512, None, ALU.mult).then_inc(ln_mu, 1)
                for m in by_two(t, AT_CENTRE):
                    dve.wait_ge(ln_mu, L + 1)
                    dve.tensor_tensor(cy[:, m, :], cy[:, m, :], rbc[:, :], ALU.subtract).then_inc(ln_c, 1)
                if t == AT_INV:
                    dve.wait_ge(ln_std, L + 1)
                    dve.reciprocal(rcol_ln[:, :], rcol_ln[:, :]).then_inc(ln_inv, 1)
                for m in by_two(t, AT_NORM):
                    dve.wait_ge(ln_row, L + 1)
                    dve.wait_ge(ln_c, L * 4 + m + 1)
                    dve.tensor_tensor(cy[:, m, :], cy[:, m, :], bank[:, 5, :], ALU.mult).then_inc(ln_n, 1)
                for m in by_two(t, AT_LO):
                    dve.wait_ge(ln_hi, L * 4 + m + 1)
                    dve.tensor_tensor(x_lo[:, m, :], cy[:, m, :], x_hi[:, m, :], ALU.subtract).then_inc(ln_lo, 1)
                if AT_CO <= t < AT_CO + 8:
                    k = t - AT_CO
                    if k % 4 == 3:
                        dve.wait_ge(unit_done, L * V_N + base + V_CO + k // 4 + 1)
                    else:
                        dve.wait_ge(co_done, L * 6 + k - k // 4 + 1)
                    dve.tensor_tensor(sgb[:, k, :], sgb[:, k, :], bank[:, conv_bank(k), :], ALU.mult).then_inc(co_ready, 1)
                if t in AT_OUT:
                    split_lo(dve, Unit(base + AT_OUT[t], L))

            for k in range(DT):
                dve.wait_ge(mg_hi, L * 8 + k + 1)
                dve.tensor_tensor(x_lo[:, k, :], sgb[:, k, :], x_hi[:, k, :], ALU.subtract).then_inc(mg_lo, 1)

            def residual(k, src):
                dve.tensor_tensor(h[:, k, :], h[:, k, :], src, ALU.add).then_inc(h_ready, 1)

            for j in range(4):
                u = Unit(base + V_OUT + j, L)
                dve.wait_ge(unit_done, u.n + 1)
                for m in range(2):
                    residual(2 * j + m, bank[:, 2 * u.slot + m, :])
                split_lo(dve, Unit(u.n0 + 3, L))
            for k in range(DT):
                pre_norm_lo(dve, pre + 1, k, "norm_ffn", L)
            inv_columns(dve, norm + 1)
            ffn_up_dve(dve, base + V_GU, norm + 1, L + 1, L)
            for g in range(4):
                for part in range(3):
                    u = Unit(base + V_DN + 3 * g + part, L)
                    if part == 2:
                        dve.wait_ge(unit_done, u.n + 1)
                        for m in range(2):
                            residual(2 * g + m, bank[:, 2 * (g % 2) + m, :])
                    if g < 3:
                        split_lo(dve, Unit(u.n0 + 3, L))

        @block.tensor
        def _(pe):
            mixer1_pe(pe)
            cross_pe(pe)
            with pe.Fori(0, LAYERS) as L:
                layer_pe(pe, L)

        @block.scalar
        def _(act):
            mixer1_act(act)
            cross_act(act)
            with act.Fori(0, LAYERS) as L:
                layer_act(act, L)

        @block.vector
        def _(dve):
            mixer1_dve(dve)
            cross_dve(dve)
            dve.tensor_scalar(neg_sink[:, :, :].rearrange("p l c -> p (l c)").rearrange("p (l c) -> p l c", l=LAYERS),
                              gains[:, LAYER_BASE:].rearrange("p (l c) -> p l c", l=LAYERS)[:, :, _cols["sinks"][0] - LAYER_BASE:
                                                                                          _cols["sinks"][0] - LAYER_BASE + 16],
                              -1.0, None, ALU.mult).then_inc(neg_sink_ready, 1)
            dve.wait_ge(neg_sink_ready, 1)
            with dve.Fori(0, LAYERS) as L:
                layer_dve(dve, L)

        @block.gpsimd
        def _(pool):
            pool.memset(ones[:, :], 1.0).then_inc(const_ready, 1)
            pool.memset(eps_c[:, 0:1], EPS)
            pool.memset(eps_c[:, 1:2], HD * EPS)
            pool.memset(eps_c[:, 2:3], float(np.pi / 2)).then_inc(const_ready, 1)
            pool.memset(kcm[:, :, :], 0.0)
            pool.memset(vblk[:, :], 0.0).then_inc(vblk_zero, 1)
            sum_squares(pool, NORM_MIX)
            for r in range(6):
                rope_pool(pool, r)
            sum_squares(pool, NORM_MEM, MEM)
            for n in range(NORM_MIXP, NORM_L):
                sum_squares(pool, n)
            ones_pad = ones[:, 0:PAD].unsqueeze(1).to_broadcast([P, 4, PAD])
            with pool.Fori(0, LAYERS) as L:
                pool.wait_ge(unit_done, L * V_N + U_L)
                pool.tensor_tensor(la[:, :, 0:PAD], ones_pad, ones_pad, ALU.subtract).then_inc(pad_ready, 1)
                sum_squares(pool, L * 2 + NORM_L)
                pool.wait_ge(tab2_in, L * 16 + 16)
                for t in range(9):
                    pool.wait_ge(q_n, L * 9 + t + 1)
                    if t >= 2:
                        pool.wait_ge(q_rope, L * 9 + t - 1)
                    pool.tensor_tensor(lcos[:, t % 2, :], lq[:, t, :], cos2, ALU.mult).then_inc(q_cos, 1)
                for k in range(DT):
                    pool.wait_ge(A["gated"], L * LJ + 3 * 8 + k + 1)
                    pool.wait_ge(co_ready, L * 8 + k + 1)
                    pool.tensor_tensor(sgb[:, k, :], sgb[:, k, :], sga[:, k, :], ALU.add).then_inc(mg_sum, 1)
                sum_squares(pool, L * 2 + NORM_L + 1)


def unit_pack(weight, cols, rows=8):
    k = weight.shape[0] // P
    part = weight[:, cols].reshape(k, P, len(cols)).transpose(1, 0, 2)
    out = []
    for c in range(0, k, rows):
        u = np.zeros((P, rows, UNIT // rows), np.float32)
        m = min(rows, k - c)
        u[:, :m, :len(cols)] = part[:, c:c + m]
        out.append(u.reshape(P, UNIT))
    return out


def spans(weight, lo, hi, rows=8, order=None):
    step = UNIT // rows
    cols = np.arange(lo, hi) if order is None else np.asarray(order)
    return [u for c in range(0, len(cols), step) for u in unit_pack(weight, cols[c:c + step], rows)]


def ffn_units(gate_up, down):
    out = []
    for j in range(FT):
        out += unit_pack(gate_up, np.r_[j * P:(j + 1) * P, FF + j * P:FF + (j + 1) * P])
    return out + spans(down, 0, D)


def tiles(v):
    v = np.asarray(v)
    return v.reshape(-1, P).T


def feature_major(a):
    return np.ascontiguousarray(a.T.reshape(-1, P, a.shape[0]).transpose(1, 0, 2).reshape(P, -1))


def rotation(half, width):
    m = np.zeros((P, P), np.float32)
    for head in range(0, P, HD):
        for i in range(half):
            m[head + half + i, head + i] = -1.0
            m[head + i, head + half + i] = 1.0
    return m


def kernel(**inputs):
    import concourse.bacc as bacc
    from concourse.bass_utils import run_bass_kernel_spmd

    g = {k: np.asarray(v) for k, v in inputs.items()}
    win = g["w_in"]
    c = 3 * 512
    kvb = c + 512
    stream = spans(win, 0, kvb) + spans(win, kvb, kvb + 256)
    stream += spans(win, 0, 0, order=np.r_[kvb + 256:kvb + 384, kvb + 512:kvb + 640])
    stream += spans(win, 0, 0, order=np.r_[kvb + 384:kvb + 512, kvb + 640:kvb + 768])
    stream += spans(g["w1_kc"], 0, 256) + spans(g["w1_vc"], 0, 256)
    stream += spans(g["w_out"], 0, D) + spans(g["w_kv_x"], 0, 2 * D) + spans(g["w_q_x"], 0, D) + spans(g["w_o_x"], 0, D)
    stream += ffn_units(g["w_gate_up"], g["w_down"])
    for l in range(LAYERS):
        wl = g["w_in_2"][l]
        q, kv, u, ug, ga = 0, 1024, 1280, 1792, 2304
        stream += spans(wl, u, u + 512) + spans(wl, ug, ug + 512) + spans(wl, q, q + 1024) + spans(wl, kv, kv + 256)
        stream += spans(wl, ga, ga + 2048) + spans(g["w_conv_out_2"][l], 0, D, rows=4) + spans(g["w_out_2"][l], 0, D)
        stream += ffn_units(g["w_gate_up_2"][l], g["w_down_2"][l])
    assert len(stream) == UNITS, len(stream)
    w = np.stack(stream)

    def pe_pairs(pe):
        return pe.reshape(16, 2, HD).transpose(1, 2, 0).reshape(P, 16)

    inv = (np.float32(10000.0) ** (-np.arange(32, dtype=np.float32) / np.float32(32))).astype(np.float32)
    cols = [tiles(g["norm_mix_pre"]), tiles(g["norm_mix_post"]), tiles(g["norm_x_pre"]), tiles(g["norm_mem"]),
            tiles(g["norm_x_post"]), tiles(g["norm_ffn_pre"]), tiles(g["norm_ffn_post"]), tiles(g["norm_conv_out"]),
            tiles(g["norm_attn_out"]), g["conv_w"].reshape(3, 4, P).transpose(2, 1, 0).reshape(P, 12),
            np.tile(inv, 4)[:, None], pe_pairs(g["pe_kc"]), pe_pairs(g["pe_vc"])]
    for l in range(LAYERS):
        cols += [tiles(g["norm_mix_2"][l]), tiles(g["norm_ffn_2"][l]), np.tile(g["q_norm_2"][l], 2)[:, None],
                 np.tile(g["k_norm_2"][l], 2)[:, None], np.broadcast_to(g["sinks_2"][l], (P, 16)),
                 g["conv_w_2"][l].reshape(TAPS, 4, P).transpose(2, 1, 0).reshape(P, 4 * TAPS), tiles(g["conv_b_2"][l]),
                 tiles(g["conv_ln_g_2"][l]), tiles(g["conv_ln_b_2"][l])]
    pack = np.ascontiguousarray(np.concatenate(cols, axis=1).astype(np.float32))
    assert pack.shape == (P, PACK_W)

    r, s = np.arange(P)[:, None], np.arange(P)[None, :]
    masks = [np.where(s > r, 0, NEG), np.where(s <= r, 0, NEG)]
    for b in range(QB):
        j = np.arange(32)[None, :]
        seen = (j < NCMP) & (16 * j + 31 <= b * P + r)
        masks.append(np.tile(np.where(seen, 0, NEG), (1, 4)))
    cmask = np.ascontiguousarray(np.concatenate(masks, axis=1).astype(np.float32))
    tables = np.concatenate([np.eye(P, dtype=np.float32), rotation(32, HD)], axis=1)
    f2 = (np.float32(500000.0) ** (-np.arange(0, 16, 2, dtype=np.float32) / np.float32(16))).astype(np.float32)
    ang = (np.arange(T, dtype=np.float32)[None, :] * f2[:, None]).astype(np.float32).astype(np.float64)
    cos_h, sin_h = np.ones((HD, T)), np.zeros((HD, T))
    cos_h[0:8], cos_h[8:16], sin_h[0:8], sin_h[8:16] = np.cos(ang), np.cos(ang), np.sin(ang), np.sin(ang)
    heads = np.kron(np.eye(2), np.ones((HD, HD)))
    rope2 = np.concatenate([np.tile(cos_h, (2, 1)), np.tile(sin_h, (2, 1)), rotation(8, HD), heads], axis=1).astype(np.float32)

    w2 = np.stack([g["w2_kc"], g["w2_vc"]]).reshape(2, 2, P, HD).transpose(2, 0, 1, 3).reshape(P, -1)
    wg = win[:, kvb + 768:].reshape(8, P, 24).transpose(1, 0, 2).reshape(P, -1)
    arrays = {
        "w": w, "x": feature_major(g["x"][0]), "mem": feature_major(g["mem"][0]), "pos": g["positions"].astype(np.int32),
        "pack": pack, "tables": tables, "cmask": cmask, "w2": np.ascontiguousarray(w2), "wg": np.ascontiguousarray(wg),
        "rope2": np.ascontiguousarray(rope2),
    }
    nc = bacc.Bacc("TRN2", target_bir_lowering=False, num_devices=1, dynamic_dma_scratch_size=1024)
    aps = {n: nc.dram_tensor(n + "_d", a.shape, mybir.dt.from_np(a.dtype), kind="ExternalInput").ap() for n, a in arrays.items()}
    out = nc.dram_tensor("out_d", (P, DT * T), F32, kind="ExternalOutput").ap()
    build(nc, out=out.rearrange("p (k t) -> p k t", k=DT), **aps)
    res = run_bass_kernel_spmd(nc, [{n + "_d": a for n, a in arrays.items()}], core_ids=[0])
    y = res.results[0]["out_d"].reshape(P, DT, T).transpose(2, 1, 0).reshape(1, T, D)
    return np.ascontiguousarray(y)
```
